# Optimizing a Trainium2 kernel written in Bass

```python
import math
import jax
import jax.numpy as jnp
from jax import lax
import numpy as np

D_MODEL = 1024
BATCH = 1
SEQ = 256
DEPTH = 2

CTX_LEN = 256
GRID_W = 64
N_MOD = 6
NA_HEADS = 8
NA_HEAD_DIM = 64
NA_WIDTH = NA_HEADS * NA_HEAD_DIM
WIN_R_MAX = 8
WIN_C = 16
QC_BLK = 16
KC_BLK = QC_BLK + WIN_C
DN_HEADS = 4
DN_HEAD_DIM = 128
DN_WIDTH = DN_HEADS * DN_HEAD_DIM
DN_CONV = 5
DN_CHUNK = 64
ROPE_BASE = 10000.0
SC_WIDTH = 512
SC_CONV = 3
N_BRANCH = 3
N_EXPERTS = 16
N_GROUPS = 4
EXPERTS_PER_GROUP = N_EXPERTS // N_GROUPS
TOP_K = 2
D_EXPERT = 512
EPS = 1e-6
NEG_INF = -1e30
P_SIZES = (3 * NA_WIDTH, 3 * DN_WIDTH, DN_WIDTH, 4 * DN_HEADS, 3 * SC_WIDTH, N_BRANCH * D_MODEL)
P_TOTAL = 3 * NA_WIDTH + 3 * DN_WIDTH + DN_WIDTH + 4 * DN_HEADS + 3 * SC_WIDTH + N_BRANCH * D_MODEL

kernel_name = "hybrid_natten_deltanet_shortconv_moe_dit"

def rms_norm(x, g):
    xf = x.astype(jnp.float32)
    y = xf * lax.rsqrt(jnp.mean(xf * xf, axis=-1, keepdims=True) + EPS)
    return (y * g.astype(jnp.float32)).astype(x.dtype)

def l2_norm(x):
    xf = x.astype(jnp.float32)
    return xf * lax.rsqrt(jnp.sum(xf * xf, axis=-1, keepdims=True) + EPS)

def modulate(h, shift, scale):
    return h * (1.0 + scale) + shift

def centred_dwconv(x, w):
    k = w.shape[0]
    return lax.conv_general_dilated(
        x, w[:, None, :].astype(x.dtype), window_strides=(1,), padding=[(k // 2, k // 2)],
        dimension_numbers=('NWC', 'WIO', 'NWC'), feature_group_count=x.shape[-1])

def axial_rope_tables(n_tokens):
    t = jnp.arange(n_tokens)
    n_freq = DN_HEAD_DIM // 4
    inv_freq = ROPE_BASE ** (-jnp.arange(n_freq, dtype=jnp.float32) / n_freq)
    pos = jnp.stack([t // GRID_W, t % GRID_W], axis=-1).astype(jnp.float32)
    ang = pos[..., None] * inv_freq
    return jnp.cos(ang), jnp.sin(ang)

def apply_axial_rope(x, cos, sin):
    b, t, h, dk = x.shape
    xr = x.reshape(b, t, h, 2, 2, dk // 4)
    x1, x2 = xr[..., 0, :], xr[..., 1, :]
    c, s = cos[None, :, None], sin[None, :, None]
    out = jnp.stack([x1 * c - x2 * s, x2 * c + x1 * s], axis=-2)
    return out.reshape(b, t, h, dk)

def na_heads(p, q_g, k_g):
    shape = p.shape[:2] + (NA_HEADS, NA_HEAD_DIM)
    q, k, v = jnp.split(p, 3, axis=-1)
    return rms_norm(q.reshape(shape), q_g), rms_norm(k.reshape(shape), k_g), v.reshape(shape)

def neighbourhood_attention(q, k, v, k_ctx, v_ctx, rpb):
    b, s, h, d = q.shape
    rows = s // GRID_W
    win_r = min(WIN_R_MAX, rows)
    n_cb = GRID_W // QC_BLK
    r = jnp.arange(rows)
    row_idx = jnp.clip(r - win_r // 2, 0, rows - win_r)[:, None] + jnp.arange(win_r)[None, :]
    q_col = jnp.arange(GRID_W).reshape(n_cb, QC_BLK)
    key_col0 = jnp.clip(q_col[:, 0] - WIN_C // 2, 0, GRID_W - KC_BLK)
    col_idx = key_col0[:, None] + jnp.arange(KC_BLK)[None, :]
    win_c0 = jnp.clip(q_col - WIN_C // 2, 0, GRID_W - WIN_C)
    kcol = col_idx[:, None, :]
    in_win = (kcol >= win_c0[..., None]) & (kcol < win_c0[..., None] + WIN_C)
    rel_r = row_idx - r[:, None] + WIN_R_MAX - 1
    rel_c = jnp.clip(kcol - q_col[..., None] + WIN_C - 1, 0, 2 * WIN_C - 2)
    bias = rpb.astype(jnp.float32)[:, rel_r[:, None, None, :, None], rel_c[None, :, :, None, :]]
    bias = jnp.where(in_win[None, None, :, :, None, :], bias, NEG_INF)
    scale = d ** -0.5
    qg = q.reshape(b, rows, n_cb, QC_BLK, h, d)
    ri = row_idx[:, None, :, None]
    ci = col_idx[None, :, None, :]
    kg = k.reshape(b, rows, GRID_W, h, d)[:, ri, ci]
    vg = v.reshape(b, rows, GRID_W, h, d)[:, ri, ci]
    s_win = jnp.einsum('brnqhd,brnwkhd->bhrnqwk', qg, kg).astype(jnp.float32) * scale + bias[None]
    s_ctx = jnp.einsum('brnqhd,bchd->bhrnqc', qg, k_ctx).astype(jnp.float32) * scale
    n_win = win_r * KC_BLK
    logits = jnp.concatenate([s_win.reshape(s_win.shape[:5] + (n_win,)), s_ctx], axis=-1)
    p = jax.nn.softmax(logits, axis=-1).astype(v.dtype)
    p_win = p[..., :n_win].reshape(s_win.shape)
    p_ctx = p[..., n_win:]
    o = (jnp.einsum('bhrnqwk,brnwkhd->brnqhd', p_win, vg)
         + jnp.einsum('bhrnqc,bchd->brnqhd', p_ctx, v_ctx))
    return o.reshape(b, s, h * d)

def context_attention(q, k, v):
    b, n, h, d = q.shape
    logits = jnp.einsum('bqhd,bkhd->bhqk', q, k).astype(jnp.float32) * d ** -0.5
    p = jax.nn.softmax(logits, axis=-1).astype(v.dtype)
    return jnp.einsum('bhqk,bkhd->bqhd', p, v).reshape(b, n, h * d)

def deltanet_inputs(qkv, ab, conv_w, a_log, dt_bias, rope):
    b, t, _ = qkv.shape
    qkv = jax.nn.silu(centred_dwconv(qkv, conv_w)).astype(jnp.float32)
    q, k, v = [u.reshape(b, t, DN_HEADS, DN_HEAD_DIM) for u in jnp.split(qkv, 3, axis=-1)]
    q, k = l2_norm(q), l2_norm(k)
    if rope is not None:
        q = apply_axial_rope(q, rope[0], rope[1])
        k = apply_axial_rope(k, rope[0], rope[1])
    ab = ab.astype(jnp.float32).reshape(b, t, 2, 2, DN_HEADS)
    g = -jnp.exp(a_log.astype(jnp.float32)) * jax.nn.softplus(ab[:, :, 0] + dt_bias.astype(jnp.float32))
    beta = jax.nn.sigmoid(ab[:, :, 1])
    to_bht = lambda u: jnp.transpose(u, (0, 2, 1, 3))
    return (to_bht(q), to_bht(k), to_bht(v),
            jnp.transpose(g, (2, 0, 3, 1)), jnp.transpose(beta, (2, 0, 3, 1)))

def gated_delta_chunked(q, k, v, g, beta, s0):
    b, h, t, dk = q.shape
    n = t // DN_CHUNK
    q = q * dk ** -0.5
    q, k, v = [u.reshape(b, h, n, DN_CHUNK, u.shape[-1]) for u in (q, k, v)]
    g = jnp.cumsum(g.reshape(b, h, n, DN_CHUNK), axis=-1)
    beta = beta.reshape(b, h, n, DN_CHUNK)
    idx = jnp.arange(DN_CHUNK)
    lower = idx[:, None] >= idx[None, :]
    strict = idx[:, None] > idx[None, :]
    decay = jnp.exp(jnp.where(lower, g[..., :, None] - g[..., None, :], -jnp.inf))
    kb = k * beta[..., None]
    lmat = jnp.where(strict, jnp.einsum('bhncd,bhnsd->bhncs', kb, k) * decay, 0.0)
    eye = jnp.eye(DN_CHUNK, dtype=q.dtype)
    tinv = lax.linalg.triangular_solve(eye + lmat, jnp.broadcast_to(eye, lmat.shape),
                                       left_side=True, lower=True, unit_diagonal=True)
    u = tinv @ (v * beta[..., None])
    w = tinv @ (kb * jnp.exp(g)[..., None])
    a_intra = jnp.einsum('bhncd,bhnsd->bhncs', q, k) * decay
    qg = q * jnp.exp(g)[..., None]
    kg = k * jnp.exp(g[..., -1:] - g)[..., None]
    glast = jnp.exp(g[..., -1])

    def step(state, xs):
        qg_i, kg_i, u_i, w_i, a_i, gl_i = xs
        v_new = u_i - jnp.einsum('bhcd,bhde->bhce', w_i, state)
        o = jnp.einsum('bhcd,bhde->bhce', qg_i, state) + jnp.einsum('bhcs,bhse->bhce', a_i, v_new)
        state = state * gl_i[..., None, None] + jnp.einsum('bhcd,bhce->bhde', kg_i, v_new)
        return state, o

    xs = tuple(jnp.moveaxis(u_, 2, 0) for u_ in (qg, kg, u, w, a_intra, glast))
    s_final, o = lax.scan(step, s0, xs)
    o = jnp.moveaxis(o, 0, 2).reshape(b, h, t, -1)
    return o, s_final

def bidirectional_deltanet(ctx_in, lat_in):
    qc, kc, vc, gc, bc = ctx_in
    ql, kl, vl, gl, bl = lat_in
    s0 = jnp.zeros((qc.shape[0], DN_HEADS, DN_HEAD_DIM, DN_HEAD_DIM), jnp.float32)
    fl = lambda u: jnp.flip(u, axis=2)
    oc_f, sc_f = gated_delta_chunked(qc, kc, vc, gc[0], bc[0], s0)
    ol_f, _ = gated_delta_chunked(ql, kl, vl, gl[0], bl[0], sc_f)
    oc_b, sc_b = gated_delta_chunked(fl(qc), fl(kc), fl(vc), fl(gc[1]), fl(bc[1]), s0)
    ol_b, _ = gated_delta_chunked(fl(ql), fl(kl), fl(vl), fl(gl[1]), fl(bl[1]), sc_b)
    return oc_f + fl(oc_b), ol_f + fl(ol_b)

def deltanet_output(o, z, out_g):
    b, t, _ = z.shape
    o = rms_norm(jnp.transpose(o, (0, 2, 1, 3)), out_g)
    o = o * jax.nn.silu(z.astype(jnp.float32)).reshape(b, t, DN_HEADS, DN_HEAD_DIM)
    return o.reshape(b, t, DN_WIDTH).astype(z.dtype)

def short_conv_mixer(p, conv_w):
    u, b_gate, c_gate = jnp.split(p, 3, axis=-1)
    return b_gate * centred_dwconv(c_gate * u, conv_w)

def merge_branches(o_na, o_dn, o_sc, gate_p, w_br_na, w_br_dn, w_br_sc, w_out):
    g_na, g_dn, g_sc = jnp.split(jax.nn.sigmoid(gate_p), N_BRANCH, axis=-1)
    merged = g_na * (o_na @ w_br_na) + g_dn * (o_dn @ w_br_dn) + g_sc * (o_sc @ w_br_sc)
    return merged @ w_out

def hybrid_mixer(h, hc, w_in, na_q_g, na_k_g, na_rpb, dn_conv_w, dn_a_log, dn_dt_bias, dn_out_g,
                 sc_conv_w, w_br_na, w_br_dn, w_br_sc, w_out, rope, with_ctx):
    cuts = np.cumsum(P_SIZES)[:-1]
    na_p, dn_qkv, dn_z, dn_ab, sc_p, gate_p = jnp.split(h @ w_in, cuts, axis=-1)
    na_pc, dn_qkvc, dn_zc, dn_abc, sc_pc, gate_pc = jnp.split(hc @ w_in, cuts, axis=-1)
    q, k, v = na_heads(na_p, na_q_g, na_k_g)
    qc, kc, vc = na_heads(na_pc, na_q_g, na_k_g)
    o_na = neighbourhood_attention(q, k, v, kc, vc, na_rpb)
    dn_lat = deltanet_inputs(dn_qkv, dn_ab, dn_conv_w, dn_a_log, dn_dt_bias, rope)
    dn_ctx = deltanet_inputs(dn_qkvc, dn_abc, dn_conv_w, dn_a_log, dn_dt_bias, None)
    oc_dn, ol_dn = bidirectional_deltanet(dn_ctx, dn_lat)
    o_dn = deltanet_output(ol_dn, dn_z, dn_out_g)
    o_sc = short_conv_mixer(sc_p, sc_conv_w)
    y = merge_branches(o_na, o_dn, o_sc, gate_p, w_br_na, w_br_dn, w_br_sc, w_out)
    if not with_ctx:
        return y, None
    o_na_c = context_attention(qc, kc, vc)
    o_dn_c = deltanet_output(oc_dn, dn_zc, dn_out_g)
    o_sc_c = short_conv_mixer(sc_pc, sc_conv_w)
    y_c = merge_branches(o_na_c, o_dn_c, o_sc_c, gate_pc, w_br_na, w_br_dn, w_br_sc, w_out)
    return y, y_c

def grouped_moe(h, w_router, router_bias, w_gate, w_up, w_down):
    b, t, d = h.shape
    tok = h.reshape(b * t, d)
    scores = jax.nn.sigmoid((tok @ w_router).astype(jnp.float32))
    biased = scores + router_bias.astype(jnp.float32)
    group_score = lax.top_k(biased.reshape(-1, N_GROUPS, EXPERTS_PER_GROUP), 2)[0].sum(-1)
    group = jnp.argmax(group_score, axis=-1)
    in_group = (jnp.arange(N_EXPERTS) // EXPERTS_PER_GROUP)[None, :] == group[:, None]
    _, top_idx = lax.top_k(jnp.where(in_group, biased, -jnp.inf), TOP_K)
    top_w = jnp.take_along_axis(scores, top_idx, axis=-1)
    top_w = top_w / jnp.sum(top_w, axis=-1, keepdims=True)
    combine = jnp.sum(jax.nn.one_hot(top_idx, N_EXPERTS, dtype=jnp.float32) * top_w[..., None], axis=1)
    hidden = jax.nn.silu(jnp.einsum('nd,edf->nef', tok, w_gate)) * jnp.einsum('nd,edf->nef', tok, w_up)
    hidden = hidden * combine.astype(h.dtype)[..., None]
    return jnp.einsum('nef,efd->nd', hidden, w_down).reshape(b, t, d)

def setup_inputs(seed: int = 0) -> dict:
    key = jax.random.key(seed)
    ks = jax.random.split(key, 32)
    f32 = jnp.float32
    nrm = lambda k, shape, scale: jax.random.normal(k, shape, f32) * scale
    dt = jnp.exp(jax.random.uniform(ks[14], (DEPTH, 2, DN_HEADS), f32, math.log(1e-3), math.log(1e-1)))
    return {
        'x': nrm(ks[0], (BATCH, SEQ, D_MODEL), 1.0),
        'c': nrm(ks[1], (BATCH, D_MODEL), 1.0),
        'ctx': nrm(ks[2], (BATCH, CTX_LEN, D_MODEL), 1.0),
        'c_ctx': nrm(ks[3], (D_MODEL,), 1.0),
        'w_ada': nrm(ks[4], (DEPTH, D_MODEL, N_MOD * D_MODEL), 0.5 * D_MODEL ** -0.5),
        'b_ada': nrm(ks[5], (DEPTH, N_MOD * D_MODEL), 0.02),
        'norm_mix_g': 1.0 + nrm(ks[6], (DEPTH, D_MODEL), 0.02),
        'norm_ffn_g': 1.0 + nrm(ks[7], (DEPTH, D_MODEL), 0.02),
        'w_in': nrm(ks[8], (DEPTH, D_MODEL, P_TOTAL), D_MODEL ** -0.5),
        'na_q_norm_g': 1.0 + nrm(ks[9], (DEPTH, NA_HEAD_DIM), 0.02),
        'na_k_norm_g': 1.0 + nrm(ks[10], (DEPTH, NA_HEAD_DIM), 0.02),
        'na_rpb': nrm(ks[11], (DEPTH, NA_HEADS, 2 * WIN_R_MAX - 1, 2 * WIN_C - 1), 0.1),
        'dn_conv_w': nrm(ks[12], (DEPTH, DN_CONV, 3 * DN_WIDTH), DN_CONV ** -0.5),
        'dn_a_log': jnp.log(jax.random.uniform(ks[13], (DEPTH, 2, DN_HEADS), f32, 1.0, 16.0)),
        'dn_dt_bias': dt + jnp.log(-jnp.expm1(-dt)),
        'dn_out_norm_g': 1.0 + nrm(ks[15], (DEPTH, DN_HEAD_DIM), 0.02),
        'sc_conv_w': nrm(ks[16], (DEPTH, SC_CONV, SC_WIDTH), SC_CONV ** -0.5),
        'w_branch_na': nrm(ks[17], (DEPTH, NA_WIDTH, D_MODEL), NA_WIDTH ** -0.5),
        'w_branch_dn': nrm(ks[18], (DEPTH, DN_WIDTH, D_MODEL), DN_WIDTH ** -0.5),
        'w_branch_sc': nrm(ks[19], (DEPTH, SC_WIDTH, D_MODEL), SC_WIDTH ** -0.5),
        'w_out': nrm(ks[20], (DEPTH, D_MODEL, D_MODEL), D_MODEL ** -0.5),
        'w_router': nrm(ks[21], (D_MODEL, N_EXPERTS), D_MODEL ** -0.5),
        'router_bias': nrm(ks[22], (N_EXPERTS,), 0.01),
        'moe_w_gate': nrm(ks[23], (DEPTH, N_EXPERTS, D_MODEL, D_EXPERT), D_MODEL ** -0.5),
        'moe_w_up': nrm(ks[24], (DEPTH, N_EXPERTS, D_MODEL, D_EXPERT), D_MODEL ** -0.5),
        'moe_w_down': nrm(ks[25], (DEPTH, N_EXPERTS, D_EXPERT, D_MODEL), D_EXPERT ** -0.5),
    }

def reference(x, c, ctx, c_ctx, w_ada, b_ada, norm_mix_g, norm_ffn_g, w_in, na_q_norm_g, na_k_norm_g,
              na_rpb, dn_conv_w, dn_a_log, dn_dt_bias, dn_out_norm_g, sc_conv_w, w_branch_na, w_branch_dn,
              w_branch_sc, w_out, w_router, router_bias, moe_w_gate, moe_w_up, moe_w_down):
    rope = axial_rope_tables(x.shape[1])
    for l in range(DEPTH):
        with_ctx = l < DEPTH - 1
        mod = (jax.nn.silu(c) @ w_ada[l] + b_ada[l])[:, None, :]
        mod_c = (jax.nn.silu(c_ctx) @ w_ada[l] + b_ada[l])[None, None, :]
        sh1, sc1, g1, sh2, sc2, g2 = jnp.split(mod, N_MOD, axis=-1)
        csh1, csc1, cg1, csh2, csc2, cg2 = jnp.split(mod_c, N_MOD, axis=-1)
        h = modulate(rms_norm(x, norm_mix_g[l]), sh1, sc1)
        hc = modulate(rms_norm(ctx, norm_mix_g[l]), csh1, csc1)
        y, y_c = hybrid_mixer(h, hc, w_in[l], na_q_norm_g[l], na_k_norm_g[l], na_rpb[l], dn_conv_w[l],
                              dn_a_log[l], dn_dt_bias[l], dn_out_norm_g[l], sc_conv_w[l], w_branch_na[l],
                              w_branch_dn[l], w_branch_sc[l], w_out[l], rope, with_ctx)
        x = x + g1 * y
        h = modulate(rms_norm(x, norm_ffn_g[l]), sh2, sc2)
        x = x + g2 * grouped_moe(h, w_router, router_bias, moe_w_gate[l], moe_w_up[l], moe_w_down[l])
        if with_ctx:
            ctx = ctx + cg1 * y_c
            hc = modulate(rms_norm(ctx, norm_ffn_g[l]), csh2, csc2)
            ctx = ctx + cg2 * grouped_moe(hc, w_router, router_bias, moe_w_gate[l], moe_w_up[l], moe_w_down[l])
    return x


_drawn_inputs = setup_inputs


def setup_inputs(seed=0):
    import zlib

    import numpy as np

    out = dict(_drawn_inputs(seed))
    spreads = {}
    factors = {'na_q_norm_g': 8.0, 'na_k_norm_g': 8.0, 'na_rpb': 32.328, 'dn_out_norm_g': 6.396}
    for name, (base, spread) in spreads.items():
        noise = np.random.default_rng([zlib.crc32(name.encode()), seed]).standard_normal(out[name].shape)
        drawn = base * np.exp(spread * noise) if base else spread * noise
        out[name] = jnp.asarray(drawn.astype(out[name].dtype))
    for name, factor in factors.items():
        out[name] = (out[name] * factor).astype(out[name].dtype)
    return out
```

```python
from contextlib import ExitStack

import numpy as np

import concourse.bass as bass
from concourse import mybir

F32 = mybir.dt.float32
U32 = mybir.dt.uint32
ALU = mybir.AluOpType
ACT = mybir.ActivationFunctionType
AX_X = mybir.AxisListType.X

P = 128
D_MODEL, SEQ, CTX_LEN, DEPTH = 1024, 256, 256, 2
GRID_W = 64
NA_HEADS, NA_D, DN_HEADS, DN_D = 8, 64, 4, 128
WIN_C, WIN_R_MAX = 16, 8
N_EXPERTS, N_GROUPS, D_EXPERT = 16, 4, 512
EPS = 1e-6
NEG_INF = -1e30
TOK = CTX_LEN + SEQ
KT = D_MODEL // P
NTT = TOK // P
RING = 6
CHUNK = 2048
NT = 54
NA_SCALE = NA_D ** -0.5
DN_CHUNK = P
LEVELS = 7
COL_NA, COL_DN, COL_Z, COL_AB, COL_SC, COL_GATE = 0, 1536, 3072, 3584, 3600, 5136
T_NQ, T_NK, T_NV, T_DQ, T_DK, T_DV, T_Z, T_U, T_B, T_C = 0, 4, 8, 12, 16, 20, 24, 28, 32, 36
T_SQ, T_RT = 46, 48
T_BIAS = 40
T_VTOK = 32
T_CONV = 50
T_E, T_PT = 50, 52
T_KTOK_DN, T_VTOK_DN = 36, 46
T_OT = 32
T_STATE = 44
T_WORK = ((4, 5, 6, 7, 8, 9, 10, 11), (20, 21, 22, 23, 50, 51, 52, 53))
T_MERGED = 12
T_BR, T_SG = 4, 8
T_ROWS, T_ROUTE = 10, 36
T_MODROW = 24
T_XROW, T_XT, T_MSG, T_HID, T_HT, T_Y = 0, 4, 8, 10, 12, 14
T_HROW, T_GATHER = 24, 24
T_ONEHOT = 18
F_HID, F_MSG, F_ACC, F_CB, F_COMBT = 0, 8, 12, 20, 22
RA_B, RA_MIX, RA_FFN, RA_C, RA_N = 0, 48, 56, 64, 80
RB_CONV, RB_SC, RB_OUT, RB_QG, RB_KG, RB_N = 0, 60, 72, 73, 74, 75
TILES_ADA, TILES_IN, TILES_MERGE, TILES_OUT, TILES_EXP = 24, 40, 48, 8, 4
TILES_LAYER = TILES_ADA + TILES_IN + TILES_MERGE + TILES_OUT + N_EXPERTS * TILES_EXP
CHUNKS_ADA, CHUNKS_IN, CHUNKS_MERGE, CHUNKS_OUT, CHUNKS_EXP = 24, 20, 18, 4, 6
CAPACITY = P
ZERO_ROW = N_EXPERTS * CAPACITY
CHUNKS_LAYER = CHUNKS_ADA + CHUNKS_IN + CHUNKS_MERGE + CHUNKS_OUT + N_EXPERTS * CHUNKS_EXP


def last_tile_of(q):
    l, m = divmod(q, CHUNKS_LAYER)
    t = TILES_LAYER * l
    for chunks, tiles, of in ((CHUNKS_ADA, TILES_ADA, lambda m: m), (CHUNKS_IN, TILES_IN, lambda m: 2 * m + 1),
                              (CHUNKS_MERGE, TILES_MERGE, lambda m: 8 * (m // 3) + (3, 5, 7)[m % 3]),
                              (CHUNKS_OUT, TILES_OUT, lambda m: 2 * m + 1)):
        if m < chunks:
            return t + of(m)
        m, t = m - chunks, t + tiles
    return t + 4 * (m // 6) + (0, 0, 1, 1, 2, 3)[m % 6]


def constants():
    a = np.arange(P)
    r, c = a[:, None], a[None, :]
    parts = {
        "ident": (r == c), "ones": np.ones((P, P)), "ones64": (r // 64 == c // 64),
        "tri0": (r <= c), "tri1": (r >= c),
        "neg0": np.where(r <= c, 0.0, NEG_INF), "neg1": np.where(r >= c, 0.0, NEG_INF),
    }
    for k in range(LEVELS):
        s = 1 << k
        m = (r // (2 * s) == c // (2 * s)) & (r // s % 2 == 1) & (c // s % 2 == 0)
        parts[f"lev{k}0"] = m
        parts[f"lev{k}1"] = m.T
    rot = np.zeros((P, P))
    for d in range(P):
        if d % 64 < 32:
            rot[d + 32, d] = -1.0
        else:
            rot[d - 32, d] = 1.0
    parts["rot"] = rot
    parts["flip"] = (r // 64 == c // 64) & (r % 64 == 63 - c % 64)
    n_freq = DN_D // 4
    inv = np.float32(10000.0) ** (-np.arange(n_freq, dtype=np.float32) / np.float32(n_freq))
    t = np.arange(SEQ)
    pos = np.stack([t // GRID_W, t % GRID_W], 0).astype(np.float32)
    ang = pos[a // 64][:, :] * inv[a % 32][:, None]
    parts["cos"], parts["sin"] = np.cos(ang), np.sin(ang)
    qc = a % 64
    c0 = np.clip(qc - WIN_C // 2, 0, GRID_W - WIN_C)[:, None]
    kc = np.arange(GRID_W)[None, :]
    parts["win"] = np.where((kc >= c0) & (kc < c0 + WIN_C), 0.0, NEG_INF / NA_SCALE)
    parts["iota"] = np.broadcast_to(c, (P, P))
    parts["ebase"] = np.broadcast_to(CAPACITY * np.arange(N_EXPERTS)[None, :], (P, N_EXPERTS))
    parts["tokid"] = r + P * np.arange(NTT)[None, :]
    parts["eps"] = np.full((P, 1), EPS)
    at, n = {}, 0
    for name, m in parts.items():
        at[name] = slice(n, n + m.shape[1])
        n += m.shape[1]
    return at, np.ascontiguousarray(np.concatenate([np.asarray(m, np.float32) for m in parts.values()], 1))


class Line:

    def __init__(self, sem, names, before=0):
        self.sem, self.names, self.seen = sem, names, 0
        self.value = {n: before + i + 1 for i, n in enumerate(names)}
        assert len(self.value) == len(names)

    def __getitem__(self, name):
        return self.value[name]

    def next(self, name):
        assert self.names[self.seen] == name, (self.names[self.seen], name)
        self.seen += 1
        return self.sem


def build(nc, x, c, ctx, c_ctx, w_ada, b_ada, norm_mix_g, norm_ffn_g, w_in, na_q_norm_g, na_k_norm_g, na_rpb,
          dn_conv_w, dn_a_log, dn_dt_bias, dn_out_norm_g, sc_conv_w, w_branch_na, w_branch_dn, w_branch_sc, w_out,
          w_router, router_bias, moe_w_gate, moe_w_up, moe_w_down, const, out):
    CA, _ = constants()
    NCONST = const.shape[1]
    rpb_pad = nc.dram_tensor("rpb_pad", [DEPTH, NA_HEADS * 15, P], F32).ap()
    h_rows = [nc.dram_tensor(f"h_rows{l}", [TOK if l < DEPTH - 1 else SEQ, D_MODEL], F32).ap() for l in range(DEPTH)]
    y_rows = [nc.dram_tensor(f"y_rows{l}", [ZERO_ROW + 1, D_MODEL], F32).ap() for l in range(DEPTH)]
    comb_rows = nc.dram_tensor("comb_rows", [DEPTH, N_EXPERTS, TOK], F32).ap()
    with ExitStack() as stack:
        def sb(name, shape, dt=F32):
            return stack.enter_context(nc.sbuf_tensor(name, shape, dt))

        def sem(name):
            return stack.enter_context(nc.semaphore(name))

        X = sb("X", [P, KT, TOK])
        H = sb("H", [P, KT, TOK])
        W = sb("W", [P, RING, CHUNK])
        T = sb("T", [P, NT, TOK])
        C = sb("C", [P, NCONST])
        rows_a = [T[0:RA_N, T_ROWS, P * l:P * l + P] for l in range(DEPTH)]
        rows_b = [T[0:RB_N, T_ROWS, P * (2 + l):P * (3 + l)] for l in range(DEPTH)]
        col_a = [sb(f"col_a{l}", [P, RA_N]) for l in range(DEPTH)]
        col_b = [sb(f"col_b{l}", [P, RB_N]) for l in range(DEPTH)]
        wab = [sb(f"wab{l}", [P, KT, 16]) for l in range(DEPTH)]
        alog = [sb(f"alog{l}", [P, 8]) for l in range(DEPTH)]
        dtb = [sb(f"dtb{l}", [P, 8]) for l in range(DEPTH)]
        rpb = T[0:NA_HEADS * 15, T_ROWS + 1, 0:P * DEPTH].rearrange("r (l c) -> r l c", l=DEPTH)
        wrt = sb("wrt", [P, KT, N_EXPERTS])
        rbias = sb("rbias", [P, N_EXPERTS])
        silu_c = sb("silu_c", [P, KT, 2])
        mod = sb("mod", [P, 48, 2])
        gain = sb("gain", [P, KT, 2])
        ab = sb("ab", [P, NTT, 2, 8])
        gdec = sb("gdec", [P, 2, NTT, 4])
        tmp_g = sb("tmp_g", [P, 3, NTT, 8])
        beta = sb("beta", [P, NTT, 8])
        negG = sb("negG", [P, 2, NTT, 4])
        ea = sb("ea", [P, 8])
        zero_row = sb("zero_row", [1, P])
        glast = sb("glast", [P, 2, 4])
        mx = sb("mx", [P, 2, 4])
        rs = T[:, T_ROUTE, :].rearrange("p (i t n) -> p i t n", i=8, t=NTT)
        rcmp = T[:, T_ROUTE + 1, 0:256].rearrange("p (t g i j) -> p t g i j", t=NTT, g=N_GROUPS, i=4)
        combT = T[0:N_EXPERTS, F_COMBT, :]
        pair = T[:, T_ROUTE + 2, 0:128].rearrange("p (t n w) -> p t n w", t=NTT, n=N_EXPERTS)
        slot_comb = sb("slot_comb", [P, N_EXPERTS])
        slot_tok = sb("slot_tok", [P, N_EXPERTS], U32)
        tok_slot = sb("tok_slot", [P, 2, NTT], U32)
        flag = sb("flag", [P, 1], U32)

        bank = [stack.enter_context(nc.psum_tensor(f"bank{i}", [P, 512], F32)) for i in range(8)]

        def cm(name):
            return C[:, CA[name]]

        def cm4(name):
            return C[:, CA[name]].unsqueeze(1).broadcast_to([P, 4, P])

        def v4(ap):
            return ap.rearrange("p (h c) -> p h c", h=4)

        s_chunk = [sem(f"s_chunk{i}") for i in range(RING)]
        s_tile = [sem(f"s_tile{b}") for b in range(2)]
        s_taken = [sem(f"s_taken{b}") for b in range(2)]
        s_const, s_xin, s_rows, s_small, s_rpb, s_rpb_out, s_out = (sem(n) for n in (
            "s_const", "s_xin", "s_rows", "s_small", "s_rpb", "s_rpb_out", "s_out"))
        s_turned, s_store = sem("s_turned"), sem("s_store")
        chain = {n: sem(f"s_{n}_chain") for n in ("dve", "act", "pool")}
        links = {n: 0 for n in chain}

        def link(eng, name, ins):
            links[name] += 1
            ins.then_inc(chain[name], 1)
            eng.wait_ge(chain[name], links[name])

        def line(name, names):
            return Line(sem(name), names)

        shared = {}

        def on(name, names):
            s_, before = shared[name] if name in shared else (sem(name), 0)
            shared[name] = s_, before + len(names)
            return Line(s_, names, before)

        setup_pe = line("setup_pe", [f"x{i}" for i in range(8)] + [f"rows{i}" for i in range(2 * DEPTH)])
        setup_dve = line("setup_dve", ["rpbzero", "rpb"] + [f"x{i}" for i in range(8)] + [f"rows{i}" for i in range(2 * DEPTH)])
        setup_act = line("setup_act", ["silu_c"])

        def names_na(l):
            return [(qt, h) for qt in range(2 if l == DEPTH - 1 else 0, NTT) for h in range(NA_HEADS)]

        def need_o(l, tt):
            return tt >= 2 or l < DEPTH - 1

        CH = [[(j, d, (j if d == 0 else (1, 0, 3, 2)[j])) for j in range(4) for d in range(2)] for _ in range(1)][0]

        def dn_pe_names(l):
            return {d: [n for j, dd, tt in CH if dd == d for n in (
                [(j, "gB"), (j, "KK")] + ([(j, "QK")] if need_o(l, tt) else []) + [(j, "L")]
                + [(j, f"{w}{k}") for k in range(1, LEVELS) for w in (("Y", "Z", "ZT") if k < LEVELS - 1 else ("Y", "ZT"))]
                + ([(j, "KS")] if j else []) + [(j, "VN")] + ([(j, "O")] if need_o(l, tt) else [])
                + ([(j, "dS")] if j < 3 else []))] for d in range(2)}

        def dn_dve_names(l):
            return {d: [n for j, dd, tt in CH if dd == d for n in (
                [(j, "M"), (j, "LT"), (j, "XT0"), (j, "X0")] + ([(j, "AT")] if need_o(l, tt) else [])
                + [(j, f"{w}{k}") for k in range(1, LEVELS) for w in (("Y", "X", "XT") if k < LEVELS - 1 else ("Y", "XT"))]
                + ([(j, "R")] if j else []) + [(j, "vn")] + ([(j, "O")] if need_o(l, tt) else [])
                + ([(j, "S")] if j < 3 else []))] for d in range(2)}

        ev = []
        for l in range(DEPTH):
            e = {}
            n = f"L{l}"
            t0 = 256 if l == DEPTH - 1 else 0
            e["t0"] = t0
            e["modr"] = line(n + "modrow_pe", ["mod"])
            e["mod"] = on("mod_dve", ["mod", "gain1", "gain2"])
            for w in ("n1", "n2"):
                e[w + "sq"] = on(w + "sq_act", list(range(KT)))
                e[w + "ms"] = line(n + w + "ms_pe", ["ms"])
                e[w + "rt"] = line(n + w + "rt_act", ["rt"])
                e[w + "h"] = on(w + "h_dve", list(range(KT)))
            e["ab"] = on("ab_pe", ["ab", "G"])
            e["abd"] = on("ab_dve", ["ab", "x", "beta_g", "negG"])
            e["aba"] = on("ab_act", ["ea", "e", "ln", "sig"])
            e["sq"] = on("sq_act", list(range(20)))
            e["st"] = on("st_pe", list(range(20)))
            e["rt"] = on("rt_act", list(range(20)))
            e["nrm"] = on("nrm_dve", list(range(20)))
            e["conv"] = on("conv_dve", list(range(12)))
            e["silu"] = on("silu_act", list(range(12)) + ["z"])
            e["rot"] = on("rot_pe", list(range(8)))
            e["sc"] = line(n + "sc_dve", ["sc"])
            e["tp"] = on("tp_pe", list(range(12)))
            e["tpc"] = on("tp_act", list(range(12)))
            e["bias_ld"] = sem(n + "bias_ld")
            e["biasf"] = on("bias_pe", list(range(6)))
            e["biasm"] = line(n + "bias_dve", list(range(6)))
            nn = len(names_na(l))
            e["aS"] = on("aS_pe", list(range(nn)))
            e["aM"] = on("aM_dve", list(range(nn)))
            e["aE"] = on("aE_act", list(range(nn)))
            e["aP"] = on("aP_dve", list(range(nn)))
            e["aT"] = on("aT_pe", list(range(nn)))
            e["aC"] = on("aC_act", list(range(nn)))
            e["aO"] = line(n + "aO_pe", list(range(nn)))
            e["aD"] = line(n + "aD_dve", list(range(nn // 2)))
            pn, dn = dn_pe_names(l), dn_dve_names(l)
            e["dp"] = [line(n + f"dn_pe{d}", pn[d]) for d in range(2)]
            e["dd"] = [line(n + f"dn_dve{d}", dn[d]) for d in range(2)]
            e["da"] = [on(f"dn_act{d}", [(j, w) for j in range(4) for w in ("eg", "DT")]) for d in range(2)]
            e["dg"] = [on(f"dn_pool{d}", [(j, w) for j, dd, tt in CH if dd == d for w in ("kgl", "qg", "gl", "kg") if w != "qg" or need_o(l, tt)])
                       for d in range(2)]
            e["mgd"] = line(n + "merge_dve", list(range(TILES_MERGE // 2)))
            e["rp"] = on("router_pe", ["logits", "cnt", "flag"])
            e["hr"] = line(n + "hrow_pe", list(range(2 * NTT)))
            e["hrc"] = line(n + "hrow_act", list(range(2 * NTT)))
            e["hrd"] = sem(n + "hrow_dma")
            e["ra"] = line(n + "router_act", ["sig"])
            e["rd"] = on("router_dve", ["comb", "rk", "ov", "flag", "slots", "back"])
            e["oh"] = on("onehot_dve", list(range(N_EXPERTS)))
            e["ohp"] = line(n + "onehot_pe", list(range(N_EXPERTS)))
            e["xg"] = [sem(n + f"xg{i}") for i in range(2)]
            e["xt"] = sem(n + "xt_pe")
            e["xca"], e["xcd"] = sem(n + "xc_act"), sem(n + "xc_dve")
            e["ht"], e["hc"] = sem(n + "ht_pe"), sem(n + "hc_act")
            e["yst"] = [sem(n + f"yst{i}") for i in range(2)]
            e["bg"] = [sem(n + f"back{i}") for i in range(2)]
            e["bs"] = line(n + "back_dve", list(range(2 * NTT)))
            e["bt"] = line(n + "back_pe", list(range(2 * NTT)))
            e["bx"] = line(n + "back_x_dve", list(range(2 * NTT)))
            e["f_chunk"] = [sem(n + f"f_chunk{i}") for i in range(RING)]
            for w in ("f_tile", "f_taken", "f_cb"):
                e[w] = [sem(n + w + str(i)) for i in range(2)]
            e["f_hid"], e["f_comb"], e["f_store"] = sem(n + "f_hid"), sem(n + "f_comb"), sem(n + "f_store")
            e["x2"] = line(n + "x2_dve", ["x2"])
            ev.append(e)

        block = stack.enter_context(nc.Block())

        def chunk_wait(eng, C0, i, per, s):
            assert per % RING == 0 or isinstance(i, int)
            if isinstance(i, int):
                q = C0 + per * i + s
                eng.wait_ge(s_chunk[q % RING], 16 * (q // RING + 1))
            else:
                q = C0 + s
                eng.wait_ge(s_chunk[q % RING], i * (16 * per // RING) + 16 * (q // RING + 1))

        def w_view(C_, k):
            return W[:, C_ % RING, :].rearrange("p (k n) -> p k n", k=k)

        @block.sync
        def _(sp):
            def load(C_, src, k):
                sp.dma_start(w_view(C_, k), src).then_inc(s_chunk[C_ % RING], 16)

            def room(C_):
                if C_ >= RING:
                    u = last_tile_of(C_ - RING)
                    sp.wait_ge(s_tile[u % 2], u // 2 + 1)

            for l in range(DEPTH):
                base = CHUNKS_LAYER * l
                wa = w_ada[l].rearrange("(k p) n -> p k n", p=P)
                for s in range(RING):
                    room(base + s)
                    load(base + s, wa[:, :, 256 * s:256 * (s + 1)], KT)
                with sp.Fori(1, CHUNKS_ADA // RING) as i:
                    for s in range(RING):
                        u = TILES_LAYER * l + s
                        sp.wait_ge(s_tile[u % 2], i * (RING // 2) + (u // 2 + 1 - RING // 2))
                        load(base + s, wa[:, :, bass.ds(i * (256 * RING) + 256 * s, 256)], KT)
                q = base + CHUNKS_ADA
                wi = w_in[l].rearrange("(k p) n -> p k n", p=P)
                cols = ([COL_NA + 256 * i for i in range(6)] + [COL_DN + 256 * i for i in range(6)]
                        + [COL_SC + 256 * i for i in range(6)] + [COL_Z + 256 * i for i in range(2)])
                for c0 in cols:
                    room(q)
                    load(q, wi[:, :, c0:c0 + 256], KT)
                    q += 1
                for hf in range(2):
                    for b, wb in enumerate((w_branch_na, w_branch_dn, w_branch_sc)):
                        room(q)
                        load(q, wb[l].rearrange("(k p) n -> p k n", p=P)[:, :, 512 * hf:512 * (hf + 1)], 4)
                        q += 1
                        for i in range(2):
                            c0 = COL_GATE + D_MODEL * b + 512 * hf + 256 * i
                            room(q)
                            load(q, wi[:, :, c0:c0 + 256], KT)
                            q += 1
                for i in range(4):
                    room(q)
                    load(q, w_out[l].rearrange("(k p) n -> p k n", p=P)[:, :, 256 * i:256 * (i + 1)], KT)
                    q += 1

                def expert(e, s, q):
                    wg, wu, wd = (m[l, bass.ds(e, 1)] if not isinstance(e, int) else m[l, e:e + 1]
                                  for m in (moe_w_gate, moe_w_up, moe_w_down))
                    if s < 4:
                        src = (wg, wu)[s // 2].rearrange("e (k p) n -> p (e k) n", p=P)[:, 4 * (s % 2):4 * (s % 2) + 4, :]
                    else:
                        src = wd.rearrange("e (k p) n -> p (e k) n", p=P)[:, :, 512 * (s - 4):512 * (s - 3)]
                    load(q, src, 4)

                for s in range(6):
                    room(q + s)
                    expert(0, s, q + s)
                with sp.Fori(1, N_EXPERTS) as e:
                    for s in range(6):
                        u = last_tile_of(q + s)
                        sp.wait_ge(s_tile[u % 2], e * 2 + (u // 2 - 1))
                        expert(e, s, q + s)

                E = ev[l]
                sp.wait_ge(E["rd"].sem, E["rd"]["flag"])
                with sp.If(sp.value_load(flag[0:1, 0:1], min_val=0, max_val=1) > 0):
                    for s in range(6):
                        u = last_tile_of(q + 6 * (N_EXPERTS - 1) + s)
                        sp.wait_ge(s_tile[u % 2], u // 2 + 1)

                    def f_load(x_, s):
                        wg, wu, wd = (m[l, bass.ds(x_, 1)] if not isinstance(x_, int) else m[l, x_:x_ + 1]
                                      for m in (moe_w_gate, moe_w_up, moe_w_down))
                        if s < 4:
                            src = (wg, wu)[s % 2].rearrange("e (k p) n -> p (e k) n", p=P)[:, :, 256 * (s // 2):256 * (s // 2 + 1)]
                        else:
                            src = wd.rearrange("e (k p) n -> p (e k) n", p=P)[:, :, 512 * (s - 4):512 * (s - 3)]
                        sp.dma_start(w_view(s, KT if s < 4 else 4), src).then_inc(E["f_chunk"][s], 16)
                    for s in range(6):
                        f_load(0, s)
                    with sp.Fori(1, N_EXPERTS) as x_:
                        for s in range(6):
                            sp.wait_ge(E["f_tile"][1], x_ * 8 + ((2, 4, 6, 8, 12, 16)[s] // 2 - 8))
                            f_load(x_, s)
                    sp.wait_ge(E["f_tile"][1], 8 * N_EXPERTS)

        @block.gpsimd
        def _(pool):
            gp = nc.gpsimd
            pool.dma_start(C[:], const).then_inc(s_const, 16)
            for i in range(NTT):
                src = (ctx if i < 2 else x)[0].rearrange("(t p) d -> t p d", p=P)[i % 2]
                pool.dma_start(T[:, 2 * i:2 * i + 2, :].rearrange("p a b -> p (a b)"), src).then_inc(s_xin, 16)
            for l in range(DEPTH):
                for r0, n, src in ((RA_B, 48, b_ada[l]), (RA_MIX, 8, norm_mix_g[l]), (RA_FFN, 8, norm_ffn_g[l]),
                                   (RA_C, 8, c[0]), (RA_C + 8, 8, c_ctx)):
                    pool.dma_start(rows_a[l][r0:r0 + n, :], src.rearrange("(n p) -> n p", p=P)).then_inc(s_rows, 16)
                pool.dma_start(rows_b[l][RB_CONV:RB_SC, :], dn_conv_w[l].rearrange("t (n p) -> (t n) p", p=P)).then_inc(s_rows, 16)
                pool.dma_start(rows_b[l][RB_SC:RB_OUT, :], sc_conv_w[l].rearrange("t (n p) -> (t n) p", p=P)).then_inc(s_rows, 16)
                pool.dma_start(rows_b[l][RB_OUT:RB_QG, :], dn_out_norm_g[l].rearrange("(n p) -> n p", p=P)).then_inc(s_rows, 16)
                for r, g in ((RB_QG, na_q_norm_g), (RB_KG, na_k_norm_g)):
                    for i in range(2):
                        pool.dma_start(rows_b[l][r:r + 1, 64 * i:64 * i + 64], g[l:l + 1]).then_inc(s_rows, 16)
                pool.dma_start(wab[l][:], w_in[l].rearrange("(k p) n -> p k n", p=P)[:, :, COL_AB:COL_AB + 16]).then_inc(s_small, 16)
                pool.dma_start(alog[l][:], dn_a_log[l].rearrange("(a d) h -> a (d h)", a=1).broadcast_to([P, 8])).then_inc(s_small, 16)
                pool.dma_start(dtb[l][:], dn_dt_bias[l].rearrange("(a d) h -> a (d h)", a=1).broadcast_to([P, 8])).then_inc(s_small, 16)
            pool.dma_start(wrt[:], w_router.rearrange("(k p) n -> p k n", p=P)).then_inc(s_small, 16)
            pool.dma_start(rbias[:], router_bias.rearrange("(a n) -> a n", a=1).broadcast_to([P, N_EXPERTS])).then_inc(s_small, 16)
            pool.wait_ge(setup_dve.sem, setup_dve["rpbzero"])
            for l in range(DEPTH):
                pool.dma_start(rpb[:, l, 48:79], na_rpb[l].rearrange("h r c -> (h r) c")).then_inc(s_rpb, 16)
            pool.wait_ge(setup_dve.sem, setup_dve["rpb"])
            for l in range(DEPTH):
                pool.dma_start(rpb_pad[l], rpb[:, l, :]).then_inc(s_rpb_out, 16)
            pool.wait_ge(s_rpb_out, 16 * DEPTH)
            for l in range(DEPTH):
                e = ev[l]
                if l:
                    pool.wait_ge(ev[l - 1]["x2"].sem, 1)
                bview = T[:, T_BIAS:T_BIAS + 6, :].rearrange("p a b -> p (a b)").rearrange("p (h j c) -> p h j c", h=8, j=6)
                for qr in range(2):
                    for h in range(NA_HEADS):
                        src = bass.AP(rpb_pad.tensor, l * 120 * P + (h * 15 + 5 - qr) * P, [[1, 64], [P, 6], [1, 64]])
                        pool.dma_start(bview[64 * qr:64 * qr + 64, h], src).then_inc(e["bias_ld"], 16)
                for j, d, tt in CH:
                    dd, da, dp, dg = e["dd"][d], e["da"][d], e["dp"][d], e["dg"][d]
                    wt = [T[:, T_WORK[d][i], :] for i in range(8)]
                    DT, EG, QG, KGL = wt[0], wt[1], wt[6], wt[7]
                    last = 127 if d == 0 else 0
                    ts_ = slice(P * tt, P * tt + P)
                    if j:
                        pool.wait_ge(dp.sem, dp[(j - 1, "dS")])
                    if j == 0:
                        pool.wait_ge(e["tpc"].sem, e["tpc"][11])
                        pool.wait_ge(e["nrm"].sem, e["nrm"][15])
                        pool.wait_ge(e["aD"].sem, len(names_na(l)) // 2)
                    pool.wait_ge(da.sem, da[(j, "DT")])
                    kt = T[:, T_KTOK_DN + tt, :]
                    gp.tensor_tensor(v4(KGL), v4(kt), v4(DT)[:, :, last:last + 1].broadcast_to([P, 4, P]),
                                     ALU.mult).then_inc(dg.next((j, "kgl")), 1)
                    if need_o(l, tt):
                        gp.tensor_tensor(v4(QG), T[:, T_DQ:T_DQ + 4, ts_], v4(EG), ALU.mult).then_inc(dg.next((j, "qg")), 1)
                    if j:
                        pool.wait_ge(dd.sem, dd[(j - 1, "S")])
                    gp.tensor_copy(glast[:, d, :], v4(EG)[:, :, last]).then_inc(dg.next((j, "gl")), 1)
                    pool.wait_ge(dg.sem, dg[(j, "gl")])
                    gp.tensor_tensor(v4(EG), T[:, T_DK:T_DK + 4, ts_], v4(EG), ALU.mult).then_inc(dg.next((j, "kg")), 1)
                for tt in range(e["t0"] // P, NTT):
                    pool.wait_ge(e["hrc"].sem, 2 * tt + 2 - e["t0"] // 64)
                    pool.dma_start(h_rows[l][P * tt - e["t0"]:P * tt - e["t0"] + P, :], T[:, T_HROW + 2 * tt:T_HROW + 2 * tt + 2, :].rearrange("p a b -> p (a b)"))\
                        .then_inc(e["hrd"], 16)
                for i in range(2):
                    pool.dma_start(y_rows[l][ZERO_ROW:ZERO_ROW + 1, 512 * i:512 * i + 512].rearrange("a (r n) -> a r n", n=P),
                                   zero_row[:].unsqueeze(1).broadcast_to([1, 4, P])).then_inc(e["yst"][i], 16)
                pool.wait_ge(e["hrd"], 16 * (NTT - e["t0"] // P))
                pool.wait_ge(e["rd"].sem, e["rd"]["slots"])
                UE = TILES_LAYER * (l + 1) - N_EXPERTS * TILES_EXP

                def gather_x(x_):
                    pool.indirect_dma_start(T[:, T_XROW + 2 * (x_ % 2):T_XROW + 2 * (x_ % 2) + 2, :].rearrange("p a b -> p (a b)"), None,
                                            h_rows[l], bass.IndirectOffsetOnAxis(ap=slot_tok[:, x_:x_ + 1], axis=0)).then_inc(e["xg"][x_ % 2], 16)
                gather_x(0)
                gather_x(1)
                for x_ in range(N_EXPERTS):
                    if x_ + 2 < N_EXPERTS:
                        pool.wait_ge(e["xt"], 2 * (x_ + 1))
                        gather_x(x_ + 2)
                    u = UE + TILES_EXP * x_ + 2
                    pool.wait_ge(s_taken[0], u // 2 + 2)
                    pool.wait_ge(s_taken[1], u // 2 + 2)
                    pool.dma_start(y_rows[l][CAPACITY * x_:CAPACITY * (x_ + 1), :],
                                   T[:, T_Y + 2 * (x_ % 2):T_Y + 2 * (x_ % 2) + 2, :].rearrange("p a b -> p (a b)")).then_inc(e["yst"][x_ % 2], 16)
                for i in range(2):
                    pool.wait_ge(e["yst"][i], 16 * (N_EXPERTS // 2 + 1))
                for n_, tt in enumerate(range(e["t0"] // P, NTT)):
                    if n_ >= 2:
                        pool.wait_ge(e["bt"].sem, 2 * (n_ - 2) + 2)
                    for i in range(2):
                        t_ = T_GATHER + 4 * (n_ % 2) + 2 * i
                        pool.indirect_dma_start(T[:, t_:t_ + 2, :].rearrange("p a b -> p (a b)"), None, y_rows[l],
                                                bass.IndirectOffsetOnAxis(ap=tok_slot[:, i, tt:tt + 1], axis=0)).then_inc(e["bg"][n_ % 2], 16)

                pool.wait_ge(e["rd"].sem, e["rd"]["flag"])
                with pool.If(pool.value_load(flag[0:1, 0:1], min_val=0, max_val=1) > 0):
                    pool.wait_ge(e["f_comb"], 2)
                    pool.dma_start(comb_rows[l, :, e["t0"]:], combT[:, e["t0"]:]).then_inc(e["f_store"], 16)
                    pool.wait_ge(e["f_store"], 16)

                    def spread(x_, i):
                        src = comb_rows[l, bass.ds(x_, 1)] if not isinstance(x_, int) else comb_rows[l, x_:x_ + 1]
                        pool.dma_start(T[:, F_CB + i, e["t0"]:], src[:, e["t0"]:].broadcast_to([P, TOK - e["t0"]])).then_inc(e["f_cb"][i], 16)
                    for i in range(2):
                        spread(i, i)
                    with pool.Fori(1, N_EXPERTS // 2) as p_:
                        for i in range(2):
                            pool.wait_ge(e["f_hid"], p_ * 8 + 4 * i)
                            spread(p_ * 2 + i, i)

        @block.tensor
        def _(pe):
            mm = nc.tensor.matmul

            def tp(out_, in_):
                k = in_.shape[0]
                return nc.tensor.transpose(out_, in_, C[0:k, CA["ident"]][:, 0:k])

            def tile(U0, per, i, j, pairs):
                u = U0 + j
                b = u % 2
                if isinstance(i, int):
                    pe.wait_ge(s_taken[b], (u + per * i) // 2 + 1)
                else:
                    pe.wait_ge(s_taken[b], i * (per // 2) + (u // 2 + 1))
                n = len(pairs)
                for k, (a_, r_) in enumerate(pairs):
                    w_ = r_.shape[1]
                    last = mm(bank[b][:, TOK - w_:TOK], a_, r_, start=(k == 0), stop=(k == n - 1))
                last.then_inc(s_tile[b], 1)

            pe.wait_ge(s_const, 16)
            pe.wait_ge(s_xin, 16 * NTT)
            for k in range(KT):
                if k >= 6:
                    pe.wait_ge(setup_dve.sem, setup_dve[f"x{k - 6}"])
                for i in range(NTT):
                    m_ = tp(bank[2 + k % 6][:, P * i:P * i + P], T[:, 2 * i + k // 4, P * (k % 4):P * (k % 4) + P])
                m_.then_inc(setup_pe.next(f"x{k}"), 1)
            pe.wait_ge(s_rows, 16 * 12 * DEPTH)
            for i in range(2 * DEPTH):
                rows_, n = ((rows_a, RA_N), (rows_b, RB_N))[i % 2]
                if i >= 2:
                    pe.wait_ge(setup_dve.sem, setup_dve[f"rows{i - 2}"])
                tp(bank[i % 2][:, 0:n], rows_[i // 2]).then_inc(setup_pe.next(f"rows{i}"), 1)
            pe.wait_ge(setup_dve.sem, setup_dve[f"rows{2 * DEPTH - 1}"])
            pe.wait_ge(setup_act.sem, 1)

            for l in range(DEPTH):
                e = ev[l]
                t0 = e["t0"]
                q = CHUNKS_LAYER * l
                U = TILES_LAYER * l
                lat, full = slice(t0, TOK), slice(0, TOK)

                if l:
                    pe.wait_ge(ev[l - 1]["x2"].sem, 1)
                with pe.Fori(0, CHUNKS_ADA // RING) as i:
                    for s in range(RING):
                        chunk_wait(pe, q, i, RING, s)
                        b = (U + s) % 2
                        pe.wait_ge(s_taken[b], i * (RING // 2) + ((U + s) // 2 + 1))
                        for k in range(KT):
                            last = mm(bank[b][0:2, 0:256], silu_c[:, k, :], w_view(q + s, KT)[:, k, :], start=(k == 0), stop=(k == KT - 1))
                        last.then_inc(s_tile[b], 1)
                q += CHUNKS_ADA
                U += TILES_ADA
                for b in range(2):
                    pe.wait_ge(s_taken[b], U // 2 + 1)
                for i in range(48):
                    last = tp(bank[2][:, 2 * i:2 * i + 2], T[0:2, T_MODROW + i // 4, P * (i % 4):P * (i % 4) + P])
                last.then_inc(e["modr"].next("mod"), 1)

                def mean_square(w, bk):
                    for k in range(KT):
                        pe.wait_ge(e[w + "sq"].sem, e[w + "sq"][k])
                        last = mm(bk[:, :], cm("ones"), T[:, k, :], start=(k == 0), stop=(k == KT - 1))
                    last.then_inc(e[w + "ms"].next("ms"), 1)

                mean_square("n1", bank[3])
                pe.wait_ge(e["bias_ld"], 16 * 16)
                for i in range(6):
                    if i >= 4:
                        pe.wait_ge(e["biasm"].sem, e["biasm"][i - 4])
                    mm(bank[4 + i % 4][:, :], cm("flip"), T[:, T_BIAS + i, :], start=True, stop=True).then_inc(e["biasf"].next(i), 1)
                for k in range(KT):
                    pe.wait_ge(e["n1h"].sem, e["n1h"][k])
                with pe.Fori(0, 2) as i:
                    for s in range(6):
                        chunk_wait(pe, q, i, 6, s)
                        cols = lat if s < 2 else full
                        for m in range(2):
                            tile(U, 12, i, 2 * s + m, [(w_view(q + s, KT)[:, k, P * m:P * m + P], H[:, k, cols]) for k in range(KT)])
                q += 12
                U += 24
                pe.wait_ge(s_small, 16 * (3 * DEPTH + 2))
                for tt in range(NTT):
                    for k in range(KT):
                        last = mm(bank[3][:, 16 * tt:16 * tt + 16], H[:, k, P * tt:P * tt + P], wab[l][:, k, :],
                                  start=(k == 0), stop=(k == KT - 1))
                last.then_inc(e["ab"].next("ab"), 1)

                def stat(n_, src, w_, cols):
                    pe.wait_ge(e["sq"].sem, e["sq"][n_])
                    if n_ >= 2:
                        pe.wait_ge(e["rt"].sem, e["rt"][n_ - 2])
                    mm(bank[4 + n_ % 2][:, cols], cm(w_), T[:, T_SQ + n_ % 2, cols], start=True, stop=True)\
                        .then_inc(e["st"].next(n_), 1)

                for s in range(8):
                    chunk_wait(pe, q, 0, 0, s)
                    for m in range(2):
                        j = 2 * s + m
                        tile(U, 0, 0, j, [(w_view(q + s, KT)[:, k, P * m:P * m + P], H[:, k, lat]) for k in range(KT)])
                        isq = j % 8 < 4
                        if j == 2:
                            pe.wait_ge(e["abd"].sem, e["abd"]["beta_g"])
                            for d in range(2):
                                g_ = mm(bank[3][:, 64 + 16 * d:80 + 16 * d], cm(f"tri{d}"), gdec[:, d].rearrange("p t h -> p (t h)"),
                                        start=True, stop=True)
                            g_.then_inc(e["ab"].next("G"), 1)
                        if j == 0:
                            pe.wait_ge(e["biasm"].sem, 6)
                        stat(j, None, "ones64" if j < 8 else "ones", lat if isq else full)
                        if j >= 8:
                            r_ = j - 8
                            if r_ >= 2:
                                pe.wait_ge(e["nrm"].sem, e["nrm"][j - 2])
                            mm(bank[6 + r_ % 2][:, 0:256], cm("rot"), T[:, T_DQ + r_, 256:512], start=True, stop=True)\
                                .then_inc(e["rot"].next(r_), 1)
                q += 8
                U += 16

                for n_ in range(12):
                    what, tt = divmod(n_, 4)
                    src = (T_NV, T_DK, T_DV)[what]
                    if n_ == 0:
                        pe.wait_ge(e["silu"].sem, e["silu"]["z"])
                        pe.wait_ge(e["nrm"].sem, e["nrm"][15])
                        pe.wait_ge(e["silu"].sem, e["silu"][11])
                    if n_ >= 2:
                        pe.wait_ge(e["tpc"].sem, e["tpc"][n_ - 2])
                    for i in range(4):
                        last = tp(bank[6 + n_ % 2][:, P * i:P * i + P], T[:, src + i, P * tt:P * tt + P])
                    last.then_inc(e["tp"].next(n_), 1)

                items = names_na(l)
                N = len(items)
                pe.wait_ge(e["tpc"].sem, e["tpc"][11])
                pe.wait_ge(e["abd"].sem, e["abd"]["negG"])
                for n_ in range(N + 2):
                    if n_ < N:
                        qt, h = items[n_]
                        keys = CTX_LEN if qt < 2 else TOK
                        hp = slice(64 * (h % 2), 64 * (h % 2) + 64)
                        if n_ >= 2:
                            pe.wait_ge(e["aE"].sem, e["aE"][n_ - 2])
                        mm(bank[2 + n_ % 2][:, 0:keys], T[hp, T_NQ + h // 2, P * qt:P * qt + P], T[hp, T_NK + h // 2, 0:keys],
                           start=True, stop=True).then_inc(e["aS"].next(n_), 1)
                    if 1 <= n_ <= N:
                        m_ = n_ - 1
                        qt, h = items[m_]
                        nk = 2 if qt < 2 else 4
                        pe.wait_ge(e["aP"].sem, e["aP"][m_])
                        if m_ >= 2:
                            pe.wait_ge(e["aC"].sem, e["aC"][m_ - 2])
                        for i in range(nk):
                            last = tp(bank[4 + m_ % 2][:, P * i:P * i + P], T[:, T_E + m_ % 2, P * i:P * i + P])
                        last.then_inc(e["aT"].next(m_), 1)
                    if n_ >= 2:
                        m_ = n_ - 2
                        qt, h = items[m_]
                        nk = 2 if qt < 2 else 4
                        pe.wait_ge(e["aC"].sem, e["aC"][m_])
                        if m_ >= 4 and m_ % 2 == 0:
                            pe.wait_ge(e["aD"].sem, e["aD"][m_ // 2 - 2])
                        hp = slice(64 * (h % 2), 64 * (h % 2) + 64)
                        for i in range(nk):
                            last = mm(bank[6 + m_ // 2 % 2][hp, 0:P], T[:, T_VTOK + i, 64 * h:64 * h + 64],
                                      T[:, T_PT + m_ % 2, P * i:P * i + P], start=(i == 0), stop=(i == nk - 1))
                        last.then_inc(e["aO"].next(m_), 1)

                pe.wait_ge(e["aD"].sem, N // 2)
                pe.wait_ge(e["abd"].sem, e["abd"]["negG"])
                for j in range(4):
                    grp = [g for g in CH if g[0] == j]

                    def both(f):
                        for g in grp:
                            f(*g)

                    def ctx_of(d):
                        wt = [v4(T[:, T_WORK[d][i], :]) for i in range(8)]
                        return e["dp"][d], e["dd"][d], e["da"][d], e["dg"][d], wt, [v4(bank[2 + 3 * d + i][:, :]) for i in range(3)]

                    def gB(j, d, tt):
                        dp, dd, da, dg, wt, bk = ctx_of(d)
                        ts_ = slice(P * tt, P * tt + P)
                        if j:
                            pe.wait_ge(dd.sem, dd[(j - 1, "S")])
                        for h in range(4):
                            last = mm(bk[0][:, h], gdec[:, d, tt, h:h + 1].broadcast_to([P, P]), cm(f"tri{d}"), start=True, stop=True)
                        last.then_inc(dp.next((j, "gB")), 1)
                        for h in range(4):
                            last = mm(bk[1][:, h], T[:, T_DK + h, ts_], T[:, T_DK + h, ts_], start=True, stop=True)
                        last.then_inc(dp.next((j, "KK")), 1)
                        if need_o(l, tt):
                            for h in range(4):
                                last = mm(bk[2][:, h], T[:, T_DK + h, ts_], T[:, T_DQ + h, ts_], start=True, stop=True)
                            last.then_inc(dp.next((j, "QK")), 1)

                    def L(j, d, tt):
                        dp, dd, da, dg, wt, bk = ctx_of(d)
                        pe.wait_ge(dd.sem, dd[(j, "LT")])
                        for h in range(4):
                            last = tp(bk[1][:, h], wt[2][:, h])
                        last.then_inc(dp.next((j, "L")), 1)

                    def Y(k):
                        def f(j, d, tt):
                            dp, dd, da, dg, wt, bk = ctx_of(d)
                            pe.wait_ge(dd.sem, dd[(j, "X0" if k == 1 else f"X{k - 1}")])
                            pe.wait_ge(da.sem, da[(j, "eg")])
                            for h in range(4):
                                last = mm(bk[0][:, h], wt[2][:, h], wt[3][:, h], start=True, stop=True)
                            last.then_inc(dp.next((j, f"Y{k}")), 1)
                        return f

                    def Z(k):
                        def f(j, d, tt):
                            dp, dd, da, dg, wt, bk = ctx_of(d)
                            pe.wait_ge(dd.sem, dd[(j, f"Y{k}")])
                            if k < LEVELS - 1:
                                for h in range(4):
                                    last = mm(bk[1][:, h], wt[4][:, h], wt[5][:, h], start=True, stop=True)
                                last.then_inc(dp.next((j, f"Z{k}")), 1)
                            for h in range(4):
                                last = mm(bk[2][:, h], wt[5][:, h], wt[4][:, h], start=True, stop=True)
                            last.then_inc(dp.next((j, f"ZT{k}")), 1)
                        return f

                    def KS(j, d, tt):
                        if not j:
                            return
                        dp, dd, da, dg, wt, bk = ctx_of(d)
                        S = v4(T[:, T_STATE + d, :])
                        pe.wait_ge(dg.sem, dg[(j, "kg")])
                        for h in range(4):
                            last = mm(bk[1][:, h], wt[1][:, h], S[:, h], start=True, stop=True)
                        last.then_inc(dp.next((j, "KS")), 1)

                    def VN(j, d, tt):
                        dp, dd, da, dg, wt, bk = ctx_of(d)
                        pe.wait_ge(dd.sem, dd[(j, f"XT{LEVELS - 1}")])
                        R = v4(T[:, T_VTOK_DN + tt, :])
                        if j:
                            pe.wait_ge(dd.sem, dd[(j, "R")])
                            R = wt[5]
                        for h in range(4):
                            last = mm(bk[0][:, h], wt[4][:, h], R[:, h], start=True, stop=True)
                        last.then_inc(dp.next((j, "VN")), 1)

                    def O(j, d, tt):
                        dp, dd, da, dg, wt, bk = ctx_of(d)
                        S = v4(T[:, T_STATE + d, :])
                        pe.wait_ge(dd.sem, dd[(j, "vn")])
                        pe.wait_ge(dg.sem, dg[(j, "kg")])
                        if need_o(l, tt):
                            for h in range(4):
                                if j:
                                    mm(bk[2][:, h], S[:, h], wt[6][:, h], start=True, stop=False)
                                last = mm(bk[2][:, h], wt[3][:, h], wt[0][:, h], start=(j == 0), stop=True)
                            last.then_inc(dp.next((j, "O")), 1)
                        if j < 3:
                            for h in range(4):
                                last = mm(bk[1][:, h], wt[7][:, h], wt[3][:, h], start=True, stop=True)
                            last.then_inc(dp.next((j, "dS")), 1)

                    both(gB)
                    both(L)
                    for k in range(1, LEVELS):
                        both(Y(k))
                        both(Z(k))
                    both(KS)
                    both(VN)
                    both(O)

                for i in range(4):
                    if i == 0:
                        pe.wait_ge(e["dd"][0].sem, len(e["dd"][0].names))
                        pe.wait_ge(e["dd"][1].sem, len(e["dd"][1].names))
                    stat(16 + i, None, "ones", lat)

                pe.wait_ge(e["nrm"].sem, e["nrm"][19])
                pe.wait_ge(e["sc"].sem, 1)
                for hf in range(2):
                    for b in range(3):
                        src = (T_NQ, T_Z, T_U)[b]
                        for s in range(3):
                            chunk_wait(pe, q, 0, 0, s)
                            if s == 0:
                                for m in range(4):
                                    tile(U, 0, 0, m, [(w_view(q, 4)[:, k, P * m:P * m + P], T[:, src + k, lat]) for k in range(4)])
                            else:
                                for m in range(2):
                                    tile(U, 0, 0, 2 + 2 * s + m, [(w_view(q + s, KT)[:, k, P * m:P * m + P], H[:, k, lat]) for k in range(KT)])
                        q += 3
                        U += 8
                pe.wait_ge(e["mgd"].sem, TILES_MERGE // 2)
                for s in range(4):
                    chunk_wait(pe, q, 0, 0, s)
                    for m in range(2):
                        tile(U, 0, 0, 2 * s + m, [(w_view(q + s, KT)[:, k, P * m:P * m + P], T[:, T_MERGED + k, lat]) for k in range(KT)])
                q += 4
                U += 8
                mean_square("n2", bank[3])
                for k in range(KT):
                    pe.wait_ge(e["n2h"].sem, e["n2h"][k])
                for tt in range(t0 // P, NTT):
                    for k in range(KT):
                        last = mm(bank[4][:, 16 * tt:16 * tt + 16], H[:, k, P * tt:P * tt + P], wrt[:, k, :],
                                  start=(k == 0), stop=(k == KT - 1))
                last.then_inc(e["rp"].next("logits"), 1)
                for n_ in range(t0 // 64, 2 * NTT):
                    tt, hf = divmod(n_, 2)
                    if n_ >= t0 // 64 + 2:
                        pe.wait_ge(e["hrc"].sem, e["hrc"][n_ - 2] - t0 // 64)
                    for i in range(4):
                        last = tp(bank[6 + n_ % 2][:, P * i:P * i + P], H[:, 4 * hf + i, P * tt:P * tt + P])
                    last.then_inc(e["hr"].sem, 1)
                pe.wait_ge(e["rd"].sem, e["rd"]["comb"])
                for tt in range(t0 // P, NTT):
                    for t_ in range(t0 // P, tt + 1):
                        last = mm(bank[5][:, 16 * tt:16 * tt + 16], cm("ones" if t_ < tt else "tri0"), rs[:, 2, t_, :],
                                  start=(t_ == t0 // P), stop=(t_ == tt))
                last.then_inc(e["rp"].next("cnt"), 1)
                for x_ in range(N_EXPERTS):
                    pe.wait_ge(e["oh"].sem, e["oh"][x_])
                    for tt in range(t0 // P, NTT):
                        last = mm(bank[4][:, 2 * x_:2 * x_ + 2], T[:, T_ONEHOT + x_ % 2, P * tt:P * tt + P], pair[:, tt, x_, :],
                                  start=(tt == t0 // P), stop=(tt == NTT - 1))
                    last.then_inc(e["ohp"].next(x_), 1)
                pe.wait_ge(e["rd"].sem, e["rd"]["ov"])
                mm(bank[5][:, 256:257], cm("ones"), mx[:, 0, 0:1], start=True, stop=True).then_inc(e["rp"].next("flag"), 1)

                def rows_turned(i, x_, first):
                    if first:
                        pe.wait_ge(e["xg"][i], 16)
                        pe.wait_ge(e["hrc"].sem, 2 * NTT - t0 // 64)
                    else:
                        pe.wait_ge(e["xg"][i], (x_ - i) * 8 + 16)
                        pe.wait_ge(e["xca"], x_)
                        pe.wait_ge(e["xcd"], x_)
                    for hf in range(2):
                        for k in range(4):
                            last = tp(bank[2 + hf][:, P * k:P * k + P], T[:, T_XROW + 2 * i + hf, P * k:P * k + P])
                        last.then_inc(e["xt"], 1)

                def expert(p_, i, tail):
                    xt = T[:, T_XT + 2 * i:T_XT + 2 * i + 2, :].rearrange("p a (k s) -> p (a k) s", k=4)
                    pe.wait_ge(e["xca"], p_ * 2 + (i + 1))
                    pe.wait_ge(e["xcd"], p_ * 2 + (i + 1))
                    for t_ in range(2):
                        pe.wait_ge(s_taken[t_], p_ * 4 + (2 * i + (U + t_) // 2 + 1))
                        for c_ in range(2):
                            C_ = q + 6 * i + 2 * t_ + c_
                            pe.wait_ge(s_chunk[C_ % RING], p_ * 32 + 16 * (C_ // RING + 1))
                            for k in range(4):
                                last = mm(bank[t_][:, :], xt[:, 4 * c_ + k, :], w_view(C_, 4)[:, k, :], start=(c_ + k == 0), stop=(c_ + k == 4))
                        last.then_inc(s_tile[t_], 1)
                    if not tail:
                        rows_turned(1 - i, p_ * 2 + (i + 1), False)
                    pe.wait_ge(s_taken[1], p_ * 4 + (2 * i + U // 2 + 2))
                    for k in range(4):
                        last = tp(bank[4 + i][:, P * k:P * k + P], T[:, T_HID + i, P * k:P * k + P])
                    last.then_inc(e["ht"], 1)
                    pe.wait_ge(e["hc"], p_ * 2 + (i + 1))
                    for t_ in range(2):
                        C_ = q + 6 * i + 4 + t_
                        pe.wait_ge(s_taken[t_], p_ * 4 + (2 * i + (U + 2 + t_) // 2 + 1))
                        pe.wait_ge(s_chunk[C_ % RING], p_ * 32 + 16 * (C_ // RING + 1))
                        for k in range(4):
                            last = mm(bank[t_][:, :], T[:, T_HT + i, P * k:P * k + P], w_view(C_, 4)[:, k, :], start=(k == 0), stop=(k == 3))
                        last.then_inc(s_tile[t_], 1)

                rows_turned(0, 0, True)
                pe.wait_ge(e["rd"].sem, e["rd"]["flag"])
                with pe.Fori(0, N_EXPERTS // 2 - 1) as p_:
                    expert(p_, 0, False)
                    expert(p_, 1, False)
                expert(N_EXPERTS // 2 - 1, 0, False)
                expert(N_EXPERTS // 2 - 1, 1, True)
                q += 6 * N_EXPERTS
                U += N_EXPERTS * TILES_EXP
                for n_ in range(2 * (NTT - t0 // P)):
                    pe.wait_ge(e["bs"].sem, n_ + 1)
                    if n_ >= 2:
                        pe.wait_ge(e["bx"].sem, n_ - 1)
                    for k in range(4):
                        last = tp(bank[6 + n_ % 2][:, P * k:P * k + P], T[:, T_GATHER + 4 * (n_ // 2 % 2) + n_ % 2, P * k:P * k + P])
                    last.then_inc(e["bt"].sem, 1)

                with pe.If(pe.value_load(flag[0:1, 0:1], min_val=0, max_val=1) > 0):
                    pe.wait_ge(e["f_hid"], 1)
                    for tt in range(t0 // P, NTT):
                        last = tp(bank[5][0:16, P * tt:P * tt + P], rs[:, 6, tt, :])
                    last.then_inc(e["f_comb"], 1)
                    with pe.Fori(0, N_EXPERTS) as x_:
                        for s in range(6):
                            pe.wait_ge(e["f_chunk"][s], x_ * 16 + 16)
                            if s == 4:
                                pe.wait_ge(e["f_hid"], x_ * 4 + 8)
                            for m in range(2 if s < 4 else 4):
                                j = 2 * s + m if s < 4 else 4 * s - 8 + m
                                pe.wait_ge(e["f_taken"][j % 2], x_ * 8 + (j // 2 + 1))
                                n = KT if s < 4 else 4
                                for k in range(n):
                                    last = mm(bank[j % 2][:, lat], w_view(s, n)[:, k, P * m:P * m + P], H[:, k, lat] if s < 4 else T[:, F_HID + k, lat],
                                              start=(k == 0), stop=(k == n - 1))
                                last.then_inc(e["f_tile"][j % 2], 1)

            pe.wait_ge(ev[-1]["x2"].sem, 1)
            for tt in range(2):
                for hf in range(2):
                    for i in range(4):
                        last = tp(bank[2 + 2 * tt + hf][:, P * i:P * i + P], X[:, 4 * hf + i, CTX_LEN + P * tt:CTX_LEN + P * tt + P])
            last.then_inc(s_turned, 1)

        @block.scalar
        def _(act):
            sc = nc.scalar
            eps = C[:, CA["eps"]]
            act.wait_ge(setup_dve.sem, setup_dve["rows0"])
            for v in range(2):
                last = sc.activation(silu_c[:, :, v], col_a[0][:, RA_C + 8 * v:RA_C + 8 * v + 8], ACT.Silu)
            last.then_inc(setup_act.next("silu_c"), 1)

            for l in range(DEPTH):
                e = ev[l]
                t0 = e["t0"]
                U = TILES_LAYER * l
                lat, full = slice(t0, TOK), slice(0, TOK)

                def taken(u, ins):
                    ins.then_inc(s_taken[u % 2], 1)

                def squares(w):
                    for k in range(KT):
                        sc.activation(T[:, k, :], X[:, k, :], ACT.Square).then_inc(e[w + "sq"].next(k), 1)
                    act.wait_ge(e[w + "ms"].sem, 1)
                    sc.activation(T[:, 8, :], bank[3][:, :], ACT.Sqrt, bias=eps, scale=1.0 / D_MODEL).then_inc(e[w + "rt"].next("rt"), 1)

                if l == 0:
                    act.wait_ge(setup_dve.sem, setup_dve["x7"])
                else:
                    act.wait_ge(ev[l - 1]["x2"].sem, 1)
                with act.Fori(0, CHUNKS_ADA // RING) as i:
                    for s in range(RING):
                        b = (U + s) % 2
                        act.wait_ge(s_tile[b], i * (RING // 2) + ((U + s) // 2 + 1))
                        sc.activation(T[0:2, bass.ds(i * (RING // 2) + (T_MODROW + s // 2), 1), 256 * (s % 2):256 * (s % 2) + 256].rearrange("p a b -> p (a b)"),
                                      bank[b][0:2, 0:256], ACT.Copy).then_inc(s_taken[b], 1)
                U += TILES_ADA
                squares("n1")
                act.wait_ge(e["n1h"].sem, e["n1h"][KT - 1])
                act.wait_ge(s_rpb_out, 16 * DEPTH)
                with act.Fori(0, 2) as i:
                    for j in range(12):
                        cols = lat if j < 4 else full
                        act.wait_ge(s_tile[j % 2], i * 6 + ((U + j) // 2 + 1))
                        taken(j, sc.activation(T[:, bass.ds(i * 12 + j, 1), cols].rearrange("p a b -> p (a b)"), bank[j % 2][:, cols], ACT.Copy))
                U += 24
                act.wait_ge(s_small, 16 * (3 * DEPTH + 2))
                sc.activation(ea[:], alog[l][:], ACT.Exp).then_inc(e["aba"].next("ea"), 1)
                act.wait_ge(e["abd"].sem, e["abd"]["x"])
                sc.activation(tmp_g[:, 1], tmp_g[:, 1], ACT.Exp).then_inc(e["aba"].next("e"), 1)
                act.wait_ge(e["aba"].sem, e["aba"]["e"])
                sc.activation(tmp_g[:, 1], tmp_g[:, 1], ACT.Ln, bias=1.0).then_inc(e["aba"].next("ln"), 1)
                sc.activation(beta[:], ab[:, :, 1, :], ACT.Sigmoid).then_inc(e["aba"].next("sig"), 1)

                def square(n_, src, cols):
                    if n_ >= 2:
                        act.wait_ge(e["st"].sem, e["st"][n_ - 2])
                    sc.activation(T[:, T_SQ + n_ % 2, cols], src, ACT.Square).then_inc(e["sq"].next(n_), 1)

                def root(n_, cols, n):
                    act.wait_ge(e["st"].sem, e["st"][n_])
                    if n_ >= 2:
                        act.wait_ge(e["nrm"].sem, e["nrm"][n_ - 2])
                    sc.activation(T[:, T_RT + n_ % 2, cols], bank[4 + n_ % 2][:, cols], ACT.Sqrt, bias=eps, scale=1.0 / n)\
                        .then_inc(e["rt"].next(n_), 1)

                for j in range(16):
                    u = U + j
                    dst = T_U + j if j < 12 else T_Z + j - 12
                    if j == 8:
                        for i in range(12):
                            cols = lat if i < 4 else full
                            act.wait_ge(e["conv"].sem, e["conv"][i])
                            sc.activation(T[:, T_DQ + i, cols], T[:, T_DQ + i, cols], ACT.Silu).then_inc(e["silu"].next(i), 1)
                    cols = lat if j % 8 < 4 else full
                    if j >= 8:
                        act.wait_ge(e["silu"].sem, e["silu"][11])
                    square(j, T[:, (T_NQ + j) if j < 8 else (T_DQ + j - 8), cols], cols)
                    act.wait_ge(s_tile[u % 2], u // 2 + 1)
                    sc.activation(T[:, dst, lat], bank[u % 2][:, lat], ACT.Copy).then_inc(s_taken[u % 2], 1)
                    root(j, cols, NA_D if j < 8 else 1)
                U += 16
                act.wait_ge(s_taken[1], U // 2 + 1)
                act.wait_ge(s_taken[0], U // 2 + 1)
                for i in range(4):
                    last = sc.activation(T[:, T_Z + i, lat], T[:, T_Z + i, lat], ACT.Silu)
                last.then_inc(e["silu"].next("z"), 1)
                for n_ in range(12):
                    what, tt = divmod(n_, 4)
                    if n_ == 0:
                        act.wait_ge(e["sc"].sem, 1)
                        act.wait_ge(e["biasm"].sem, 6)
                    act.wait_ge(e["tp"].sem, e["tp"][n_])
                    dst = (T_VTOK, T_KTOK_DN, T_VTOK_DN)[what] + tt
                    sc.activation(T[:, dst, :], bank[6 + n_ % 2][:, :], ACT.Copy).then_inc(e["tpc"].next(n_), 1)

                items = names_na(l)
                N = len(items)
                for n_ in range(N + 1):
                    if n_ < N:
                        qt, h = items[n_]
                        keys = CTX_LEN if qt < 2 else TOK
                        act.wait_ge(e["aM"].sem, e["aM"][n_])
                        if n_ >= 2:
                            act.wait_ge(e["aT"].sem, e["aT"][n_ - 2])
                            act.wait_ge(e["aP"].sem, e["aP"][n_ - 2])
                        sc.activation(T[:, T_E + n_ % 2, 0:keys], bank[2 + n_ % 2][:, 0:keys], ACT.Exp, bias=mx[:, n_ % 2, 1:2],
                                      scale=NA_SCALE, accum_out=mx[:, n_ % 2, 2:3]).then_inc(e["aE"].next(n_), 1)
                    if n_ >= 1:
                        m_ = n_ - 1
                        qt, h = items[m_]
                        keys = CTX_LEN if qt < 2 else TOK
                        act.wait_ge(e["aT"].sem, e["aT"][m_])
                        if m_ >= 2:
                            act.wait_ge(e["aO"].sem, e["aO"][m_ - 2])
                        sc.activation(T[:, T_PT + m_ % 2, 0:keys], bank[4 + m_ % 2][:, 0:keys], ACT.Copy).then_inc(e["aC"].next(m_), 1)

                for j, d, tt in CH:
                    dd, da, dp, dg = e["dd"][d], e["da"][d], e["dp"][d], e["dg"][d]
                    wt = [T[:, T_WORK[d][i], :] for i in range(8)]
                    act.wait_ge(dd.sem, dd[(j, "M")])
                    if j:
                        act.wait_ge(dp.sem, dp[(j - 1, "dS")])
                    sc.activation(wt[1], bank[2 + 3 * d][:, :], ACT.Exp).then_inc(da.next((j, "eg")), 1)
                    sc.activation(wt[0], wt[0], ACT.Exp).then_inc(da.next((j, "DT")), 1)
                act.wait_ge(e["dd"][0].sem, len(e["dd"][0].names))
                act.wait_ge(e["dd"][1].sem, len(e["dd"][1].names))
                for n_ in range(16, 20):
                    square(n_, T[:, T_OT + n_ - 16, lat], lat)
                    root(n_, lat, DN_D)
                for n_ in range(TILES_MERGE):
                    u = U + n_
                    r_, m_ = divmod(n_, 8)
                    act.wait_ge(s_tile[u % 2], u // 2 + 1)
                    if r_:
                        act.wait_ge(e["mgd"].sem, e["mgd"][4 * (r_ - 1) + m_ % 4])
                    if m_ < 4:
                        sc.activation(T[:, T_BR + m_, lat], bank[u % 2][:, lat], ACT.Copy).then_inc(s_taken[u % 2], 1)
                    else:
                        sc.activation(T[:, T_SG + m_ - 4, lat], bank[u % 2][:, lat], ACT.Sigmoid).then_inc(s_taken[u % 2], 1)
                U += TILES_MERGE + TILES_OUT
                act.wait_ge(s_taken[0], U // 2 + 1)
                act.wait_ge(s_taken[1], U // 2 + 1)
                squares("n2")
                act.wait_ge(e["rp"].sem, e["rp"]["logits"])
                sc.activation(rs[:, 0, t0 // P:, :], bank[4][:, 0:64].rearrange("p (t n) -> p t n", t=4)[:, t0 // P:, :], ACT.Sigmoid)\
                    .then_inc(e["ra"].next("sig"), 1)
                for n_ in range(t0 // 64, 2 * NTT):
                    act.wait_ge(e["hr"].sem, n_ + 1 - t0 // 64)
                    sc.activation(T[:, T_HROW + n_, :], bank[6 + n_ % 2][:, :], ACT.Copy).then_inc(e["hrc"].sem, 1)
                act.wait_ge(e["xt"], 1)
                sc.activation(T[:, T_XT, :], bank[2][:, :], ACT.Copy).then_inc(e["xca"], 1)

                def expert(p_, i, tail):
                    act.wait_ge(s_tile[0], p_ * 4 + (2 * i + U // 2 + 1))
                    sc.activation(T[:, T_MSG + i, :], bank[0][:, :], ACT.Silu).then_inc(s_taken[0], 1)
                    if not tail:
                        act.wait_ge(e["xt"], p_ * 4 + (2 * i + 3))
                        sc.activation(T[:, T_XT + 2 * (1 - i), :], bank[2][:, :], ACT.Copy).then_inc(e["xca"], 1)
                    act.wait_ge(e["ht"], p_ * 2 + (i + 1))
                    sc.activation(T[:, T_HT + i, :], bank[4 + i][:, :], ACT.Copy).then_inc(e["hc"], 1)
                    act.wait_ge(s_tile[1], p_ * 4 + (2 * i + U // 2 + 2))
                    act.wait_ge(e["yst"][i], p_ * 16 + 16)
                    sc.activation(T[:, T_Y + 2 * i + 1, :], bank[1][:, :], ACT.Copy).then_inc(s_taken[1], 1)

                with act.Fori(0, N_EXPERTS // 2 - 1) as p_:
                    expert(p_, 0, False)
                    expert(p_, 1, False)
                expert(N_EXPERTS // 2 - 1, 0, False)
                expert(N_EXPERTS // 2 - 1, 1, True)
                act.wait_ge(e["rd"].sem, e["rd"]["flag"])
                with act.If(act.value_load(flag[0:1, 0:1], min_val=0, max_val=1) > 0):
                    with act.Fori(0, N_EXPERTS) as x_:
                        for f in range(4):
                            j = (0, 1, 4, 5)[f]
                            act.wait_ge(e["f_tile"][j % 2], x_ * 8 + (j // 2 + 1))
                            act.wait_ge(e["f_hid"], x_ * 4 + (f + 1))
                            sc.activation(T[:, F_MSG + f, lat], bank[j % 2][:, lat], ACT.Silu).then_inc(e["f_taken"][j % 2], 1)

            act.wait_ge(s_store, 1)
            act.dma_start(out[0].rearrange("(t p) d -> p t d", p=P), T[:, 0:4, :].rearrange("p (t a) b -> p t (a b)", t=2)).then_inc(s_out, 16)
            act.wait_ge(s_out, 16)

        @block.vector
        def _(dve):
            ve = nc.vector

            def lk(ins):
                link(dve, "dve", ins)

            ve.memset(zero_row[:], 0.0)
            ve.memset(rpb[:], 0.0).then_inc(setup_dve.next("rpbzero"), 1)
            dve.wait_ge(s_rpb, 16 * DEPTH)
            ve.tensor_scalar(rpb[:], rpb[:], 1.0 / NA_SCALE, None, ALU.mult).then_inc(setup_dve.next("rpb"), 1)
            for k in range(KT):
                dve.wait_ge(setup_pe.sem, setup_pe[f"x{k}"])
                ve.tensor_copy(X[:, k, :], bank[2 + k % 6][:, :]).then_inc(setup_dve.next(f"x{k}"), 1)
            for i in range(2 * DEPTH):
                dst = ((col_a, RA_N), (col_b, RB_N))[i % 2]
                dve.wait_ge(setup_pe.sem, setup_pe[f"rows{i}"])
                ve.tensor_copy(dst[0][i // 2][:, :], bank[i % 2][:, 0:dst[1]]).then_inc(setup_dve.next(f"rows{i}"), 1)
            for b in range(2):
                ve.memset(mx[:, b, :], 0.0).then_inc(s_taken[b], 1)

            for l in range(DEPTH):
                e = ev[l]
                t0 = e["t0"]
                U = TILES_LAYER * l
                lat, full = slice(t0, TOK), slice(0, TOK)
                segs = [(s0, v) for s0, v in ((0, 1), (CTX_LEN, 0)) if s0 >= t0]
                allsegs = [(0, 1), (CTX_LEN, 0)]
                U += TILES_ADA
                dve.wait_ge(e["modr"].sem, 1)
                lk(ve.tensor_tensor(mod[:], bank[2][:, 0:96].rearrange("p (n v) -> p n v", v=2),
                                    col_a[l][:, RA_B:RA_B + 48].unsqueeze(2).broadcast_to([P, 48, 2]), ALU.add))

                def norm(w, sc_at, sh_at, row, segs_):
                    lk(ve.scalar_tensor_tensor(out=gain[:], in0=mod[:, sc_at:sc_at + 8, :], scalar=1.0,
                                               in1=col_a[l][:, row:row + 8].unsqueeze(2).broadcast_to([P, 8, 2]), op0=ALU.add, op1=ALU.mult))
                    dve.wait_ge(e[w + "rt"].sem, 1)
                    lk(ve.reciprocal(T[:, 9, :], T[:, 8, :]))
                    for k in range(KT):
                        lk(ve.tensor_tensor(H[:, k, :], X[:, k, :], T[:, 9, :], ALU.mult))
                        for n_, (s0, v) in enumerate(segs_):
                            last = ve.tensor_scalar(H[:, k, s0:s0 + 256], H[:, k, s0:s0 + 256], gain[:, k, v:v + 1],
                                                    mod[:, sh_at + k, v:v + 1], ALU.mult, ALU.add)
                        last.then_inc(e[w + "h"].next(k), 1)

                norm("n1", 8, 0, RA_MIX, allsegs)
                for i in range(6):
                    dve.wait_ge(e["biasf"].sem, e["biasf"][i])
                    ve.tensor_tensor(T[:, T_BIAS + i, :].rearrange("p (n c) -> p n c", c=64), bank[4 + i % 4][:, :].rearrange("p (n c) -> p n c", c=64),
                                     C[:, CA["win"]].unsqueeze(1).broadcast_to([P, 8, 64]), ALU.add).then_inc(e["biasm"].next(i), 1)
                dve.wait_ge(e["ab"].sem, e["ab"]["ab"])
                ve.tensor_copy(ab[:], bank[3][:, 0:64].rearrange("p (t w n) -> p t w n", t=4, w=2)).then_inc(e["abd"].next("ab"), 1)
                dve.wait_ge(e["abd"].sem, e["abd"]["ab"])
                lk(ve.tensor_tensor(tmp_g[:, 0], ab[:, :, 0, :], dtb[l][:].unsqueeze(1).broadcast_to([P, NTT, 8]), ALU.add))
                lk(ve.tensor_scalar(tmp_g[:, 2], tmp_g[:, 0], -1.0, None, ALU.mult))
                ve.tensor_tensor(tmp_g[:, 1], tmp_g[:, 0], tmp_g[:, 2], ALU.min).then_inc(e["abd"].next("x"), 1)
                dve.wait_ge(e["aba"].sem, e["aba"]["sig"])
                lk(ve.scalar_tensor_tensor(out=tmp_g[:, 0], in0=tmp_g[:, 0], scalar=0.0, in1=tmp_g[:, 1], op0=ALU.max, op1=ALU.add))
                for d in range(2):
                    last = ve.scalar_tensor_tensor(out=gdec[:, d], in0=tmp_g[:, 0, :, 4 * d:4 * d + 4], scalar=-1.0,
                                                   in1=ea[:, 4 * d:4 * d + 4].unsqueeze(1).broadcast_to([P, NTT, 4]), op0=ALU.mult, op1=ALU.mult)
                last.then_inc(e["abd"].next("beta_g"), 1)
                dve.wait_ge(e["ab"].sem, e["ab"]["G"])
                ve.tensor_scalar(negG[:], bank[3][:, 64:96].rearrange("p (d t h) -> p d t h", d=2, t=4), -1.0, None, ALU.mult)\
                    .then_inc(e["abd"].next("negG"), 1)

                def conv(dst, src, taps, col, cols):
                    n = (TOK - cols.start) // 256
                    half = taps // 2
                    lk(ve.tensor_scalar(T[:, dst, cols], T[:, src, cols], col(half), None, ALU.mult))
                    for t_ in range(taps):
                        s_ = t_ - half
                        if s_ == 0:
                            continue
                        o_ = T[:, dst, cols].rearrange("p (s n) -> p s n", s=n)[:, :, max(0, -s_):256 - max(0, s_)]
                        i_ = T[:, src, cols].rearrange("p (s n) -> p s n", s=n)[:, :, max(0, s_):256 - max(0, -s_)]
                        last = ve.scalar_tensor_tensor(out=o_, in0=i_, scalar=col(t_), in1=o_, op0=ALU.mult, op1=ALU.add)
                        if t_ < taps - 1:
                            lk(last)
                    return last

                def normed(n_, i_, cols, g, rope):
                    dve.wait_ge(e["rt"].sem, e["rt"][n_])
                    rt_ = T[:, T_RT + n_ % 2, cols]
                    lk(ve.reciprocal(rt_, rt_))
                    if rope:
                        dve.wait_ge(e["rot"].sem, e["rot"][n_ - 8])
                        dve.wait_ge(e["silu"].sem, e["silu"][11])
                        t_ = T[:, i_, 256:512]
                        rb_ = bank[6 + n_ % 2][:, 0:256]
                        ve.tensor_tensor(rb_, rb_, cm("sin"), ALU.mult)
                        lk(ve.tensor_tensor(t_, t_, cm("cos"), ALU.mult))
                        lk(ve.tensor_tensor(t_, t_, rb_, ALU.add))
                    ve.scalar_tensor_tensor(out=T[:, i_, cols], in0=T[:, i_, cols], scalar=g, in1=rt_, op0=ALU.mult, op1=ALU.mult)\
                        .then_inc(e["nrm"].next(n_), 1)

                def conv_dn(i):
                    cols = lat if i < 4 else full
                    lk(conv(T_CONV, T_DQ + i, 5, lambda t_: col_b[l][:, RB_CONV + 12 * t_ + i:RB_CONV + 12 * t_ + i + 1], cols))
                    ve.tensor_copy(T[:, T_DQ + i, cols], T[:, T_CONV, cols]).then_inc(e["conv"].next(i), 1)
                    dve.wait_ge(e["conv"].sem, e["conv"][i])

                dve.wait_ge(s_taken[1], (U + 24) // 2 + 1)
                dve.wait_ge(s_taken[0], (U + 24) // 2 + 1)
                for j in range(8):
                    conv_dn(j)
                    g_ = col_b[l][:, RB_QG:RB_QG + 1] if j < 4 else col_b[l][:, RB_KG:RB_KG + 1]
                    normed(j, T_NQ + j, lat if j < 4 else full, g_, False)
                for j in range(8, 12):
                    conv_dn(j)
                for j in range(8, 16):
                    q_ = j < 12
                    if j == 13:
                        for i in range(4):
                            if i == 0:
                                dve.wait_ge(s_taken[1], (U + 36) // 2 + 1)
                                dve.wait_ge(s_taken[0], (U + 36) // 2 + 1)
                            lk(ve.tensor_tensor(T[:, T_C + i, lat], T[:, T_C + i, lat], T[:, T_U + i, lat], ALU.mult))
                            lk(conv(T_U + i, T_C + i, 3, lambda t_: col_b[l][:, RB_SC + 4 * t_ + i:RB_SC + 4 * t_ + i + 1], lat))
                            last = ve.tensor_tensor(T[:, T_U + i, lat], T[:, T_U + i, lat], T[:, T_B + i, lat], ALU.mult)
                        last.then_inc(e["sc"].next("sc"), 1)
                    normed(j, T_DQ + j - 8, lat if q_ else full, DN_D ** -0.5 if q_ else 1.0, True)
                U += TILES_IN

                items = names_na(l)
                N = len(items)
                for n_ in range(N + 2):
                    if n_ < N:
                        qt, h = items[n_]
                        keys = CTX_LEN if qt < 2 else TOK
                        b_ = bank[2 + n_ % 2]
                        dve.wait_ge(e["aS"].sem, e["aS"][n_])
                        if qt >= 2:
                            t_ = qt - 2
                            bv = T[:, T_BIAS:T_BIAS + 6, :].rearrange("p a b -> p (a b)").rearrange("p (h j) -> p h j", h=8)[
                                :, h, 64 * (2 - 2 * t_):64 * (6 - 2 * t_)]
                            lk(ve.tensor_tensor(b_[:, 256:512], b_[:, 256:512], bv, ALU.add))
                        lk(ve.tensor_reduce(mx[:, n_ % 2, 0:1], b_[:, 0:keys], AX_X, ALU.max))
                        ve.tensor_scalar(mx[:, n_ % 2, 1:2], mx[:, n_ % 2, 0:1], -NA_SCALE, None, ALU.mult).then_inc(e["aM"].next(n_), 1)
                    if 1 <= n_ <= N:
                        m_ = n_ - 1
                        qt, h = items[m_]
                        keys = CTX_LEN if qt < 2 else TOK
                        dve.wait_ge(e["aE"].sem, e["aE"][m_])
                        lk(ve.reciprocal(mx[:, m_ % 2, 3:4], mx[:, m_ % 2, 2:3]))
                        ve.tensor_scalar(T[:, T_E + m_ % 2, 0:keys], T[:, T_E + m_ % 2, 0:keys], mx[:, m_ % 2, 3:4], None, ALU.mult)\
                            .then_inc(e["aP"].next(m_), 1)
                    if n_ >= 2 and n_ % 2 == 1:
                        m_ = n_ - 2
                        qt, h = items[m_]
                        dve.wait_ge(e["aO"].sem, e["aO"][m_])
                        ve.tensor_copy(T[:, T_NQ + h // 2, P * qt:P * qt + P], bank[6 + m_ // 2 % 2][:, 0:P]).then_inc(e["aD"].next(m_ // 2), 1)

                dve.wait_ge(e["tpc"].sem, e["tpc"][11])
                dve.wait_ge(e["aO"].sem, N)
                ident4 = cm4("ident")
                for j in range(4):
                    grp = [g for g in CH if g[0] == j]

                    def both(f):
                        for g in grp:
                            f(*g)

                    def ctx_of(d):
                        wt = [v4(T[:, T_WORK[d][i], :]) for i in range(8)]
                        return e["dp"][d], e["dd"][d], e["da"][d], e["dg"][d], wt, [v4(bank[2 + 3 * d + i][:, :]) for i in range(3)]

                    def M(j, d, tt):
                        dp, dd, da, dg, wt, bk = ctx_of(d)
                        dve.wait_ge(dp.sem, dp[(j, "gB")])
                        for h in range(4):
                            last = ve.scalar_tensor_tensor(out=wt[0][:, h], in0=bk[0][:, h], scalar=negG[:, d, tt, h:h + 1],
                                                           in1=cm(f"neg{d}"), op0=ALU.add, op1=ALU.add)
                        last.then_inc(dd.next((j, "M")), 1)

                    def LT(j, d, tt):
                        dp, dd, da, dg, wt, bk = ctx_of(d)
                        dve.wait_ge(dp.sem, dp[(j, "KK")])
                        dve.wait_ge(da.sem, da[(j, "DT")])
                        for h in range(4):
                            last = ve.scalar_tensor_tensor(out=wt[2][:, h], in0=bk[1][:, h], scalar=beta[:, tt, 4 * d + h:4 * d + h + 1],
                                                           in1=wt[0][:, h], op0=ALU.mult, op1=ALU.mult)
                        last.then_inc(dd.next((j, "LT")), 1)
                        dve.wait_ge(dd.sem, dd[(j, "LT")])
                        lk(ve.tensor_tensor(wt[4], wt[2], cm4(f"lev0{1 - d}"), ALU.mult))
                        ve.tensor_tensor(wt[4], ident4, wt[4], ALU.subtract).then_inc(dd.next((j, "XT0")), 1)

                    def X0(j, d, tt):
                        dp, dd, da, dg, wt, bk = ctx_of(d)
                        dve.wait_ge(dp.sem, dp[(j, "L")])
                        lk(ve.tensor_tensor(wt[3], bk[1], cm4(f"lev0{d}"), ALU.mult))
                        ve.tensor_tensor(wt[3], ident4, wt[3], ALU.subtract).then_inc(dd.next((j, "X0")), 1)
                        if need_o(l, tt):
                            dve.wait_ge(dg.sem, dg[(j, "kgl")])
                            dve.wait_ge(dp.sem, dp[(j, "QK")])
                            ve.tensor_tensor(wt[0], bk[2], wt[0], ALU.mult).then_inc(dd.next((j, "AT")), 1)

                    def Yk(k):
                        def f(j, d, tt):
                            dp, dd, da, dg, wt, bk = ctx_of(d)
                            dve.wait_ge(dp.sem, dp[(j, f"Y{k}")])
                            ve.tensor_tensor(wt[5], bk[0], cm4(f"lev{k}{d}"), ALU.mult).then_inc(dd.next((j, f"Y{k}")), 1)
                        return f

                    def Zk(k):
                        def f(j, d, tt):
                            dp, dd, da, dg, wt, bk = ctx_of(d)
                            dve.wait_ge(dp.sem, dp[(j, f"ZT{k}")])
                            if k < LEVELS - 1:
                                ve.tensor_tensor(wt[3], wt[3], bk[1], ALU.subtract).then_inc(dd.next((j, f"X{k}")), 1)
                            ve.tensor_tensor(wt[4], wt[4], bk[2], ALU.subtract).then_inc(dd.next((j, f"XT{k}")), 1)
                        return f

                    def R(j, d, tt):
                        if not j:
                            return
                        dp, dd, da, dg, wt, bk = ctx_of(d)
                        dve.wait_ge(dp.sem, dp[(j, "KS")])
                        ve.tensor_tensor(wt[5], v4(T[:, T_VTOK_DN + tt, :]), bk[1], ALU.subtract).then_inc(dd.next((j, "R")), 1)

                    def vn(j, d, tt):
                        dp, dd, da, dg, wt, bk = ctx_of(d)
                        dve.wait_ge(dp.sem, dp[(j, "VN")])
                        ve.tensor_tensor(wt[3], bk[0], beta[:, tt, 4 * d:4 * d + 4].unsqueeze(2).broadcast_to([P, 4, P]), ALU.mult)\
                            .then_inc(dd.next((j, "vn")), 1)

                    def OS(j, d, tt):
                        dp, dd, da, dg, wt, bk = ctx_of(d)
                        if need_o(l, tt):
                            dve.wait_ge(dp.sem, dp[(j, "O")])
                            o_ = T[:, T_OT:T_OT + 4, P * tt:P * tt + P]
                            if j % 2 == 0:
                                ve.tensor_copy(o_, bk[2]).then_inc(dd.next((j, "O")), 1)
                            else:
                                pj = [g for g in CH if g[1] == 1 - d and g[2] == tt][0][0]
                                dve.wait_ge(e["dd"][1 - d].sem, e["dd"][1 - d][(pj, "O")])
                                ve.tensor_tensor(o_, o_, bk[2], ALU.add).then_inc(dd.next((j, "O")), 1)
                        if j < 3:
                            S = T[:, T_STATE + d, :]
                            dve.wait_ge(dp.sem, dp[(j, "dS")])
                            if j == 0:
                                ve.tensor_copy(v4(S), bk[1]).then_inc(dd.next((j, "S")), 1)
                            else:
                                dve.wait_ge(dg.sem, dg[(j, "gl")])
                                for h in range(4):
                                    last = ve.scalar_tensor_tensor(out=v4(S)[:, h], in0=v4(S)[:, h], scalar=glast[:, d, h:h + 1],
                                                                   in1=bk[1][:, h], op0=ALU.mult, op1=ALU.add)
                                last.then_inc(dd.next((j, "S")), 1)

                    both(M)
                    both(LT)
                    both(X0)
                    for k in range(1, LEVELS):
                        both(Yk(k))
                        both(Zk(k))
                    both(R)
                    both(vn)
                    both(OS)

                for n_ in range(16, 20):
                    i = n_ - 16
                    dve.wait_ge(e["rt"].sem, e["rt"][n_])
                    rt_ = T[:, T_RT + n_ % 2, lat]
                    lk(ve.reciprocal(rt_, rt_))
                    dve.wait_ge(e["silu"].sem, e["silu"]["z"])
                    lk(ve.scalar_tensor_tensor(out=rt_, in0=T[:, T_OT + i, lat], scalar=col_b[l][:, RB_OUT:RB_OUT + 1], in1=rt_,
                                               op0=ALU.mult, op1=ALU.mult))
                    ve.tensor_tensor(T[:, T_Z + i, lat], rt_, T[:, T_Z + i, lat], ALU.mult).then_inc(e["nrm"].next(n_), 1)

                for r_ in range(6):
                    hf, b = divmod(r_, 3)
                    for m in range(4):
                        u = U + 8 * r_ + 4 + m
                        dve.wait_ge(s_taken[u % 2], u // 2 + 2)
                        sg_, br_ = T[:, T_SG + m, lat], T[:, T_BR + m, lat]
                        mg_ = T[:, T_MERGED + 4 * hf + m, lat]
                        if b == 0:
                            ve.tensor_tensor(mg_, sg_, br_, ALU.mult).then_inc(e["mgd"].next(4 * r_ + m), 1)
                        else:
                            lk(ve.tensor_tensor(sg_, sg_, br_, ALU.mult))
                            ve.tensor_tensor(mg_, mg_, sg_, ALU.add).then_inc(e["mgd"].next(4 * r_ + m), 1)
                U += TILES_MERGE
                for m in range(KT):
                    u = U + m
                    dve.wait_ge(s_tile[u % 2], u // 2 + 1)
                    for n_, (s0, v) in enumerate(segs):
                        last = ve.scalar_tensor_tensor(out=X[:, m, s0:s0 + 256], in0=bank[u % 2][:, s0:s0 + 256], scalar=mod[:, 16 + m, v:v + 1],
                                                       in1=X[:, m, s0:s0 + 256], op0=ALU.mult, op1=ALU.add)
                        if n_ == len(segs) - 1:
                            last.then_inc(s_taken[u % 2], 1)
                U += TILES_OUT
                dve.wait_ge(s_taken[0], U // 2 + 1)
                dve.wait_ge(s_taken[1], U // 2 + 1)
                norm("n2", 32, 24, RA_FFN, allsegs)

                tr = slice(t0 // P, NTT)
                nt = NTT - t0 // P
                dve.wait_ge(e["ra"].sem, 1)
                R_ = lambda i: rs[:, i, tr, :]
                lk(ve.tensor_tensor(R_(1), R_(0), rbias[:].unsqueeze(1).broadcast_to([P, nt, 16]), ALU.add))
                g4 = lambda i: rs[:, i, tr, :].rearrange("p t (g x) -> p (t g) x", g=4)

                def rank(vals, cmp_):
                    for j in range(4):
                        for lo, hi, op in ((0, j, ALU.is_gt), (j + 1, 4, ALU.is_ge)):
                            if hi > lo:
                                last = ve.tensor_tensor(cmp_[:, :, lo:hi, j], vals[:, :, j:j + 1].broadcast_to([P, cmp_.shape[1], hi - lo]),
                                                        vals[:, :, lo:hi], op)
                        last = ve.memset(cmp_[:, :, j, j], 0.0)
                    return last
                rc = rcmp[:, tr].rearrange("p t g i j -> p (t g) i j")
                lk(rank(g4(1), rc))
                lk(ve.tensor_reduce(g4(2), rc, AX_X, ALU.add))
                lk(ve.tensor_scalar(R_(2), R_(2), 1.5, None, ALU.is_lt))
                lk(ve.tensor_tensor(R_(3), R_(2), R_(1), ALU.mult))
                gs = rs[:, 4, tr, 0:4]
                lk(ve.tensor_reduce(gs.rearrange("p t g -> p t g"), rs[:, 3, tr, :].rearrange("p t (g x) -> p t g x", g=4), AX_X, ALU.add))
                rg = rcmp[:, tr, 0]
                lk(rank(gs, rg))
                lk(ve.tensor_reduce(rs[:, 5, tr, 0:4], rg, AX_X, ALU.add))
                lk(ve.tensor_scalar(rs[:, 5, tr, 0:4], rs[:, 5, tr, 0:4], 0.5, None, ALU.is_lt))
                lk(ve.tensor_tensor(rs[:, 2, tr, :].rearrange("p t (g x) -> p t g x", g=4), rs[:, 2, tr, :].rearrange("p t (g x) -> p t g x", g=4),
                                    rs[:, 5, tr, 0:4].unsqueeze(3).broadcast_to([P, nt, 4, 4]), ALU.mult))
                lk(ve.tensor_tensor(R_(6), R_(2), R_(0), ALU.mult))
                lk(ve.tensor_reduce(rs[:, 4, tr, 4:5], R_(6), AX_X, ALU.add))
                lk(ve.reciprocal(rs[:, 4, tr, 5:6], rs[:, 4, tr, 4:5]))
                lk(ve.tensor_tensor(R_(7), R_(6), rs[:, 4, tr, 5:6].broadcast_to([P, nt, 16]), ALU.mult))
                ve.tensor_copy(pair[:, tr, :, 0], cm("tokid")[:, 0:nt].unsqueeze(2).broadcast_to([P, nt, 16]))
                ve.tensor_copy(pair[:, tr, :, 1], R_(7)).then_inc(e["rd"].next("comb"), 1)
                dve.wait_ge(e["rp"].sem, e["rp"]["cnt"])
                cnt = bank[5][:, 0:64].rearrange("p (t n) -> p t n", t=NTT)[:, tr]
                lk(ve.tensor_tensor(R_(3), cnt, R_(2), ALU.mult))
                ve.tensor_scalar(R_(3), R_(3), -1.0, None, ALU.add).then_inc(e["rd"].next("rk"), 1)
                dve.wait_ge(e["rd"].sem, e["rd"]["rk"])
                lk(ve.tensor_scalar(R_(4), R_(3), CAPACITY - 0.5, None, ALU.is_ge))
                ve.tensor_reduce(mx[:, 0, 0:1], rs[:, 4, tr, :].rearrange("p t n -> p (t n)"), AX_X, ALU.add).then_inc(e["rd"].next("ov"), 1)
                for x_ in range(N_EXPERTS):
                    if x_ >= 2:
                        dve.wait_ge(e["ohp"].sem, e["ohp"][x_ - 2])
                    oh_ = T[:, T_ONEHOT + x_ % 2, :].rearrange("p (t s) -> p t s", t=NTT)[:, tr]
                    ve.tensor_tensor(oh_, cm("iota").unsqueeze(1).broadcast_to([P, nt, P]), R_(3)[:, :, x_:x_ + 1].broadcast_to([P, nt, P]),
                                     ALU.is_equal).then_inc(e["oh"].next(x_), 1)
                dve.wait_ge(e["rp"].sem, e["rp"]["flag"])
                ve.tensor_scalar(flag[:], bank[5][:, 256:257], 1.0, None, ALU.min).then_inc(e["rd"].next("flag"), 1)
                dve.wait_ge(e["ohp"].sem, N_EXPERTS)
                slots = bank[4][:, 0:32].rearrange("p (n w) -> p n w", w=2)
                ve.tensor_copy(slot_tok[:], slots[:, :, 0])
                ve.tensor_copy(slot_comb[:], slots[:, :, 1]).then_inc(e["rd"].next("slots"), 1)
                lk(ve.tensor_tensor(R_(1), R_(3), cm("ebase").unsqueeze(1).broadcast_to([P, nt, 16]), ALU.add))
                lk(ve.scalar_tensor_tensor(out=R_(1), in0=R_(4), scalar=2.0 * ZERO_ROW, in1=R_(1), op0=ALU.mult, op1=ALU.add))
                lk(ve.scalar_tensor_tensor(out=R_(5), in0=R_(1), scalar=1.0, in1=R_(2), op0=ALU.add, op1=ALU.mult))
                lk(ve.tensor_reduce(mx[:, 0:1, :].rearrange("p a b -> p (a b)")[:, 0:nt], R_(5), AX_X, ALU.max))
                ve.tensor_scalar(tok_slot[:, 0, tr], mx[:, 0, 0:nt], -1.0, float(ZERO_ROW), ALU.add, ALU.min)
                lk(ve.scalar_tensor_tensor(out=R_(5), in0=R_(2), scalar=-8.0 * ZERO_ROW, in1=R_(1), op0=ALU.mult, op1=ALU.add))
                lk(ve.tensor_reduce(mx[:, 1, 0:nt], R_(5), AX_X, ALU.min))
                ve.tensor_scalar(tok_slot[:, 1, tr], mx[:, 1, 0:nt], 8.0 * ZERO_ROW, float(ZERO_ROW), ALU.add, ALU.min)\
                    .then_inc(e["rd"].next("back"), 1)

                dve.wait_ge(e["xt"], 2)
                ve.tensor_copy(T[:, T_XT + 1, :], bank[3][:, :]).then_inc(e["xcd"], 1)

                def expert(p_, i, tail):
                    dve.wait_ge(s_taken[0], p_ * 4 + (2 * i + U // 2 + 2))
                    dve.wait_ge(s_tile[1], p_ * 4 + (2 * i + U // 2 + 1))
                    comb = slot_comb[:, 2 * p_ + i:2 * p_ + i + 1] if isinstance(p_, int) else slot_comb[:, bass.ds(p_ * 2 + i, 1)]
                    ve.scalar_tensor_tensor(out=T[:, T_HID + i, :], in0=bank[1][:, :], scalar=comb, in1=T[:, T_MSG + i, :],
                                            op0=ALU.mult, op1=ALU.mult).then_inc(s_taken[1], 1)
                    if not tail:
                        dve.wait_ge(e["xt"], p_ * 4 + (2 * i + 4))
                        ve.tensor_copy(T[:, T_XT + 2 * (1 - i) + 1, :], bank[3][:, :]).then_inc(e["xcd"], 1)
                    dve.wait_ge(s_tile[0], p_ * 4 + (2 * i + U // 2 + 2))
                    dve.wait_ge(e["yst"][i], p_ * 16 + 16)
                    ve.tensor_copy(T[:, T_Y + 2 * i, :], bank[0][:, :]).then_inc(s_taken[0], 1)

                with dve.Fori(0, N_EXPERTS // 2 - 1) as p_:
                    expert(p_, 0, False)
                    expert(p_, 1, False)
                expert(N_EXPERTS // 2 - 1, 0, False)
                expert(N_EXPERTS // 2 - 1, 1, True)
                U += N_EXPERTS * TILES_EXP
                n_tt = NTT - t0 // P

                def both_added(n_):
                    dve.wait_ge(e["bg"][n_ % 2], 32 * (n_ // 2 + 1))
                    for hf in range(2):
                        if n_ >= 2:
                            dve.wait_ge(e["bt"].sem, 2 * (n_ - 2) + hf + 1)
                        t_ = T_GATHER + 4 * (n_ % 2) + hf
                        ve.tensor_tensor(T[:, t_, :], T[:, t_, :], T[:, t_ + 2, :], ALU.add).then_inc(e["bs"].sem, 1)

                both_added(0)
                for n_ in range(n_tt):
                    if n_ + 1 < n_tt:
                        both_added(n_ + 1)
                    tt = t0 // P + n_
                    v = 1 if tt < 2 else 0
                    for hf in range(2):
                        dve.wait_ge(e["bt"].sem, 2 * n_ + hf + 1)
                        for k in range(4):
                            m = 4 * hf + k
                            last = ve.scalar_tensor_tensor(out=X[:, m, P * tt:P * tt + P], in0=bank[6 + hf][:, P * k:P * k + P],
                                                           scalar=mod[:, 40 + m, v:v + 1], in1=X[:, m, P * tt:P * tt + P], op0=ALU.mult, op1=ALU.add)
                        last.then_inc(e["bx"].sem, 1)

                with dve.If(dve.value_load(flag[0:1, 0:1], min_val=0, max_val=1) > 0):
                    dve.wait_ge(e["bx"].sem, 2 * n_tt)
                    for b in range(2):
                        ve.memset(mx[:, b, :], 0.0).then_inc(e["f_taken"][b], 1)
                    for m in range(KT):
                        ve.memset(T[:, F_ACC + m, lat], 0.0)
                    ve.tensor_tensor(R_(6), R_(7), R_(4), ALU.mult).then_inc(e["f_hid"], 4)
                    dve.wait_ge(e["f_comb"], 1)
                    ve.tensor_copy(combT[:, lat], bank[5][0:16, lat]).then_inc(e["f_comb"], 1)
                    with dve.Fori(0, N_EXPERTS // 2) as p_:
                        for i in range(2):
                            dve.wait_ge(e["f_cb"][i], p_ * 16 + 16)
                            for f in range(4):
                                ug, uu = (0, 1, 4, 5)[f], (2, 3, 6, 7)[f]
                                dve.wait_ge(e["f_taken"][ug % 2], p_ * 16 + (8 * i + ug // 2 + 2))
                                dve.wait_ge(e["f_tile"][uu % 2], p_ * 16 + (8 * i + uu // 2 + 1))
                                ve.tensor_tensor(T[:, F_HID + f, lat], T[:, F_MSG + f, lat], bank[uu % 2][:, lat], ALU.mult).then_inc(e["f_taken"][uu % 2], 1)
                                dve.wait_ge(e["f_taken"][uu % 2], p_ * 16 + (8 * i + uu // 2 + 2))
                                ve.tensor_tensor(T[:, F_HID + f, lat], T[:, F_HID + f, lat], T[:, F_CB + i, lat], ALU.mult).then_inc(e["f_hid"], 1)
                            for m in range(KT):
                                ud = 8 + m
                                dve.wait_ge(e["f_tile"][ud % 2], p_ * 16 + (8 * i + ud // 2 + 1))
                                ve.tensor_tensor(T[:, F_ACC + m, lat], T[:, F_ACC + m, lat], bank[ud % 2][:, lat], ALU.add).then_inc(e["f_taken"][ud % 2], 1)
                    for b in range(2):
                        dve.wait_ge(e["f_taken"][b], 8 * N_EXPERTS + 1)
                    for m in range(KT):
                        for s0, v in segs:
                            ve.scalar_tensor_tensor(out=X[:, m, s0:s0 + 256], in0=T[:, F_ACC + m, s0:s0 + 256], scalar=mod[:, 40 + m, v:v + 1],
                                                    in1=X[:, m, s0:s0 + 256], op0=ALU.mult, op1=ALU.add)
                dve.wait_ge(e["bx"].sem, 2 * n_tt)
                ve.memset(mx[:, 0, 0:1], 0.0).then_inc(e["x2"].next("x2"), 1)

            dve.wait_ge(s_turned, 1)
            for i in range(4):
                last = ve.tensor_copy(T[:, i, :], bank[2 + i][:, :])
            last.then_inc(s_store, 1)


_INS = ['x', 'c', 'ctx', 'c_ctx', 'w_ada', 'b_ada', 'norm_mix_g', 'norm_ffn_g', 'w_in', 'na_q_norm_g', 'na_k_norm_g',
        'na_rpb', 'dn_conv_w', 'dn_a_log', 'dn_dt_bias', 'dn_out_norm_g', 'sc_conv_w', 'w_branch_na', 'w_branch_dn',
        'w_branch_sc', 'w_out', 'w_router', 'router_bias', 'moe_w_gate', 'moe_w_up', 'moe_w_down']


def kernel(**inputs):
    import concourse.bacc as _bacc
    from concourse.bass_utils import run_bass_kernel_spmd as _run

    nc = _bacc.Bacc("TRN2", target_bir_lowering=False, num_devices=1)
    arrays, args = {}, {}
    for name in _INS + ["const"]:
        a = constants()[1] if name == "const" else np.ascontiguousarray(inputs[name])
        arrays[f"in_{name}_dram"] = a
        args[name] = nc.dram_tensor(f"in_{name}_dram", a.shape, mybir.dt.from_np(a.dtype), kind="ExternalInput").ap()
    out = nc.dram_tensor("out_0_dram", (1, SEQ, D_MODEL), F32, kind="ExternalOutput").ap()
    build(nc, out=out, **args)
    r = _run(nc, [arrays], core_ids=[0])
    return r.results[0]["out_0_dram"]
```

```python
from contextlib import ExitStack

import numpy as np

import concourse.bass as bass
from concourse import mybir

F32 = mybir.dt.float32
F32R = mybir.dt.float32r
U32 = mybir.dt.uint32
ALU = mybir.AluOpType
ACT = mybir.ActivationFunctionType
AX_X = mybir.AxisListType.X

P = 128
D_MODEL, SEQ, CTX_LEN, DEPTH = 1024, 256, 256, 2
GRID_W = 64
NA_HEADS, NA_D, DN_HEADS, DN_D = 8, 64, 4, 128
WIN_C, WIN_R_MAX = 16, 8
N_EXPERTS, N_GROUPS, D_EXPERT = 16, 4, 512
EPS = 1e-6
NEG_INF = -1e30
TOK = CTX_LEN + SEQ
KT = D_MODEL // P
NTT = TOK // P
RING = 6
CHUNK = 2048
NT = 54
NA_SCALE = NA_D ** -0.5
DN_CHUNK = P
LEVELS = 7
COL_NA, COL_DN, COL_Z, COL_AB, COL_SC, COL_GATE = 0, 1536, 3072, 3584, 3600, 5136
T_NQ, T_NK, T_NV, T_DQ, T_DK, T_DV, T_Z, T_U, T_B, T_C = 0, 4, 8, 12, 16, 20, 24, 28, 32, 36
T_SQ, T_RT = 46, 48
T_BIAS = 40
T_VTOK = 32
T_CONV = 50
T_E = (50, 51, 8, 9)
T_PT = 52
T_KTOK_DN, T_VTOK_DN = 36, 46
T_OT = 32
T_STATE = 44
T_WORK = ((4, 5, 6, 7, 8, 9, 10, 11), (20, 21, 22, 23, 50, 51, 52, 53))
T_MERGED = 12
T_BR, T_SG = 4, 8
T_ROWS = 10
T_RCMP, T_PAIR, T_RS = 20, 21, 23
T_MODROW = 24
T_XROW, T_XT, T_MSG, T_HID, T_HT, T_Y = 0, 4, 8, 10, 12, 14
T_HROW, T_GATHER = 24, 24
T_ONEHOT = 18
T_HI_ADA, N_HI_ADA = 12, 3
T_HI_EXP, N_HI_EXP = 32, 4
T_HI_IN, N_HI_IN = 46, 2
T_H_HI, T_H_LO = 24, 32
T_HI_HALF = (20, 22, 52)
T_HM_HI, T_NA_HI, T_DN_HI, T_SC_HI = 36, (44, 45, 50, 51), (32, 33, 34, 35), (46, 47, 48, 49)
T_MG_HI = T_NA_HI + T_DN_HI
T_XT_LO, T_HT_LO = 48, 52
F_HID, F_MSG, F_ACC, F_CB, F_COMBT = 0, 8, 12, 20, 22
RA_B, RA_MIX, RA_FFN, RA_N = 0, 48, 56, 64
RB_CONV, RB_SC, RB_OUT, RB_QG, RB_KG, RB_N = 0, 60, 72, 73, 74, 75
TILES_ADA, TILES_IN, TILES_MERGE, TILES_OUT, TILES_EXP = 24, 40, 48, 8, 4
TILES_LAYER = TILES_ADA + TILES_IN + TILES_MERGE + TILES_OUT + N_EXPERTS * TILES_EXP
CHUNKS_ADA, CHUNKS_IN, CHUNKS_MERGE, CHUNKS_OUT, CHUNKS_EXP = 24, 20, 18, 4, 6
CAPACITY = P
ZERO_ROW = N_EXPERTS * CAPACITY
SPLIT_ADA, SPLIT_IN, SPLIT_MERGE, SPLIT_OUT, SPLIT_EXP = 24, 12, 36, 8, 96
SPLIT_LAYER = SPLIT_ADA + SPLIT_IN + SPLIT_MERGE + SPLIT_OUT + SPLIT_EXP
CHUNKS_LAYER = CHUNKS_ADA + CHUNKS_IN + CHUNKS_MERGE + CHUNKS_OUT + N_EXPERTS * CHUNKS_EXP


def last_tile_of(q):
    l, m = divmod(q, CHUNKS_LAYER)
    t = TILES_LAYER * l
    for chunks, tiles, of in ((CHUNKS_ADA, TILES_ADA, lambda m: m), (CHUNKS_IN, TILES_IN, lambda m: 2 * m + 1),
                              (CHUNKS_MERGE, TILES_MERGE, lambda m: 8 * (m // 3) + (3, 5, 7)[m % 3]),
                              (CHUNKS_OUT, TILES_OUT, lambda m: 2 * m + 1)):
        if m < chunks:
            return t + of(m)
        m, t = m - chunks, t + tiles
    return t + 4 * (m // 6) + (0, 0, 1, 1, 2, 3)[m % 6]


def last_tile_of_piece(v):
    r, a = divmod(v, 6)
    return (8 * r + (2 * a + 1 if a < 2 else a + 2)) if v < SPLIT_MERGE else TILES_MERGE + v - SPLIT_MERGE


def constants():
    a = np.arange(P)
    r, c = a[:, None], a[None, :]
    parts = {
        "ident": (r == c), "ones": np.ones((P, P)), "ones64": (r // 64 == c // 64),
        "tri0": (r <= c), "tri1": (r >= c),
        "neg0": np.where(r <= c, 0.0, NEG_INF), "neg1": np.where(r >= c, 0.0, NEG_INF),
    }
    for k in range(LEVELS):
        s = 1 << k
        m = (r // (2 * s) == c // (2 * s)) & (r // s % 2 == 1) & (c // s % 2 == 0)
        parts[f"lev{k}0"] = m
        parts[f"lev{k}1"] = m.T
    rot = np.zeros((P, P))
    for d in range(P):
        if d % 64 < 32:
            rot[d + 32, d] = -1.0
        else:
            rot[d - 32, d] = 1.0
    parts["rot"] = rot
    parts["flip"] = (r // 64 == c // 64) & (r % 64 == 63 - c % 64)
    n_freq = DN_D // 4
    inv = np.float32(10000.0) ** (-np.arange(n_freq, dtype=np.float32) / np.float32(n_freq))
    t = np.arange(SEQ)
    pos = np.stack([t // GRID_W, t % GRID_W], 0).astype(np.float32)
    ang = pos[a // 64][:, :] * inv[a % 32][:, None]
    parts["cos"], parts["sin"] = np.cos(ang), np.sin(ang)
    qc = a % 64
    c0 = np.clip(qc - WIN_C // 2, 0, GRID_W - WIN_C)[:, None]
    kc = np.arange(GRID_W)[None, :]
    parts["win"] = np.where((kc >= c0) & (kc < c0 + WIN_C), 0.0, NEG_INF / NA_SCALE)
    parts["iota"] = np.broadcast_to(c, (P, P))
    parts["ebase"] = np.broadcast_to(CAPACITY * np.arange(N_EXPERTS)[None, :], (P, N_EXPERTS))
    parts["tokid"] = r + P * np.arange(NTT)[None, :]
    parts["eps"] = np.full((P, 1), EPS)
    at, n = {}, 0
    for name, m in parts.items():
        at[name] = slice(n, n + m.shape[1])
        n += m.shape[1]
    return at, np.ascontiguousarray(np.concatenate([np.asarray(m, np.float32) for m in parts.values()], 1))


class Line:

    def __init__(self, sem, names, before=0):
        self.sem, self.names, self.seen = sem, names, 0
        self.value = {n: before + i + 1 for i, n in enumerate(names)}
        assert len(self.value) == len(names)

    def __getitem__(self, name):
        return self.value[name]

    def next(self, name):
        assert self.names[self.seen] == name, (self.names[self.seen], name)
        self.seen += 1
        return self.sem


def build(nc, x, c, ctx, c_ctx, w_ada, b_ada, norm_mix_g, norm_ffn_g, w_in, na_q_norm_g, na_k_norm_g, na_rpb,
          dn_conv_w, dn_a_log, dn_dt_bias, dn_out_norm_g, sc_conv_w, w_branch_na, w_branch_dn, w_branch_sc, w_out,
          w_router, router_bias, moe_w_gate, moe_w_up, moe_w_down, const, out):
    CA, _ = constants()
    NCONST = const.shape[1]
    rpb_pad = nc.dram_tensor("rpb_pad", [DEPTH, NA_HEADS * 15, P], F32).ap()
    h_rows = [nc.dram_tensor(f"h_rows{l}", [TOK if l < DEPTH - 1 else SEQ, D_MODEL], F32).ap() for l in range(DEPTH)]
    y_rows = [nc.dram_tensor(f"y_rows{l}", [ZERO_ROW + 1, D_MODEL], F32).ap() for l in range(DEPTH)]
    comb_rows = nc.dram_tensor("comb_rows", [DEPTH, N_EXPERTS, TOK], F32).ap()
    with ExitStack() as stack:
        def sb(name, shape, dt=F32):
            return stack.enter_context(nc.sbuf_tensor(name, shape, dt))

        def sem(name):
            return stack.enter_context(nc.semaphore(name))

        X = sb("X", [P, KT, TOK])
        h_at = nc.sbuf_base
        H = sb("H", [P, KT, TOK])
        H_R = nc.alloc_sbuf_tensor_at("H_R", [P, KT, TOK], F32R, offset=h_at)
        w_at = nc.sbuf_base
        W = sb("W", [P, RING, CHUNK])
        W_R = nc.alloc_sbuf_tensor_at("W_R", [P, RING, CHUNK], F32R, offset=w_at)
        t_at = nc.sbuf_base
        T = sb("T", [P, NT, TOK])
        T_R = nc.alloc_sbuf_tensor_at("T_R", [P, NT, TOK], F32R, offset=t_at)
        onehot = nc.alloc_sbuf_tensor_at("onehot", [P, 2, TOK], F32R, offset=t_at + 4 * TOK * T_ONEHOT)
        C = sb("C", [P, NCONST])
        rows_a = [T[0:RA_N, T_ROWS, P * l:P * l + P] for l in range(DEPTH)]
        rows_b = [T[0:RB_N, T_ROWS, P * (2 + l):P * (3 + l)] for l in range(DEPTH)]
        col_a = [sb(f"col_a{l}", [P, RA_N]) for l in range(DEPTH)]
        col_b = [sb(f"col_b{l}", [P, RB_N]) for l in range(DEPTH)]
        wab = [sb(f"wab{l}", [P, KT, 16]) for l in range(DEPTH)]
        alog = [sb(f"alog{l}", [P, 8]) for l in range(DEPTH)]
        dtb = [sb(f"dtb{l}", [P, 8]) for l in range(DEPTH)]
        rows_c = T[0:2 * KT, T_ROWS + 1, 256:384]
        rpb = T[0:NA_HEADS * 15, T_ROWS + 1, 0:P * DEPTH].rearrange("r (l c) -> r l c", l=DEPTH)
        wrt = sb("wrt", [P, KT, N_EXPERTS])
        rbias = sb("rbias", [P, N_EXPERTS])
        silu_c = sb("silu_c", [P, KT, 2])
        silu_r = sb("silu_r", [P, KT, 4], F32R)
        mod = sb("mod", [P, 48, 2])
        gain = sb("gain", [P, KT, 2])
        ab = sb("ab", [P, NTT, 2, 8])
        gdec = sb("gdec", [P, 2, NTT, 4])
        tmp_g = sb("tmp_g", [P, 3, NTT, 8])
        beta = sb("beta", [P, NTT, 8])
        negG = sb("negG", [P, 2, NTT, 4])
        ea = sb("ea", [P, 8])
        zero_row = sb("zero_row", [1, P])
        glast = sb("glast", [P, 2, 4])
        mx = sb("mx", [P, 4, 4])
        rs = T[:, T_RS, :].rearrange("p (i t n) -> p i t n", i=8, t=NTT)
        rcmp = T[:, T_RCMP, 0:256].rearrange("p (t g i j) -> p t g i j", t=NTT, g=N_GROUPS, i=4)
        combT = T[0:N_EXPERTS, F_COMBT, :]
        pair = T_R[:, T_PAIR, 0:256].rearrange("p (t n w) -> p t n w", t=NTT, n=N_EXPERTS)
        slot_comb = sb("slot_comb", [P, N_EXPERTS])
        slot_tok = sb("slot_tok", [P, N_EXPERTS], U32)
        tok_slot = sb("tok_slot", [P, 2, NTT], U32)
        flag = sb("flag", [P, 1], U32)

        bank = [stack.enter_context(nc.psum_tensor(f"bank{i}", [P, 512], F32)) for i in range(8)]

        def cm(name):
            return C[:, CA[name]]

        def cm4(name):
            return C[:, CA[name]].unsqueeze(1).broadcast_to([P, 4, P])

        def v4(ap):
            return ap.rearrange("p (h c) -> p h c", h=4)

        s_chunk = [sem(f"s_chunk{i}") for i in range(RING)]
        s_tile = [sem(f"s_tile{b}") for b in range(2)]
        s_taken = [sem(f"s_taken{b}") for b in range(2)]
        s_const, s_first, s_xin, s_rows, s_small, s_rpb, s_rpb_out, s_out = (sem(n) for n in (
            "s_const", "s_first", "s_xin", "s_rows", "s_small", "s_rpb", "s_rpb_out", "s_out"))
        s_turned, s_store = sem("s_turned"), sem("s_store")
        s_hi, s_lo = sem("s_hi"), sem("s_lo")
        chain = {n: sem(f"s_{n}_chain") for n in ("dve", "act", "pool")}
        links = {n: 0 for n in chain}

        def link(eng, name, ins):
            links[name] += 1
            ins.then_inc(chain[name], 1)
            eng.wait_ge(chain[name], links[name])

        def line(name, names):
            return Line(sem(name), names)

        shared = {}

        def on(name, names):
            s_, before = shared[name] if name in shared else (sem(name), 0)
            shared[name] = s_, before + len(names)
            return Line(s_, names, before)

        setup_pe = line("setup_pe", ["c"] + [f"x{i}" for i in range(8)] + [f"rows{i}" for i in range(2 * DEPTH)])
        setup_dve = line("setup_dve", ["rpbzero", "silu_r", "rpb"] + [f"x{i}" for i in range(8)] + [f"rows{i}" for i in range(2 * DEPTH)])
        setup_act = line("setup_act", ["silu_c", "silu_hi"])

        def names_na(l):
            return [(qt, h) for qt in range(2 if l == DEPTH - 1 else 0, NTT) for h in range(NA_HEADS)]

        def need_o(l, tt):
            return tt >= 2 or l < DEPTH - 1

        CH = [[(j, d, (j if d == 0 else (1, 0, 3, 2)[j])) for j in range(4) for d in range(2)] for _ in range(1)][0]

        def dn_pe_names(l):
            return {d: [n for j, dd, tt in CH if dd == d for n in (
                [(j, "gB"), (j, "KK")] + ([(j, "QK")] if need_o(l, tt) else []) + [(j, "L")]
                + [(j, f"{w}{k}") for k in range(1, LEVELS) for w in (("Y", "Z", "ZT") if k < LEVELS - 1 else ("Y", "ZT"))]
                + ([(j, "KS")] if j else []) + [(j, "VN")] + ([(j, "O")] if need_o(l, tt) else [])
                + ([(j, "dS")] if j < 3 else []))] for d in range(2)}

        def dn_dve_names(l):
            return {d: [n for j, dd, tt in CH if dd == d for n in (
                [(j, "M"), (j, "LT"), (j, "XT0"), (j, "X0")] + ([(j, "AT")] if need_o(l, tt) else [])
                + [(j, f"{w}{k}") for k in range(1, LEVELS) for w in (("Y", "X", "XT") if k < LEVELS - 1 else ("Y", "XT"))]
                + ([(j, "R")] if j else []) + [(j, "vn")] + ([(j, "O")] if need_o(l, tt) else [])
                + ([(j, "S")] if j < 3 else []))] for d in range(2)}

        ev = []
        for l in range(DEPTH):
            e = {}
            n = f"L{l}"
            t0 = 256 if l == DEPTH - 1 else 0
            e["t0"] = t0
            e["modr"] = line(n + "modrow_pe", ["mod"])
            e["mod"] = on("mod_dve", ["mod", "gain1", "gain2"])
            for w in ("n1", "n2"):
                e[w + "sq"] = on("norm_sq_act", list(range(KT)))
                e[w + "ms"] = on("norm_ms_pe", ["ms"])
                e[w + "rt"] = on("norm_rt_act", ["rt"])
                e[w + "x"] = on("norm_x_dve", list(range(KT)))
                e[w + "h"] = on("norm_h_act", list(range(KT)))
            parts = [(w, k) for w, n_ in (("h", 8), ("na", 4), ("H", 8), ("dn", 4), ("sc", 4), ("mg", 8)) for k in range(n_)]
            e["hi"], e["lo"] = on("hi_act", parts), on("lo_dve", parts)
            e["ab"] = on("ab_pe", ["ab", "G"])
            e["abd"] = on("ab_dve", ["ab", "x", "beta_g", "negG"])
            e["aba"] = on("ab_act", ["ea", "e", "ln", "sig"])
            e["sq"] = on("sq_act", list(range(20)))
            e["st"] = on("st_pe", list(range(20)))
            e["rt"] = on("rt_act", list(range(20)))
            e["nrm"] = on("nrm_dve", list(range(20)))
            e["conv"] = on("conv_dve", list(range(12)))
            e["silu"] = on("silu_act", list(range(12)) + ["z"])
            e["rot"] = on("rot_pe", list(range(8)))
            e["sc"] = line(n + "sc_dve", ["sc"])
            e["tp"] = on("tp_pe", list(range(12)))
            e["tpc"] = on("tp_act", list(range(12)))
            e["bias_ld"] = sem(n + "bias_ld")
            e["biasf"] = on("bias_pe", list(range(6)))
            e["biasm"] = line(n + "bias_dve", list(range(6)))
            nn = len(names_na(l))
            e["aS"] = on("aS_pe", list(range(nn)))
            e["aM"] = on("aM_dve", list(range(nn)))
            e["aE"] = on("aE_act", list(range(nn)))
            e["aP"] = on("aP_dve", list(range(nn)))
            e["aT"] = on("aT_pe", list(range(nn)))
            e["aC"] = on("aC_act", list(range(nn)))
            e["aO"] = line(n + "aO_pe", list(range(nn)))
            e["aD"] = line(n + "aD_dve", list(range(nn // 2)))
            pn, dn = dn_pe_names(l), dn_dve_names(l)
            e["dp"] = [line(n + f"dn_pe{d}", pn[d]) for d in range(2)]
            e["dd"] = [line(n + f"dn_dve{d}", dn[d]) for d in range(2)]
            e["da"] = [on(f"dn_act{d}", [(j, w) for j in range(4) for w in ("eg", "DT")]) for d in range(2)]
            e["dg"] = [on(f"dn_pool{d}", [(j, w) for j, dd, tt in CH if dd == d for w in ("kgl", "qg", "gl", "kg") if w != "qg" or need_o(l, tt)])
                       for d in range(2)]
            e["mgd"] = line(n + "merge_dve", list(range(TILES_MERGE // 2)))
            e["rp"] = on("router_pe", ["logits", "scores", "cnt", "flag"])
            e["hr"] = line(n + "hrow_pe", list(range(2 * NTT)))
            e["hrc"] = line(n + "hrow_act", list(range(2 * NTT)))
            e["hrd"] = sem(n + "hrow_dma")
            e["ra"] = line(n + "router_act", ["sig"])
            e["rd"] = on("router_dve", ["comb", "rk", "ov", "flag", "slots", "back"])
            e["oh"] = on("onehot_dve", list(range(N_EXPERTS)))
            e["ohp"] = line(n + "onehot_pe", list(range(N_EXPERTS)))
            e["xg"] = [sem(n + f"xg{i}") for i in range(2)]
            e["xt"] = sem(n + "xt_pe")
            e["xca"], e["xcd"] = sem(n + "xc_act"), sem(n + "xc_dve")
            e["ht"], e["hc"], e["hcd"] = sem(n + "ht_pe"), sem(n + "hc_act"), sem(n + "hc_dve")
            e["yst"] = [sem(n + f"yst{i}") for i in range(2)]
            e["bg"] = [sem(n + f"back{i}") for i in range(2)]
            e["bs"] = line(n + "back_dve", list(range(2 * NTT)))
            e["bt"] = line(n + "back_pe", list(range(2 * NTT)))
            e["bx"] = line(n + "back_x_dve", list(range(2 * NTT)))
            e["f_chunk"] = [sem(n + f"f_chunk{i}") for i in range(RING)]
            for w in ("f_tile", "f_taken", "f_cb"):
                e[w] = [sem(n + w + str(i)) for i in range(2)]
            e["f_hid"], e["f_comb"], e["f_store"] = sem(n + "f_hid"), sem(n + "f_comb"), sem(n + "f_store")
            e["x2"] = line(n + "x2_dve", ["x2"])
            ev.append(e)

        block = stack.enter_context(nc.Block())

        def chunk_wait(eng, C0, i, per, s):
            assert per % RING == 0 or isinstance(i, int)
            if isinstance(i, int):
                q = C0 + per * i + s
                eng.wait_ge(s_chunk[q % RING], 16 * (q // RING + 1))
            else:
                q = C0 + s
                eng.wait_ge(s_chunk[q % RING], i * (16 * per // RING) + 16 * (q // RING + 1))

        def hi_view(C_, k, t_hi, n_hi):
            b_ = t_hi + 4 * (C_ % n_hi)
            return T_R[:, b_:b_ + 4, :].rearrange("p a b -> p (a b)").rearrange("p (k n) -> p k n", k=k)

        def lo_view(C_, k):
            return W_R[:, C_ % RING, :].rearrange("p (k n) -> p k n", k=k)

        def flat(ap):
            return ap.rearrange("p a b -> p (a b)")

        def piece(Q, v):
            C_, half = Q + v // 2, v % 2
            k = 4 if v < SPLIT_MERGE and v % 6 < 2 else KT
            cols = slice(CHUNK // k // 2 * half, CHUNK // k // 2 * (half + 1))
            hi = flat(T_R[:, T_HI_HALF[v % 3]:T_HI_HALF[v % 3] + 2, :]).rearrange("p (k n) -> p k n", k=k)
            return w_view(C_, k)[:, :, cols], hi, lo_view(C_, k)[:, :, cols]

        def three(hi, lo, x_hi, x_lo, n):
            return [p_ for k in range(n) for p_ in ((hi(k), x_hi(k)), (lo(k), x_hi(k)), (hi(k), x_lo(k)))]

        def w_view(C_, k):
            return W[:, C_ % RING, :].rearrange("p (k n) -> p k n", k=k)

        @block.sync
        def _(sp):
            def load(C_, src, k):
                sp.dma_start(w_view(C_, k), src).then_inc(s_chunk[C_ % RING], 16)

            def room(C_):
                if C_ >= RING:
                    u = last_tile_of(C_ - RING)
                    sp.wait_ge(s_tile[u % 2], u // 2 + 1)

            for l in range(DEPTH):
                base = CHUNKS_LAYER * l
                wa = w_ada[l].rearrange("(k p) n -> p k n", p=P)
                for s in range(RING):
                    room(base + s)
                    load(base + s, wa[:, :, 256 * s:256 * (s + 1)], KT)
                with sp.Fori(1, CHUNKS_ADA // RING) as i:
                    for s in range(RING):
                        u = TILES_LAYER * l + s
                        sp.wait_ge(s_tile[u % 2], i * (RING // 2) + (u // 2 + 1 - RING // 2))
                        load(base + s, wa[:, :, bass.ds(i * (256 * RING) + 256 * s, 256)], KT)
                q = base + CHUNKS_ADA
                wi = w_in[l].rearrange("(k p) n -> p k n", p=P)
                cols = ([COL_NA + 256 * i for i in range(6)] + [COL_DN + 256 * i for i in range(6)]
                        + [COL_SC + 256 * i for i in range(6)] + [COL_Z + 256 * i for i in range(2)])
                for c0 in cols:
                    room(q)
                    load(q, wi[:, :, c0:c0 + 256], KT)
                    q += 1
                for hf in range(2):
                    for b, wb in enumerate((w_branch_na, w_branch_dn, w_branch_sc)):
                        room(q)
                        load(q, wb[l].rearrange("(k p) n -> p k n", p=P)[:, :, 512 * hf:512 * (hf + 1)], 4)
                        q += 1
                        for i in range(2):
                            c0 = COL_GATE + D_MODEL * b + 512 * hf + 256 * i
                            room(q)
                            load(q, wi[:, :, c0:c0 + 256], KT)
                            q += 1
                for i in range(4):
                    room(q)
                    load(q, w_out[l].rearrange("(k p) n -> p k n", p=P)[:, :, 256 * i:256 * (i + 1)], KT)
                    q += 1

                def expert(e, s, q):
                    wg, wu, wd = (m[l, bass.ds(e, 1)] if not isinstance(e, int) else m[l, e:e + 1]
                                  for m in (moe_w_gate, moe_w_up, moe_w_down))
                    if s < 4:
                        src = (wg, wu)[s // 2].rearrange("e (k p) n -> p (e k) n", p=P)[:, 4 * (s % 2):4 * (s % 2) + 4, :]
                    else:
                        src = wd.rearrange("e (k p) n -> p (e k) n", p=P)[:, :, 512 * (s - 4):512 * (s - 3)]
                    load(q, src, 4)

                for s in range(6):
                    room(q + s)
                    expert(0, s, q + s)
                with sp.Fori(1, N_EXPERTS) as e:
                    for s in range(6):
                        u = last_tile_of(q + s)
                        sp.wait_ge(s_tile[u % 2], e * 2 + (u // 2 - 1))
                        expert(e, s, q + s)

                E = ev[l]
                sp.wait_ge(E["rd"].sem, E["rd"]["flag"])
                with sp.If(sp.value_load(flag[0:1, 0:1], min_val=0, max_val=1) > 0):
                    for s in range(6):
                        u = last_tile_of(q + 6 * (N_EXPERTS - 1) + s)
                        sp.wait_ge(s_tile[u % 2], u // 2 + 1)

                    def f_load(x_, s):
                        wg, wu, wd = (m[l, bass.ds(x_, 1)] if not isinstance(x_, int) else m[l, x_:x_ + 1]
                                      for m in (moe_w_gate, moe_w_up, moe_w_down))
                        if s < 4:
                            src = (wg, wu)[s % 2].rearrange("e (k p) n -> p (e k) n", p=P)[:, :, 256 * (s // 2):256 * (s // 2 + 1)]
                        else:
                            src = wd.rearrange("e (k p) n -> p (e k) n", p=P)[:, :, 512 * (s - 4):512 * (s - 3)]
                        sp.dma_start(w_view(s, KT if s < 4 else 4), src).then_inc(E["f_chunk"][s], 16)
                    for s in range(6):
                        f_load(0, s)
                    with sp.Fori(1, N_EXPERTS) as x_:
                        for s in range(6):
                            sp.wait_ge(E["f_tile"][1], x_ * 8 + ((2, 4, 6, 8, 12, 16)[s] // 2 - 8))
                            f_load(x_, s)
                    sp.wait_ge(E["f_tile"][1], 8 * N_EXPERTS)

        @block.gpsimd
        def _(pool):
            gp = nc.gpsimd
            pool.wait_ge(setup_dve.sem, setup_dve["rpbzero"])
            for l in range(DEPTH):
                pool.dma_start(rpb[:, l, 48:79], na_rpb[l].rearrange("h r c -> (h r) c")).then_inc(s_rpb, 16)
            pool.dma_start(C[:, P:], const[:, P:]).then_inc(s_const, 16)
            for l in range(DEPTH):
                for r0, n, src in ((RA_B, 48, b_ada[l]), (RA_MIX, 8, norm_mix_g[l]), (RA_FFN, 8, norm_ffn_g[l])):
                    pool.dma_start(rows_a[l][r0:r0 + n, :], src.rearrange("(n p) -> n p", p=P)).then_inc(s_rows, 16)
                pool.dma_start(rows_b[l][RB_CONV:RB_SC, :], dn_conv_w[l].rearrange("t (n p) -> (t n) p", p=P)).then_inc(s_rows, 16)
                pool.dma_start(rows_b[l][RB_SC:RB_OUT, :], sc_conv_w[l].rearrange("t (n p) -> (t n) p", p=P)).then_inc(s_rows, 16)
                pool.dma_start(rows_b[l][RB_OUT:RB_QG, :], dn_out_norm_g[l].rearrange("(n p) -> n p", p=P)).then_inc(s_rows, 16)
                for r, g in ((RB_QG, na_q_norm_g), (RB_KG, na_k_norm_g)):
                    for i in range(2):
                        pool.dma_start(rows_b[l][r:r + 1, 64 * i:64 * i + 64], g[l:l + 1]).then_inc(s_rows, 16)
                pool.dma_start(wab[l][:], w_in[l].rearrange("(k p) n -> p k n", p=P)[:, :, COL_AB:COL_AB + 16]).then_inc(s_small, 16)
                pool.dma_start(alog[l][:], dn_a_log[l].rearrange("(a d) h -> a (d h)", a=1).broadcast_to([P, 8])).then_inc(s_small, 16)
                pool.dma_start(dtb[l][:], dn_dt_bias[l].rearrange("(a d) h -> a (d h)", a=1).broadcast_to([P, 8])).then_inc(s_small, 16)
            pool.dma_start(wrt[:], w_router.rearrange("(k p) n -> p k n", p=P)).then_inc(s_small, 16)
            pool.dma_start(rbias[:], router_bias.rearrange("(a n) -> a n", a=1).broadcast_to([P, N_EXPERTS])).then_inc(s_small, 16)
            pool.wait_ge(setup_dve.sem, setup_dve["rpb"])
            for l in range(DEPTH):
                pool.dma_start(rpb_pad[l], rpb[:, l, :]).then_inc(s_rpb_out, 16)
            pool.wait_ge(s_rpb_out, 16 * DEPTH)
            for l in range(DEPTH):
                e = ev[l]
                if l:
                    pool.wait_ge(ev[l - 1]["x2"].sem, 1)
                bview = T[:, T_BIAS:T_BIAS + 6, :].rearrange("p a b -> p (a b)").rearrange("p (h j c) -> p h j c", h=8, j=6)
                for qr in range(2):
                    for h in range(NA_HEADS):
                        src = bass.AP(rpb_pad.tensor, l * 120 * P + (h * 15 + 5 - qr) * P, [[1, 64], [P, 6], [1, 64]])
                        pool.dma_start(bview[64 * qr:64 * qr + 64, h], src).then_inc(e["bias_ld"], 16)
                for j, d, tt in CH:
                    dd, da, dp, dg = e["dd"][d], e["da"][d], e["dp"][d], e["dg"][d]
                    wt = [T[:, T_WORK[d][i], :] for i in range(8)]
                    DT, EG, QG, KGL = wt[0], wt[1], wt[6], wt[7]
                    last = 127 if d == 0 else 0
                    ts_ = slice(P * tt, P * tt + P)
                    if j:
                        pool.wait_ge(dp.sem, dp[(j - 1, "dS")])
                    if j == 0:
                        pool.wait_ge(e["tpc"].sem, e["tpc"][11])
                        pool.wait_ge(e["nrm"].sem, e["nrm"][15])
                        pool.wait_ge(e["aD"].sem, len(names_na(l)) // 2)
                    pool.wait_ge(da.sem, da[(j, "DT")])
                    kt = T[:, T_KTOK_DN + tt, :]
                    gp.tensor_tensor(v4(KGL), v4(kt), v4(DT)[:, :, last:last + 1].broadcast_to([P, 4, P]),
                                     ALU.mult).then_inc(dg.next((j, "kgl")), 1)
                    if need_o(l, tt):
                        gp.tensor_tensor(v4(QG), T[:, T_DQ:T_DQ + 4, ts_], v4(EG), ALU.mult).then_inc(dg.next((j, "qg")), 1)
                    if j:
                        pool.wait_ge(dd.sem, dd[(j - 1, "S")])
                    gp.tensor_copy(glast[:, d, :], v4(EG)[:, :, last]).then_inc(dg.next((j, "gl")), 1)
                    pool.wait_ge(dg.sem, dg[(j, "gl")])
                    gp.tensor_tensor(v4(EG), T[:, T_DK:T_DK + 4, ts_], v4(EG), ALU.mult).then_inc(dg.next((j, "kg")), 1)
                for tt in range(e["t0"] // P, NTT):
                    pool.wait_ge(e["hrc"].sem, 2 * tt + 2 - e["t0"] // 64)
                    pool.dma_start(h_rows[l][P * tt - e["t0"]:P * tt - e["t0"] + P, :], T[:, T_HROW + 2 * tt:T_HROW + 2 * tt + 2, :].rearrange("p a b -> p (a b)"))\
                        .then_inc(e["hrd"], 16)
                for i in range(2):
                    pool.dma_start(y_rows[l][ZERO_ROW:ZERO_ROW + 1, 512 * i:512 * i + 512].rearrange("a (r n) -> a r n", n=P),
                                   zero_row[:].unsqueeze(1).broadcast_to([1, 4, P])).then_inc(e["yst"][i], 16)
                pool.wait_ge(e["hrd"], 16 * (NTT - e["t0"] // P))
                pool.wait_ge(e["rd"].sem, e["rd"]["slots"])
                UE = TILES_LAYER * (l + 1) - N_EXPERTS * TILES_EXP

                def gather_x(x_):
                    pool.indirect_dma_start(T[:, T_XROW + 2 * (x_ % 2):T_XROW + 2 * (x_ % 2) + 2, :].rearrange("p a b -> p (a b)"), None,
                                            h_rows[l], bass.IndirectOffsetOnAxis(ap=slot_tok[:, x_:x_ + 1], axis=0)).then_inc(e["xg"][x_ % 2], 16)
                gather_x(0)
                gather_x(1)
                for x_ in range(N_EXPERTS):
                    if x_ + 2 < N_EXPERTS:
                        pool.wait_ge(e["xt"], 2 * (x_ + 1))
                        gather_x(x_ + 2)
                    u = UE + TILES_EXP * x_ + 2
                    pool.wait_ge(s_taken[0], u // 2 + 2)
                    pool.wait_ge(s_taken[1], u // 2 + 2)
                    pool.dma_start(y_rows[l][CAPACITY * x_:CAPACITY * (x_ + 1), :],
                                   T[:, T_Y + 2 * (x_ % 2):T_Y + 2 * (x_ % 2) + 2, :].rearrange("p a b -> p (a b)")).then_inc(e["yst"][x_ % 2], 16)
                for i in range(2):
                    pool.wait_ge(e["yst"][i], 16 * (N_EXPERTS // 2 + 1))
                for n_, tt in enumerate(range(e["t0"] // P, NTT)):
                    if n_ >= 2:
                        pool.wait_ge(e["bt"].sem, 2 * (n_ - 2) + 2)
                    for i in range(2):
                        t_ = T_GATHER + 4 * (n_ % 2) + 2 * i
                        pool.indirect_dma_start(T[:, t_:t_ + 2, :].rearrange("p a b -> p (a b)"), None, y_rows[l],
                                                bass.IndirectOffsetOnAxis(ap=tok_slot[:, i, tt:tt + 1], axis=0)).then_inc(e["bg"][n_ % 2], 16)

                pool.wait_ge(e["rd"].sem, e["rd"]["flag"])
                with pool.If(pool.value_load(flag[0:1, 0:1], min_val=0, max_val=1) > 0):
                    pool.wait_ge(e["f_comb"], 2)
                    pool.dma_start(comb_rows[l, :, e["t0"]:], combT[:, e["t0"]:]).then_inc(e["f_store"], 16)
                    pool.wait_ge(e["f_store"], 16)

                    def spread(x_, i):
                        src = comb_rows[l, bass.ds(x_, 1)] if not isinstance(x_, int) else comb_rows[l, x_:x_ + 1]
                        pool.dma_start(T[:, F_CB + i, e["t0"]:], src[:, e["t0"]:].broadcast_to([P, TOK - e["t0"]])).then_inc(e["f_cb"][i], 16)
                    for i in range(2):
                        spread(i, i)
                    with pool.Fori(1, N_EXPERTS // 2) as p_:
                        for i in range(2):
                            pool.wait_ge(e["f_hid"], p_ * 8 + 4 * i)
                            spread(p_ * 2 + i, i)

        @block.tensor
        def _(pe):
            mm = nc.tensor.matmul

            def tp(out_, in_):
                k = in_.shape[0]
                return nc.tensor.transpose(out_, in_, C[0:k, CA["ident"]][:, 0:k])

            def tile(U0, per, i, j, pairs):
                u = U0 + j
                b = u % 2
                if isinstance(i, int):
                    pe.wait_ge(s_taken[b], (u + per * i) // 2 + 1)
                else:
                    pe.wait_ge(s_taken[b], i * (per // 2) + (u // 2 + 1))
                n = len(pairs)
                for k, (a_, r_) in enumerate(pairs):
                    w_ = r_.shape[1]
                    last = mm(bank[b][:, TOK - w_:TOK], a_, r_, start=(k == 0), stop=(k == n - 1))
                last.then_inc(s_tile[b], 1)

            pe.wait_ge(s_first, 16 * 3)
            tp(bank[0][:, 0:2 * KT], rows_c).then_inc(setup_pe.next("c"), 1)
            pe.wait_ge(s_xin, 16 * NTT)
            for k in range(KT):
                if k >= 6:
                    pe.wait_ge(setup_dve.sem, setup_dve[f"x{k - 6}"])
                for i in range(NTT):
                    m_ = tp(bank[2 + k % 6][:, P * i:P * i + P], T[:, 2 * i + k // 4, P * (k % 4):P * (k % 4) + P])
                m_.then_inc(setup_pe.next(f"x{k}"), 1)
            pe.wait_ge(setup_dve.sem, setup_dve["silu_r"])

            for l in range(DEPTH):
                e = ev[l]
                t0 = e["t0"]
                q = CHUNKS_LAYER * l
                U = TILES_LAYER * l
                lat, full = slice(t0, TOK), slice(0, TOK)

                if l:
                    pe.wait_ge(ev[l - 1]["x2"].sem, 1)
                K = SPLIT_LAYER * l
                with pe.Fori(0, CHUNKS_ADA // RING) as i:
                    for s in range(RING):
                        pe.wait_ge(s_lo, i * RING + (K + s + 1))
                        b = (U + s) % 2
                        pe.wait_ge(s_taken[b], i * (RING // 2) + ((U + s) // 2 + 1))
                        for k in range(KT):
                            mm(bank[b][0:4, 0:256], silu_r[:, k, :], hi_view(q + s, KT, T_HI_ADA, N_HI_ADA)[:, k, :], start=(k == 0), stop=False)
                            last = mm(bank[b][0:4, 0:256], silu_r[:, k, :], lo_view(q + s, KT)[:, k, :], start=False, stop=(k == KT - 1))
                        last.then_inc(s_tile[b], 1)
                K += SPLIT_ADA
                q += CHUNKS_ADA
                U += TILES_ADA
                if l == 0:
                    pe.wait_ge(s_rows, 16 * 10 * DEPTH)
                    pe.wait_ge(setup_dve.sem, setup_dve["x7"])
                    for i in range(2 * DEPTH):
                        rows_, n = ((rows_a, RA_N), (rows_b, RB_N))[i % 2]
                        tp(bank[4 + i][:, 0:n], rows_[i // 2]).then_inc(setup_pe.next(f"rows{i}"), 1)
                    pe.wait_ge(s_const, 16)
                for b in range(2):
                    pe.wait_ge(s_taken[b], U // 2 + 1)
                for i in range(48):
                    last = tp(bank[2][:, 4 * i:4 * i + 4], T[0:4, T_MODROW + i // 4, P * (i % 4):P * (i % 4) + P])
                last.then_inc(e["modr"].next("mod"), 1)

                def mean_square(w, bk, cols):
                    for k in range(KT):
                        pe.wait_ge(e[w + "sq"].sem, e[w + "sq"][k])
                        last = mm(bk[:, cols], cm("ones"), T[:, k, cols], start=(k == 0), stop=(k == KT - 1))
                    last.then_inc(e[w + "ms"].next("ms"), 1)

                mean_square("n1", bank[3], full)
                pe.wait_ge(e["lo"].sem, e["lo"][("h", KT - 1)])
                with pe.Fori(0, 2) as i:
                    for s in range(6):
                        pe.wait_ge(s_lo, i * 6 + (K + s + 1))
                        cols = lat if s < 2 else full
                        hi_, lo_ = hi_view(q + s, KT, T_HI_IN, N_HI_IN), lo_view(q + s, KT)
                        for m in range(2):
                            tile(U, 12, i, 2 * s + m, three(lambda k: hi_[:, k, P * m:P * m + P], lambda k: lo_[:, k, P * m:P * m + P],
                                                            lambda k: T_R[:, T_H_HI + k, cols], lambda k: T_R[:, T_H_LO + k, cols], KT))
                q += 12
                K += SPLIT_IN
                U += 24
                pe.wait_ge(e["bias_ld"], 16 * 16)
                for i in range(6):
                    mm(bank[(4, 5, 6, 7, 2, 3)[i]][:, :], cm("flip"), T[:, T_BIAS + i, :], start=True, stop=True).then_inc(e["biasf"].next(i), 1)
                pe.wait_ge(s_small, 16 * (3 * DEPTH + 2))
                pe.wait_ge(e["biasm"].sem, e["biasm"][5])
                for tt in range(NTT):
                    for k in range(KT):
                        last = mm(bank[3][:, 16 * tt:16 * tt + 16], H[:, k, P * tt:P * tt + P], wab[l][:, k, :],
                                  start=(k == 0), stop=(k == KT - 1))
                last.then_inc(e["ab"].next("ab"), 1)

                def stat(n_, src, w_, cols):
                    pe.wait_ge(e["sq"].sem, e["sq"][n_])
                    if n_ >= 2:
                        pe.wait_ge(e["rt"].sem, e["rt"][n_ - 2])
                    mm(bank[4 + n_ % 2][:, cols], cm(w_), T[:, T_SQ + n_ % 2, cols], start=True, stop=True)\
                        .then_inc(e["st"].next(n_), 1)

                for s in range(8):
                    chunk_wait(pe, q, 0, 0, s)
                    for m in range(2):
                        j = 2 * s + m
                        tile(U, 0, 0, j, [(w_view(q + s, KT)[:, k, P * m:P * m + P], H[:, k, lat]) for k in range(KT)])
                        isq = j % 8 < 4
                        if j == 2:
                            pe.wait_ge(e["abd"].sem, e["abd"]["beta_g"])
                            for d in range(2):
                                g_ = mm(bank[3][:, 64 + 16 * d:80 + 16 * d], cm(f"tri{d}"), gdec[:, d].rearrange("p t h -> p (t h)"),
                                        start=True, stop=True)
                            g_.then_inc(e["ab"].next("G"), 1)
                        if j == 0:
                            pe.wait_ge(e["biasm"].sem, 6)
                        stat(j, None, "ones64" if j < 8 else "ones", lat if isq else full)
                        if j >= 8:
                            r_ = j - 8
                            if r_ >= 2:
                                pe.wait_ge(e["nrm"].sem, e["nrm"][j - 2])
                            mm(bank[6 + r_ % 2][:, 0:256], cm("rot"), T[:, T_DQ + r_, 256:512], start=True, stop=True)\
                                .then_inc(e["rot"].next(r_), 1)
                q += 8
                U += 16

                for n_ in range(12):
                    what, tt = divmod(n_, 4)
                    src = (T_NV, T_DK, T_DV)[what]
                    if n_ == 0:
                        pe.wait_ge(e["silu"].sem, e["silu"]["z"])
                        pe.wait_ge(e["nrm"].sem, e["nrm"][15])
                        pe.wait_ge(e["silu"].sem, e["silu"][11])
                    if n_ >= 2:
                        pe.wait_ge(e["tpc"].sem, e["tpc"][n_ - 2])
                    for i in range(4):
                        last = tp(bank[6 + n_ % 2][:, P * i:P * i + P], T[:, src + i, P * tt:P * tt + P])
                    last.then_inc(e["tp"].next(n_), 1)

                items = names_na(l)
                N = len(items)
                pe.wait_ge(e["tpc"].sem, e["tpc"][11])
                pe.wait_ge(e["abd"].sem, e["abd"]["negG"])
                for b in range(2):
                    pe.wait_ge(s_taken[b], U // 2 + 1)
                for n_ in range(N + 3):
                    if n_ < N:
                        qt, h = items[n_]
                        keys = CTX_LEN if qt < 2 else TOK
                        hp = slice(64 * (h % 2), 64 * (h % 2) + 64)
                        if n_ >= 4:
                            pe.wait_ge(e["aE"].sem, e["aE"][n_ - 4])
                        mm(bank[n_ % 4][:, 0:keys], T[hp, T_NQ + h // 2, P * qt:P * qt + P], T[hp, T_NK + h // 2, 0:keys],
                           start=True, stop=True).then_inc(e["aS"].next(n_), 1)
                    if 2 <= n_ <= N + 1:
                        m_ = n_ - 2
                        qt, h = items[m_]
                        nk = 2 if qt < 2 else 4
                        pe.wait_ge(e["aP"].sem, e["aP"][m_])
                        if m_ >= 2:
                            pe.wait_ge(e["aC"].sem, e["aC"][m_ - 2])
                        for i in range(nk):
                            last = tp(bank[4 + m_ % 2][:, P * i:P * i + P], T[:, T_E[m_ % 4], P * i:P * i + P])
                        last.then_inc(e["aT"].next(m_), 1)
                    if n_ >= 3:
                        m_ = n_ - 3
                        qt, h = items[m_]
                        nk = 2 if qt < 2 else 4
                        pe.wait_ge(e["aC"].sem, e["aC"][m_])
                        if m_ >= 4 and m_ % 2 == 0:
                            pe.wait_ge(e["aD"].sem, e["aD"][m_ // 2 - 2])
                        hp = slice(64 * (h % 2), 64 * (h % 2) + 64)
                        for i in range(nk):
                            last = mm(bank[6 + m_ // 2 % 2][hp, 0:P], T[:, T_VTOK + i, 64 * h:64 * h + 64],
                                      T[:, T_PT + m_ % 2, P * i:P * i + P], start=(i == 0), stop=(i == nk - 1))
                        last.then_inc(e["aO"].next(m_), 1)

                pe.wait_ge(e["aD"].sem, N // 2)
                pe.wait_ge(e["abd"].sem, e["abd"]["negG"])
                for j in range(4):
                    grp = [g for g in CH if g[0] == j]

                    def both(f):
                        for g in grp:
                            f(*g)

                    def ctx_of(d):
                        wt = [v4(T[:, T_WORK[d][i], :]) for i in range(8)]
                        return e["dp"][d], e["dd"][d], e["da"][d], e["dg"][d], wt, [v4(bank[2 + 3 * d + i][:, :]) for i in range(3)]

                    def gB(j, d, tt):
                        dp, dd, da, dg, wt, bk = ctx_of(d)
                        ts_ = slice(P * tt, P * tt + P)
                        if j:
                            pe.wait_ge(dd.sem, dd[(j - 1, "S")])
                        for h in range(4):
                            last = mm(bk[0][:, h], gdec[:, d, tt, h:h + 1].broadcast_to([P, P]), cm(f"tri{d}"), start=True, stop=True)
                        last.then_inc(dp.next((j, "gB")), 1)
                        for h in range(4):
                            last = mm(bk[1][:, h], T[:, T_DK + h, ts_], T[:, T_DK + h, ts_], start=True, stop=True)
                        last.then_inc(dp.next((j, "KK")), 1)
                        if need_o(l, tt):
                            for h in range(4):
                                last = mm(bk[2][:, h], T[:, T_DK + h, ts_], T[:, T_DQ + h, ts_], start=True, stop=True)
                            last.then_inc(dp.next((j, "QK")), 1)

                    def L(j, d, tt):
                        dp, dd, da, dg, wt, bk = ctx_of(d)
                        pe.wait_ge(dd.sem, dd[(j, "LT")])
                        for h in range(4):
                            last = tp(bk[1][:, h], wt[2][:, h])
                        last.then_inc(dp.next((j, "L")), 1)

                    def Y(k):
                        def f(j, d, tt):
                            dp, dd, da, dg, wt, bk = ctx_of(d)
                            pe.wait_ge(dd.sem, dd[(j, "X0" if k == 1 else f"X{k - 1}")])
                            pe.wait_ge(da.sem, da[(j, "eg")])
                            for h in range(4):
                                last = mm(bk[0][:, h], wt[2][:, h], wt[3][:, h], start=True, stop=True)
                            last.then_inc(dp.next((j, f"Y{k}")), 1)
                        return f

                    def Z(k):
                        def f(j, d, tt):
                            dp, dd, da, dg, wt, bk = ctx_of(d)
                            pe.wait_ge(dd.sem, dd[(j, f"Y{k}")])
                            if k < LEVELS - 1:
                                for h in range(4):
                                    last = mm(bk[1][:, h], wt[4][:, h], wt[5][:, h], start=True, stop=True)
                                last.then_inc(dp.next((j, f"Z{k}")), 1)
                            for h in range(4):
                                last = mm(bk[2][:, h], wt[5][:, h], wt[4][:, h], start=True, stop=True)
                            last.then_inc(dp.next((j, f"ZT{k}")), 1)
                        return f

                    def KS(j, d, tt):
                        if not j:
                            return
                        dp, dd, da, dg, wt, bk = ctx_of(d)
                        S = v4(T[:, T_STATE + d, :])
                        pe.wait_ge(dg.sem, dg[(j, "kg")])
                        for h in range(4):
                            last = mm(bk[1][:, h], wt[1][:, h], S[:, h], start=True, stop=True)
                        last.then_inc(dp.next((j, "KS")), 1)

                    def VN(j, d, tt):
                        dp, dd, da, dg, wt, bk = ctx_of(d)
                        pe.wait_ge(dd.sem, dd[(j, f"XT{LEVELS - 1}")])
                        R = v4(T[:, T_VTOK_DN + tt, :])
                        if j:
                            pe.wait_ge(dd.sem, dd[(j, "R")])
                            R = wt[5]
                        for h in range(4):
                            last = mm(bk[0][:, h], wt[4][:, h], R[:, h], start=True, stop=True)
                        last.then_inc(dp.next((j, "VN")), 1)

                    def O(j, d, tt):
                        dp, dd, da, dg, wt, bk = ctx_of(d)
                        S = v4(T[:, T_STATE + d, :])
                        pe.wait_ge(dd.sem, dd[(j, "vn")])
                        pe.wait_ge(dg.sem, dg[(j, "kg")])
                        if need_o(l, tt):
                            for h in range(4):
                                if j:
                                    mm(bk[2][:, h], S[:, h], wt[6][:, h], start=True, stop=False)
                                last = mm(bk[2][:, h], wt[3][:, h], wt[0][:, h], start=(j == 0), stop=True)
                            last.then_inc(dp.next((j, "O")), 1)
                        if j < 3:
                            for h in range(4):
                                last = mm(bk[1][:, h], wt[7][:, h], wt[3][:, h], start=True, stop=True)
                            last.then_inc(dp.next((j, "dS")), 1)

                    both(gB)
                    both(L)
                    for k in range(1, LEVELS):
                        both(Y(k))
                        both(Z(k))
                    both(KS)
                    both(VN)
                    both(O)

                pe.wait_ge(e["dd"][0].sem, len(e["dd"][0].names))
                pe.wait_ge(e["dd"][1].sem, len(e["dd"][1].names))
                for v in range(SPLIT_MERGE):
                    r_, a = divmod(v, 6)
                    b = r_ % 3
                    pe.wait_ge(s_lo, K + v + 1)
                    _, hi_, lo_ = piece(q, v)
                    if a < 2:
                        pe.wait_ge(e["lo"].sem, e["lo"][(("na", "dn", "sc")[b], 3)])
                        s_hi_, s_lo_ = (T_NA_HI, T_DN_HI, T_SC_HI)[b], (T_NQ, T_Z, T_U)[b]
                        for m in range(2):
                            tile(U, 0, 0, 8 * r_ + 2 * a + m, three(lambda k: hi_[:, k, P * m:P * m + P], lambda k: lo_[:, k, P * m:P * m + P],
                                                                    lambda k: T_R[:, s_hi_[k], lat], lambda k: T_R[:, s_lo_ + k, lat], 4))
                    else:
                        if r_ == 0:
                            stat(14 + a, None, "ones", lat)
                        pe.wait_ge(e["lo"].sem, e["lo"][("H", KT - 1)])
                        tile(U, 0, 0, 8 * r_ + 2 + a, three(lambda k: hi_[:, k, :], lambda k: lo_[:, k, :],
                                                            lambda k: T_R[:, T_HM_HI + k, lat], lambda k: H_R[:, k, lat], KT))
                pe.wait_ge(e["lo"].sem, e["lo"][("mg", KT - 1)])
                for v in range(SPLIT_MERGE, SPLIT_MERGE + SPLIT_OUT):
                    pe.wait_ge(s_lo, K + v + 1)
                    _, hi_, lo_ = piece(q, v)
                    tile(U, 0, 0, last_tile_of_piece(v), three(lambda k: hi_[:, k, :], lambda k: lo_[:, k, :],
                                                               lambda k: T_R[:, T_MG_HI[k], lat], lambda k: T_R[:, T_MERGED + k, lat], KT))
                K += SPLIT_MERGE + SPLIT_OUT
                q += CHUNKS_MERGE + CHUNKS_OUT
                U += TILES_MERGE + TILES_OUT
                mean_square("n2", bank[3], lat)
                for k in range(KT):
                    pe.wait_ge(e["n2h"].sem, e["n2h"][k])
                    last = mm(bank[4][0:16, lat], wrt[:, k, :], H[:, k, lat], start=(k == 0), stop=(k == KT - 1))
                last.then_inc(e["rp"].next("logits"), 1)
                pe.wait_ge(e["ra"].sem, e["ra"]["sig"])
                for tt in range(t0 // P, NTT):
                    last = tp(bank[4][:, 16 * tt:16 * tt + 16], T[0:16, T_ONEHOT, P * tt:P * tt + P])
                last.then_inc(e["rp"].next("scores"), 1)
                for n_ in range(t0 // 64, 2 * NTT):
                    tt, hf = divmod(n_, 2)
                    if n_ >= t0 // 64 + 2:
                        pe.wait_ge(e["hrc"].sem, e["hrc"][n_ - 2] - t0 // 64)
                    for i in range(4):
                        last = tp(bank[6 + n_ % 2][:, P * i:P * i + P], H[:, 4 * hf + i, P * tt:P * tt + P])
                    last.then_inc(e["hr"].sem, 1)
                pe.wait_ge(e["rd"].sem, e["rd"]["comb"])
                for tt in range(t0 // P, NTT):
                    for t_ in range(t0 // P, tt + 1):
                        last = mm(bank[5][:, 16 * tt:16 * tt + 16], cm("ones" if t_ < tt else "tri0"), rs[:, 2, t_, :],
                                  start=(t_ == t0 // P), stop=(t_ == tt))
                last.then_inc(e["rp"].next("cnt"), 1)
                for x_ in range(N_EXPERTS):
                    pe.wait_ge(e["oh"].sem, e["oh"][x_])
                    for tt in range(t0 // P, NTT):
                        last = mm(bank[4][:, 4 * x_:4 * x_ + 4], onehot[:, x_ % 2, P * tt:P * tt + P], pair[:, tt, x_, :],
                                  start=(tt == t0 // P), stop=(tt == NTT - 1))
                    last.then_inc(e["ohp"].next(x_), 1)
                pe.wait_ge(e["rd"].sem, e["rd"]["ov"])
                mm(bank[5][:, 256:257], cm("ones"), mx[:, 0, 0:1], start=True, stop=True).then_inc(e["rp"].next("flag"), 1)

                def rows_turned(i, x_, first):
                    if first:
                        pe.wait_ge(e["xg"][i], 16)
                        pe.wait_ge(e["hrc"].sem, 2 * NTT - t0 // 64)
                    else:
                        pe.wait_ge(e["xg"][i], (x_ - i) * 8 + 16)
                        pe.wait_ge(e["xcd"], x_)
                    for hf in range(2):
                        for k in range(4):
                            last = tp(bank[2 + hf][:, P * k:P * k + P], T[:, T_XROW + 2 * i + hf, P * k:P * k + P])
                        last.then_inc(e["xt"], 1)

                def expert(p_, i, tail):
                    xt, xt_lo = (T_R[:, t_ + 2 * i:t_ + 2 * i + 2, :].rearrange("p a (k s) -> p (a k) s", k=4) for t_ in (T_XT, T_XT_LO))
                    pe.wait_ge(e["xcd"], p_ * 2 + (i + 1))
                    for t_ in range(2):
                        pe.wait_ge(s_taken[t_], p_ * 4 + (2 * i + (U + t_) // 2 + 1))
                        for c_ in range(2):
                            C_ = q + 6 * i + 2 * t_ + c_
                            pe.wait_ge(s_lo, p_ * 12 + (K + 6 * i + 2 * t_ + c_ + 1))
                            w_hi, w_lo = hi_view(C_, 4, T_HI_EXP, N_HI_EXP), lo_view(C_, 4)
                            for k in range(4):
                                mm(bank[t_][:, :], xt[:, 4 * c_ + k, :], w_hi[:, k, :], start=(c_ + k == 0), stop=False)
                                mm(bank[t_][:, :], xt[:, 4 * c_ + k, :], w_lo[:, k, :], start=False, stop=False)
                                last = mm(bank[t_][:, :], xt_lo[:, 4 * c_ + k, :], w_hi[:, k, :], start=False, stop=(c_ + k == 4))
                        last.then_inc(s_tile[t_], 1)
                    if not tail:
                        rows_turned(1 - i, p_ * 2 + (i + 1), False)
                    pe.wait_ge(s_taken[1], p_ * 4 + (2 * i + U // 2 + 2))
                    for k in range(4):
                        last = tp(bank[4 + i][:, P * k:P * k + P], T[:, T_HID + i, P * k:P * k + P])
                    last.then_inc(e["ht"], 1)
                    pe.wait_ge(e["hcd"], p_ * 2 + (i + 1))
                    for t_ in range(2):
                        C_ = q + 6 * i + 4 + t_
                        pe.wait_ge(s_taken[t_], p_ * 4 + (2 * i + (U + 2 + t_) // 2 + 1))
                        pe.wait_ge(s_lo, p_ * 12 + (K + 6 * i + 4 + t_ + 1))
                        w_hi, w_lo = hi_view(C_, 4, T_HI_EXP, N_HI_EXP), lo_view(C_, 4)
                        for k in range(4):
                            h_hi, h_lo = T_R[:, T_HT + i, P * k:P * k + P], T_R[:, T_HT_LO + i, P * k:P * k + P]
                            mm(bank[t_][:, :], h_hi, w_hi[:, k, :], start=(k == 0), stop=False)
                            mm(bank[t_][:, :], h_hi, w_lo[:, k, :], start=False, stop=False)
                            last = mm(bank[t_][:, :], h_lo, w_hi[:, k, :], start=False, stop=(k == 3))
                        last.then_inc(s_tile[t_], 1)

                rows_turned(0, 0, True)
                pe.wait_ge(e["rd"].sem, e["rd"]["flag"])
                with pe.Fori(0, N_EXPERTS // 2 - 1) as p_:
                    expert(p_, 0, False)
                    expert(p_, 1, False)
                expert(N_EXPERTS // 2 - 1, 0, False)
                expert(N_EXPERTS // 2 - 1, 1, True)
                q += 6 * N_EXPERTS
                U += N_EXPERTS * TILES_EXP
                for n_ in range(2 * (NTT - t0 // P)):
                    pe.wait_ge(e["bs"].sem, n_ + 1)
                    if n_ >= 2:
                        pe.wait_ge(e["bx"].sem, n_ - 1)
                    for k in range(4):
                        last = tp(bank[6 + n_ % 2][:, P * k:P * k + P], T[:, T_GATHER + 4 * (n_ // 2 % 2) + n_ % 2, P * k:P * k + P])
                    last.then_inc(e["bt"].sem, 1)

                with pe.If(pe.value_load(flag[0:1, 0:1], min_val=0, max_val=1) > 0):
                    pe.wait_ge(e["f_hid"], 1)
                    for tt in range(t0 // P, NTT):
                        last = tp(bank[5][0:16, P * tt:P * tt + P], rs[:, 6, tt, :])
                    last.then_inc(e["f_comb"], 1)
                    with pe.Fori(0, N_EXPERTS) as x_:
                        for s in range(6):
                            pe.wait_ge(e["f_chunk"][s], x_ * 16 + 16)
                            if s == 4:
                                pe.wait_ge(e["f_hid"], x_ * 4 + 8)
                            for m in range(2 if s < 4 else 4):
                                j = 2 * s + m if s < 4 else 4 * s - 8 + m
                                pe.wait_ge(e["f_taken"][j % 2], x_ * 8 + (j // 2 + 1))
                                n = KT if s < 4 else 4
                                for k in range(n):
                                    last = mm(bank[j % 2][:, lat], w_view(s, n)[:, k, P * m:P * m + P], H[:, k, lat] if s < 4 else T[:, F_HID + k, lat],
                                              start=(k == 0), stop=(k == n - 1))
                                last.then_inc(e["f_tile"][j % 2], 1)

            pe.wait_ge(ev[-1]["x2"].sem, 1)
            for tt in range(2):
                for hf in range(2):
                    for i in range(4):
                        last = tp(bank[2 + 2 * tt + hf][:, P * i:P * i + P], X[:, 4 * hf + i, CTX_LEN + P * tt:CTX_LEN + P * tt + P])
            last.then_inc(s_turned, 1)

        @block.scalar
        def _(act):
            sc = nc.scalar
            eps = C[:, CA["eps"]]
            act.dma_start(C[:, 0:P], const[:, 0:P]).then_inc(s_first, 16)
            for v, src in enumerate((c[0], c_ctx)):
                act.dma_start(rows_c[8 * v:8 * v + 8, :], src.rearrange("(n p) -> n p", p=P)).then_inc(s_first, 16)
            for i in range(NTT):
                src = (ctx if i < 2 else x)[0].rearrange("(t p) d -> t p d", p=P)[i % 2]
                act.dma_start(flat(T[:, 2 * i:2 * i + 2, :]), src).then_inc(s_xin, 16)
            act.wait_ge(setup_pe.sem, setup_pe["c"])
            for v in range(2):
                last = sc.activation(silu_c[:, :, v], bank[0][:, 8 * v:8 * v + 8], ACT.Silu)
            last.then_inc(setup_act.next("silu_c"), 1)
            act.wait_ge(setup_act.sem, setup_act["silu_c"])
            sc.activation(silu_r[:, :, 0:2], silu_c[:], ACT.Copy).then_inc(setup_act.next("silu_hi"), 1)

            for l in range(DEPTH):
                e = ev[l]
                t0 = e["t0"]
                U = TILES_LAYER * l
                lat, full = slice(t0, TOK), slice(0, TOK)

                def taken(u, ins):
                    ins.then_inc(s_taken[u % 2], 1)

                def squares(w, cols, u0):
                    for k in range(KT):
                        if u0:
                            act.wait_ge(s_taken[(u0 + k) % 2], (u0 + k) // 2 + 2)
                        sc.activation(T[:, k, cols], X[:, k, cols], ACT.Square).then_inc(e[w + "sq"].next(k), 1)
                    act.wait_ge(e[w + "ms"].sem, e[w + "ms"]["ms"])
                    link(act, "act", sc.activation(T[:, 8, cols], bank[3][:, cols], ACT.Ln, bias=eps, scale=1.0 / D_MODEL))
                    sc.activation(T[:, 8, cols], T[:, 8, cols], ACT.Exp, scale=-0.5).then_inc(e[w + "rt"].next("rt"), 1)

                def modulate(w, k, sh_at, segs_):
                    act.wait_ge(e[w + "x"].sem, e[w + "x"][k])
                    for s0, v in segs_:
                        last = sc.activation(H[:, k, s0:s0 + 256], H[:, k, s0:s0 + 256], ACT.Identity, scale=gain[:, k, v:v + 1],
                                             bias=mod[:, sh_at + k, v:v + 1])
                    last.then_inc(e[w + "h"].next(k), 1)

                if l == 0:
                    act.wait_ge(setup_dve.sem, setup_dve["x7"])
                else:
                    act.wait_ge(ev[l - 1]["x2"].sem, 1)
                q = CHUNKS_LAYER * l

                def high(C_, t_hi, n_hi):
                    sc.activation(flat(hi_view(C_, 4, t_hi, n_hi)), flat(w_view(C_, 4)), ACT.Copy).then_inc(s_hi, 1)

                for s in range(RING):
                    chunk_wait(act, q, 0, 0, s)
                    if s >= N_HI_ADA:
                        act.wait_ge(s_tile[(U + s - N_HI_ADA) % 2], (U + s - N_HI_ADA) // 2 + 1)
                    high(q + s, T_HI_ADA, N_HI_ADA)
                with act.Fori(1, CHUNKS_ADA // RING) as i:
                    for s in range(RING):
                        chunk_wait(act, q, i, RING, s)
                        u = U + s - N_HI_ADA + RING
                        act.wait_ge(s_tile[u % 2], i * (RING // 2) + (u // 2 + 1 - RING // 2))
                        high(q + s, T_HI_ADA, N_HI_ADA)
                U += TILES_ADA
                q += CHUNKS_ADA

                def part_hi(w, k, dst, src):
                    sc.activation(dst, src, ACT.Copy).then_inc(e["hi"].next((w, k)), 1)

                squares("n1", full, 0)
                for k in range(KT):
                    modulate("n1", k, 0, ((0, 1), (CTX_LEN, 0)))
                    act.wait_ge(e["n1h"].sem, e["n1h"][k])
                    part_hi("h", k, T_R[:, T_H_HI + k, :], H[:, k, :])
                for s in range(N_HI_IN):
                    chunk_wait(act, q, 0, 0, s)
                    high(q + s, T_HI_IN, N_HI_IN)
                act.wait_ge(s_rpb_out, 16 * DEPTH)
                for j in range(24):
                    cols = lat if j % 12 < 4 else full
                    act.wait_ge(s_tile[j % 2], (U + j) // 2 + 1)
                    taken(j, sc.activation(T[:, j, cols], bank[j % 2][:, cols], ACT.Copy))
                    if j % 2 == 1 and j // 2 + N_HI_IN < SPLIT_IN:
                        chunk_wait(act, q, 0, 0, j // 2 + N_HI_IN)
                        high(q + j // 2 + N_HI_IN, T_HI_IN, N_HI_IN)
                U += 24
                q += CHUNKS_IN
                act.wait_ge(s_small, 16 * (3 * DEPTH + 2))
                sc.activation(ea[:], alog[l][:], ACT.Exp).then_inc(e["aba"].next("ea"), 1)
                act.wait_ge(e["abd"].sem, e["abd"]["x"])
                sc.activation(tmp_g[:, 1], tmp_g[:, 1], ACT.Exp).then_inc(e["aba"].next("e"), 1)
                act.wait_ge(e["aba"].sem, e["aba"]["e"])
                sc.activation(tmp_g[:, 1], tmp_g[:, 1], ACT.Ln, bias=1.0).then_inc(e["aba"].next("ln"), 1)
                sc.activation(beta[:], ab[:, :, 1, :], ACT.Sigmoid).then_inc(e["aba"].next("sig"), 1)

                def square(n_, src, cols):
                    if n_ >= 2:
                        act.wait_ge(e["st"].sem, e["st"][n_ - 2])
                    sc.activation(T[:, T_SQ + n_ % 2, cols], src, ACT.Square).then_inc(e["sq"].next(n_), 1)

                def root(n_, cols, n):
                    act.wait_ge(e["st"].sem, e["st"][n_])
                    if n_ >= 2:
                        act.wait_ge(e["nrm"].sem, e["nrm"][n_ - 2])
                    rt_ = T[:, T_RT + n_ % 2, cols]
                    link(act, "act", sc.activation(rt_, bank[4 + n_ % 2][:, cols], ACT.Ln, bias=eps, scale=1.0 / n))
                    sc.activation(rt_, rt_, ACT.Exp, scale=-0.5).then_inc(e["rt"].next(n_), 1)

                for j in range(16):
                    u = U + j
                    dst = T_U + j if j < 12 else T_Z + j - 12
                    if j == 8:
                        for i in range(12):
                            cols = lat if i < 4 else full
                            act.wait_ge(e["conv"].sem, e["conv"][i])
                            sc.activation(T[:, T_DQ + i, cols], T[:, T_DQ + i, cols], ACT.Silu).then_inc(e["silu"].next(i), 1)
                    cols = lat if j % 8 < 4 else full
                    if j >= 8:
                        act.wait_ge(e["silu"].sem, e["silu"][11])
                    square(j, T[:, (T_NQ + j) if j < 8 else (T_DQ + j - 8), cols], cols)
                    act.wait_ge(s_tile[u % 2], u // 2 + 1)
                    sc.activation(T[:, dst, lat], bank[u % 2][:, lat], ACT.Copy).then_inc(s_taken[u % 2], 1)
                    root(j, cols, NA_D if j < 8 else 1)
                U += 16
                act.wait_ge(s_taken[1], U // 2 + 1)
                act.wait_ge(s_taken[0], U // 2 + 1)
                for i in range(4):
                    last = sc.activation(T[:, T_Z + i, lat], T[:, T_Z + i, lat], ACT.Silu)
                last.then_inc(e["silu"].next("z"), 1)
                for n_ in range(12):
                    what, tt = divmod(n_, 4)
                    if n_ == 0:
                        act.wait_ge(e["sc"].sem, 1)
                        act.wait_ge(e["biasm"].sem, 6)
                    act.wait_ge(e["tp"].sem, e["tp"][n_])
                    dst = (T_VTOK, T_KTOK_DN, T_VTOK_DN)[what] + tt
                    sc.activation(T[:, dst, :], bank[6 + n_ % 2][:, :], ACT.Copy).then_inc(e["tpc"].next(n_), 1)

                items = names_na(l)
                N = len(items)
                for n_ in range(N + 2):
                    if n_ < N:
                        qt, h = items[n_]
                        keys = CTX_LEN if qt < 2 else TOK
                        act.wait_ge(e["aM"].sem, e["aM"][n_])
                        if n_ >= 4:
                            act.wait_ge(e["aT"].sem, e["aT"][n_ - 4])
                        sc.activation(T[:, T_E[n_ % 4], 0:keys], bank[n_ % 4][:, 0:keys], ACT.Exp, bias=mx[:, n_ % 4, 1:2],
                                      scale=NA_SCALE, accum_out=mx[:, n_ % 4, 2:3]).then_inc(e["aE"].next(n_), 1)
                    if n_ >= 2:
                        m_ = n_ - 2
                        qt, h = items[m_]
                        keys = CTX_LEN if qt < 2 else TOK
                        act.wait_ge(e["aT"].sem, e["aT"][m_])
                        if m_ >= 2:
                            act.wait_ge(e["aO"].sem, e["aO"][m_ - 2])
                        sc.activation(T[:, T_PT + m_ % 2, 0:keys], bank[4 + m_ % 2][:, 0:keys], ACT.Copy).then_inc(e["aC"].next(m_), 1)

                for j, d, tt in CH:
                    dd, da, dp, dg = e["dd"][d], e["da"][d], e["dp"][d], e["dg"][d]
                    wt = [T[:, T_WORK[d][i], :] for i in range(8)]
                    act.wait_ge(dd.sem, dd[(j, "M")])
                    if j:
                        act.wait_ge(dp.sem, dp[(j - 1, "dS")])
                    sc.activation(wt[1], bank[2 + 3 * d][:, :], ACT.Exp).then_inc(da.next((j, "eg")), 1)
                    sc.activation(wt[0], wt[0], ACT.Exp).then_inc(da.next((j, "DT")), 1)
                act.wait_ge(e["dd"][0].sem, len(e["dd"][0].names))
                act.wait_ge(e["dd"][1].sem, len(e["dd"][1].names))
                def piece_hi(v):
                    chunk_wait(act, q, 0, 0, v // 2)
                    w_, hi_, _ = piece(q, v)
                    sc.activation(hi_, w_, ACT.Copy).then_inc(s_hi, 1)

                for i in range(2):
                    square(16 + i, T[:, T_OT + i, lat], lat)
                for k in range(4):
                    part_hi("na", k, T_R[:, T_NA_HI[k], lat], T[:, T_NQ + k, lat])
                for v in range(3):
                    piece_hi(v)
                for v in range(SPLIT_MERGE):
                    r_, a = divmod(v, 6)
                    if v == 1:
                        for k in range(KT):
                            part_hi("H", k, T_R[:, T_HM_HI + k, lat], H[:, k, lat])
                    for n_ in ((8 * r_ + 2 * a, 8 * r_ + 2 * a + 1) if a < 2 else (8 * r_ + a + 2,)):
                        u, m_ = U + n_, n_ % 8
                        act.wait_ge(s_tile[u % 2], u // 2 + 1)
                        if r_:
                            act.wait_ge(e["mgd"].sem, e["mgd"][4 * (r_ - 1) + m_ % 4])
                        if m_ < 4:
                            sc.activation(T[:, T_BR + m_, lat], bank[u % 2][:, lat], ACT.Copy).then_inc(s_taken[u % 2], 1)
                        else:
                            sc.activation(T[:, T_SG + m_ - 4, lat], bank[u % 2][:, lat], ACT.Sigmoid).then_inc(s_taken[u % 2], 1)
                    piece_hi(v + 3)
                    if r_ == 0 and a >= 2:
                        root(14 + a, lat, DN_D)
                        if a < 4:
                            square(16 + a, T[:, T_OT + a, lat], lat)
                    if v == 5:
                        for k in range(4):
                            act.wait_ge(e["nrm"].sem, e["nrm"][19])
                            part_hi("dn", k, T_R[:, T_DN_HI[k], lat], T[:, T_Z + k, lat])
                        for k in range(4):
                            part_hi("sc", k, T_R[:, T_SC_HI[k], lat], T[:, T_U + k, lat])
                    if v == 29:
                        for k in range(4):
                            part_hi("mg", k, T_R[:, T_MG_HI[k], lat], T[:, T_MERGED + k, lat])
                for k in range(4, 8):
                    act.wait_ge(e["mgd"].sem, e["mgd"][16 + k])
                    part_hi("mg", k, T_R[:, T_MG_HI[k], lat], T[:, T_MERGED + k, lat])
                U += TILES_MERGE
                for m in range(TILES_OUT - 3):
                    act.wait_ge(s_tile[(U + m) % 2], (U + m) // 2 + 1)
                    piece_hi(SPLIT_MERGE + m + 3)
                U += TILES_OUT
                q += CHUNKS_MERGE + CHUNKS_OUT
                squares("n2", lat, U - TILES_OUT)
                for k in range(KT):
                    modulate("n2", k, 24, ((0, 1), (CTX_LEN, 0))[t0 // CTX_LEN:])
                act.wait_ge(e["rp"].sem, e["rp"]["logits"])
                sc.activation(T[0:16, T_ONEHOT, lat], bank[4][0:16, lat], ACT.Sigmoid).then_inc(e["ra"].next("sig"), 1)
                for n_ in range(t0 // 64, 2 * NTT):
                    act.wait_ge(e["hr"].sem, n_ + 1 - t0 // 64)
                    sc.activation(T[:, T_HROW + n_, :], bank[6 + n_ % 2][:, :], ACT.Copy).then_inc(e["hrc"].sem, 1)
                for s in range(N_HI_EXP):
                    act.wait_ge(s_chunk[(q + s) % RING], 16 * ((q + s) // RING + 1))
                    high(q + s, T_HI_EXP, N_HI_EXP)

                def rows_hi(i, n_):
                    for hf in range(2):
                        act.wait_ge(e["xt"], n_ + hf)
                        sc.activation(T_R[:, T_XT + 2 * i + hf, :], bank[2 + hf][:, :], ACT.Copy).then_inc(e["xca"], 1)

                rows_hi(0, 1)

                def chunk_hi(p_, c_):
                    C_ = q + c_
                    act.wait_ge(s_chunk[C_ % RING], p_ * 32 + 16 * (C_ // RING + 1))
                    high(C_, T_HI_EXP, N_HI_EXP)

                def expert(p_, i, tail):
                    act.wait_ge(s_tile[0], p_ * 4 + (2 * i + U // 2 + 1))
                    sc.activation(T[:, T_MSG + i, :], bank[0][:, :], ACT.Silu).then_inc(s_taken[0], 1)
                    chunk_hi(p_, 6 * i + 4)
                    chunk_hi(p_, 6 * i + 5)
                    if not tail:
                        rows_hi(1 - i, p_ * 4 + (2 * i + 3))
                    act.wait_ge(e["ht"], p_ * 2 + (i + 1))
                    sc.activation(T_R[:, T_HT + i, :], bank[4 + i][:, :], ACT.Copy).then_inc(e["hc"], 1)
                    if not tail:
                        chunk_hi(p_, 6 * i + 6)
                        chunk_hi(p_, 6 * i + 7)
                        act.wait_ge(s_tile[0], p_ * 4 + (2 * i + U // 2 + 2))
                        chunk_hi(p_, 6 * i + 8)
                    act.wait_ge(s_tile[1], p_ * 4 + (2 * i + U // 2 + 2))
                    act.wait_ge(e["yst"][i], p_ * 16 + 16)
                    sc.activation(T[:, T_Y + 2 * i + 1, :], bank[1][:, :], ACT.Copy).then_inc(s_taken[1], 1)
                    if not tail:
                        chunk_hi(p_, 6 * i + 9)

                with act.Fori(0, N_EXPERTS // 2 - 1) as p_:
                    expert(p_, 0, False)
                    expert(p_, 1, False)
                expert(N_EXPERTS // 2 - 1, 0, False)
                expert(N_EXPERTS // 2 - 1, 1, True)
                act.wait_ge(e["rd"].sem, e["rd"]["flag"])
                with act.If(act.value_load(flag[0:1, 0:1], min_val=0, max_val=1) > 0):
                    with act.Fori(0, N_EXPERTS) as x_:
                        for f in range(4):
                            j = (0, 1, 4, 5)[f]
                            act.wait_ge(e["f_tile"][j % 2], x_ * 8 + (j // 2 + 1))
                            act.wait_ge(e["f_hid"], x_ * 4 + (f + 1))
                            sc.activation(T[:, F_MSG + f, lat], bank[j % 2][:, lat], ACT.Silu).then_inc(e["f_taken"][j % 2], 1)

            act.wait_ge(s_store, 1)
            act.dma_start(out[0].rearrange("(t p) d -> p t d", p=P), T[:, 0:4, :].rearrange("p (t a) b -> p t (a b)", t=2)).then_inc(s_out, 16)
            act.wait_ge(s_out, 16)

        @block.vector
        def _(dve):
            ve = nc.vector

            def lk(ins):
                link(dve, "dve", ins)

            ve.memset(zero_row[:], 0.0)
            ve.memset(rpb[:], 0.0).then_inc(setup_dve.next("rpbzero"), 1)
            for b in range(2):
                ve.memset(mx[:, b, :], 0.0).then_inc(s_taken[b], 1)
            dve.wait_ge(setup_act.sem, setup_act["silu_hi"])
            ve.tensor_tensor(silu_r[:, :, 2:4], silu_c[:], silu_r[:, :, 0:2], ALU.subtract).then_inc(setup_dve.next("silu_r"), 1)
            dve.wait_ge(s_rpb, 16 * DEPTH)
            ve.tensor_scalar(rpb[:], rpb[:], 1.0 / NA_SCALE, None, ALU.mult).then_inc(setup_dve.next("rpb"), 1)
            for k in range(KT):
                dve.wait_ge(setup_pe.sem, setup_pe[f"x{k}"])
                ve.tensor_copy(X[:, k, :], bank[2 + k % 6][:, :]).then_inc(setup_dve.next(f"x{k}"), 1)

            for l in range(DEPTH):
                e = ev[l]
                t0 = e["t0"]
                U = TILES_LAYER * l
                lat, full = slice(t0, TOK), slice(0, TOK)
                segs = [(s0, v) for s0, v in ((0, 1), (CTX_LEN, 0)) if s0 >= t0]
                q, K = CHUNKS_LAYER * l, SPLIT_LAYER * l

                def low(C_, t_hi, n_hi):
                    w_ = flat(w_view(C_, 4))
                    ve.tensor_tensor(flat(lo_view(C_, 4)), w_, flat(hi_view(C_, 4, t_hi, n_hi)), ALU.subtract).then_inc(s_lo, 1)

                def mod_row(i, s):
                    b = (U + s) % 2
                    dve.wait_ge(s_tile[b], i * (RING // 2) + ((U + s) // 2 + 1))
                    tile_ = T[0:4, T_MODROW + i * (RING // 2) + s // 2, :] if isinstance(i, int) else \
                        flat(T[0:4, bass.ds(i * (RING // 2) + (T_MODROW + s // 2), 1), :])
                    ve.tensor_copy(tile_[:, 256 * (s % 2):256 * (s % 2) + 256], bank[b][0:4, 0:256]).then_inc(s_taken[b], 1)

                dve.wait_ge(s_hi, K + 1)
                low(q, T_HI_ADA, N_HI_ADA)
                n_ = CHUNKS_ADA // RING - 1
                with dve.Fori(0, n_) as i:
                    for s in range(RING):
                        dve.wait_ge(s_hi, i * RING + (K + s + 2))
                        low(q + s + 1, T_HI_ADA, N_HI_ADA)
                        mod_row(i, s)
                for s in range(RING):
                    if s < RING - 1:
                        dve.wait_ge(s_hi, n_ * RING + K + s + 2)
                        low(q + s + 1, T_HI_ADA, N_HI_ADA)
                    mod_row(n_, s)
                U += TILES_ADA
                K += SPLIT_ADA
                q += CHUNKS_ADA

                def part_lo(w, k, dst, src, hi):
                    dve.wait_ge(e["hi"].sem, e["hi"][(w, k)])
                    ve.tensor_tensor(dst, src, hi, ALU.subtract).then_inc(e["lo"].next((w, k)), 1)

                def piece_lo(v):
                    dve.wait_ge(s_hi, K + v + 1)
                    w_, hi_, lo_ = piece(q, v)
                    ve.tensor_tensor(lo_, w_, hi_, ALU.subtract).then_inc(s_lo, 1)

                if l == 0:
                    for i in range(2 * DEPTH):
                        dst = ((col_a, RA_N), (col_b, RB_N))[i % 2]
                        dve.wait_ge(setup_pe.sem, setup_pe[f"rows{i}"])
                        ve.tensor_copy(dst[0][i // 2][:, :], bank[4 + i][:, 0:dst[1]]).then_inc(setup_dve.next(f"rows{i}"), 1)
                    dve.wait_ge(setup_dve.sem, setup_dve[f"rows{2 * DEPTH - 1}"])
                dve.wait_ge(e["modr"].sem, 1)
                rows4 = bank[2][:, 0:192].rearrange("p (n v) -> p n v", v=4)
                lk(ve.tensor_tensor(mod[:], rows4[:, :, 0:2], col_a[l][:, RA_B:RA_B + 48].unsqueeze(2).broadcast_to([P, 48, 2]), ALU.add))
                lk(ve.tensor_tensor(mod[:], rows4[:, :, 2:4], mod[:], ALU.add))

                def norm(w, sc_at, row, cols):
                    lk(ve.scalar_tensor_tensor(out=gain[:], in0=mod[:, sc_at:sc_at + 8, :], scalar=1.0,
                                               in1=col_a[l][:, row:row + 8].unsqueeze(2).broadcast_to([P, 8, 2]), op0=ALU.add, op1=ALU.mult))
                    dve.wait_ge(e[w + "rt"].sem, e[w + "rt"]["rt"])
                    for k in range(KT):
                        ve.tensor_tensor(H[:, k, cols], X[:, k, cols], T[:, 8, cols], ALU.mult).then_inc(e[w + "x"].next(k), 1)

                norm("n1", 8, RA_MIX, full)
                for k in range(KT):
                    part_lo("h", k, T_R[:, T_H_LO + k, :], H[:, k, :], T_R[:, T_H_HI + k, :])
                with dve.Fori(0, 2) as i:
                    for s in range(6):
                        dve.wait_ge(s_hi, i * 6 + (K + s + 1))
                        low(q + s, T_HI_IN, N_HI_IN)
                q += CHUNKS_IN
                K += SPLIT_IN
                for i in range(6):
                    dve.wait_ge(e["biasf"].sem, e["biasf"][i])
                    ve.tensor_tensor(T[:, T_BIAS + i, :].rearrange("p (n c) -> p n c", c=64), bank[(4, 5, 6, 7, 2, 3)[i]][:, :].rearrange("p (n c) -> p n c", c=64),
                                     C[:, CA["win"]].unsqueeze(1).broadcast_to([P, 8, 64]), ALU.add).then_inc(e["biasm"].next(i), 1)
                dve.wait_ge(e["ab"].sem, e["ab"]["ab"])
                ve.tensor_copy(ab[:], bank[3][:, 0:64].rearrange("p (t w n) -> p t w n", t=4, w=2)).then_inc(e["abd"].next("ab"), 1)
                dve.wait_ge(e["abd"].sem, e["abd"]["ab"])
                lk(ve.tensor_tensor(tmp_g[:, 0], ab[:, :, 0, :], dtb[l][:].unsqueeze(1).broadcast_to([P, NTT, 8]), ALU.add))
                lk(ve.tensor_scalar(tmp_g[:, 2], tmp_g[:, 0], -1.0, None, ALU.mult))
                ve.tensor_tensor(tmp_g[:, 1], tmp_g[:, 0], tmp_g[:, 2], ALU.min).then_inc(e["abd"].next("x"), 1)
                dve.wait_ge(e["aba"].sem, e["aba"]["sig"])
                lk(ve.scalar_tensor_tensor(out=tmp_g[:, 0], in0=tmp_g[:, 0], scalar=0.0, in1=tmp_g[:, 1], op0=ALU.max, op1=ALU.add))
                for d in range(2):
                    last = ve.scalar_tensor_tensor(out=gdec[:, d], in0=tmp_g[:, 0, :, 4 * d:4 * d + 4], scalar=-1.0,
                                                   in1=ea[:, 4 * d:4 * d + 4].unsqueeze(1).broadcast_to([P, NTT, 4]), op0=ALU.mult, op1=ALU.mult)
                last.then_inc(e["abd"].next("beta_g"), 1)
                dve.wait_ge(e["ab"].sem, e["ab"]["G"])
                ve.tensor_scalar(negG[:], bank[3][:, 64:96].rearrange("p (d t h) -> p d t h", d=2, t=4), -1.0, None, ALU.mult)\
                    .then_inc(e["abd"].next("negG"), 1)

                def conv(dst, src, taps, col, cols):
                    n = (TOK - cols.start) // 256
                    half = taps // 2
                    lk(ve.tensor_scalar(T[:, dst, cols], T[:, src, cols], col(half), None, ALU.mult))
                    for t_ in range(taps):
                        s_ = t_ - half
                        if s_ == 0:
                            continue
                        o_ = T[:, dst, cols].rearrange("p (s n) -> p s n", s=n)[:, :, max(0, -s_):256 - max(0, s_)]
                        i_ = T[:, src, cols].rearrange("p (s n) -> p s n", s=n)[:, :, max(0, s_):256 - max(0, -s_)]
                        last = ve.scalar_tensor_tensor(out=o_, in0=i_, scalar=col(t_), in1=o_, op0=ALU.mult, op1=ALU.add)
                        if t_ < taps - 1:
                            lk(last)
                    return last

                def normed(n_, i_, cols, g, rope):
                    dve.wait_ge(e["rt"].sem, e["rt"][n_])
                    rt_ = T[:, T_RT + n_ % 2, cols]
                    if rope:
                        dve.wait_ge(e["rot"].sem, e["rot"][n_ - 8])
                        dve.wait_ge(e["silu"].sem, e["silu"][11])
                        t_ = T[:, i_, 256:512]
                        rb_ = bank[6 + n_ % 2][:, 0:256]
                        ve.tensor_tensor(rb_, rb_, cm("sin"), ALU.mult)
                        lk(ve.tensor_tensor(t_, t_, cm("cos"), ALU.mult))
                        lk(ve.tensor_tensor(t_, t_, rb_, ALU.add))
                    ve.scalar_tensor_tensor(out=T[:, i_, cols], in0=T[:, i_, cols], scalar=g, in1=rt_, op0=ALU.mult, op1=ALU.mult)\
                        .then_inc(e["nrm"].next(n_), 1)

                def conv_dn(i):
                    cols = lat if i < 4 else full
                    lk(conv(T_CONV, T_DQ + i, 5, lambda t_: col_b[l][:, RB_CONV + 12 * t_ + i:RB_CONV + 12 * t_ + i + 1], cols))
                    ve.tensor_copy(T[:, T_DQ + i, cols], T[:, T_CONV, cols]).then_inc(e["conv"].next(i), 1)
                    dve.wait_ge(e["conv"].sem, e["conv"][i])

                dve.wait_ge(s_taken[1], (U + 24) // 2 + 1)
                dve.wait_ge(s_taken[0], (U + 24) // 2 + 1)
                for j in range(8):
                    conv_dn(j)
                    g_ = col_b[l][:, RB_QG:RB_QG + 1] if j < 4 else col_b[l][:, RB_KG:RB_KG + 1]
                    normed(j, T_NQ + j, lat if j < 4 else full, g_, False)
                for j in range(8, 12):
                    conv_dn(j)
                for j in range(8, 16):
                    q_ = j < 12
                    if j == 13:
                        for i in range(4):
                            if i == 0:
                                dve.wait_ge(s_taken[1], (U + 36) // 2 + 1)
                                dve.wait_ge(s_taken[0], (U + 36) // 2 + 1)
                            lk(ve.tensor_tensor(T[:, T_C + i, lat], T[:, T_C + i, lat], T[:, T_U + i, lat], ALU.mult))
                            lk(conv(T_U + i, T_C + i, 3, lambda t_: col_b[l][:, RB_SC + 4 * t_ + i:RB_SC + 4 * t_ + i + 1], lat))
                            last = ve.tensor_tensor(T[:, T_U + i, lat], T[:, T_U + i, lat], T[:, T_B + i, lat], ALU.mult)
                        last.then_inc(e["sc"].next("sc"), 1)
                    normed(j, T_DQ + j - 8, lat if q_ else full, DN_D ** -0.5 if q_ else 1.0, True)
                U += TILES_IN

                items = names_na(l)
                N = len(items)
                for n_ in range(N + 3):
                    if n_ < N:
                        qt, h = items[n_]
                        keys = CTX_LEN if qt < 2 else TOK
                        b_ = bank[n_ % 4]
                        if n_ >= 4:
                            dve.wait_ge(e["aE"].sem, e["aE"][n_ - 4])
                        dve.wait_ge(e["aS"].sem, e["aS"][n_])
                        if qt >= 2:
                            t_ = qt - 2
                            bv = T[:, T_BIAS:T_BIAS + 6, :].rearrange("p a b -> p (a b)").rearrange("p (h j) -> p h j", h=8)[
                                :, h, 64 * (2 - 2 * t_):64 * (6 - 2 * t_)]
                            lk(ve.tensor_tensor(b_[:, 256:512], b_[:, 256:512], bv, ALU.add))
                        lk(ve.tensor_reduce(mx[:, n_ % 4, 0:1], b_[:, 0:keys], AX_X, ALU.max))
                        ve.tensor_scalar(mx[:, n_ % 4, 1:2], mx[:, n_ % 4, 0:1], -NA_SCALE, None, ALU.mult).then_inc(e["aM"].next(n_), 1)
                    if 1 <= n_ <= N:
                        m_ = n_ - 1
                        qt, h = items[m_]
                        keys = CTX_LEN if qt < 2 else TOK
                        dve.wait_ge(e["aE"].sem, e["aE"][m_])
                        lk(ve.reciprocal(mx[:, m_ % 4, 3:4], mx[:, m_ % 4, 2:3]))
                        ve.tensor_scalar(T[:, T_E[m_ % 4], 0:keys], T[:, T_E[m_ % 4], 0:keys], mx[:, m_ % 4, 3:4], None, ALU.mult)\
                            .then_inc(e["aP"].next(m_), 1)
                    if n_ >= 4 and n_ % 2 == 0:
                        m_ = n_ - 3
                        qt, h = items[m_]
                        dve.wait_ge(e["aO"].sem, e["aO"][m_])
                        ve.tensor_copy(T[:, T_NQ + h // 2, P * qt:P * qt + P], bank[6 + m_ // 2 % 2][:, 0:P]).then_inc(e["aD"].next(m_ // 2), 1)

                dve.wait_ge(e["tpc"].sem, e["tpc"][11])
                dve.wait_ge(e["aO"].sem, N)
                ident4 = cm4("ident")
                for j in range(4):
                    grp = [g for g in CH if g[0] == j]

                    def both(f):
                        for g in grp:
                            f(*g)

                    def ctx_of(d):
                        wt = [v4(T[:, T_WORK[d][i], :]) for i in range(8)]
                        return e["dp"][d], e["dd"][d], e["da"][d], e["dg"][d], wt, [v4(bank[2 + 3 * d + i][:, :]) for i in range(3)]

                    def M(j, d, tt):
                        dp, dd, da, dg, wt, bk = ctx_of(d)
                        dve.wait_ge(dp.sem, dp[(j, "gB")])
                        for h in range(4):
                            last = ve.scalar_tensor_tensor(out=wt[0][:, h], in0=bk[0][:, h], scalar=negG[:, d, tt, h:h + 1],
                                                           in1=cm(f"neg{d}"), op0=ALU.add, op1=ALU.add)
                        last.then_inc(dd.next((j, "M")), 1)

                    def LT(j, d, tt):
                        dp, dd, da, dg, wt, bk = ctx_of(d)
                        dve.wait_ge(dp.sem, dp[(j, "KK")])
                        dve.wait_ge(da.sem, da[(j, "DT")])
                        for h in range(4):
                            last = ve.scalar_tensor_tensor(out=wt[2][:, h], in0=bk[1][:, h], scalar=beta[:, tt, 4 * d + h:4 * d + h + 1],
                                                           in1=wt[0][:, h], op0=ALU.mult, op1=ALU.mult)
                        last.then_inc(dd.next((j, "LT")), 1)
                        dve.wait_ge(dd.sem, dd[(j, "LT")])
                        lk(ve.tensor_tensor(wt[4], wt[2], cm4(f"lev0{1 - d}"), ALU.mult))
                        ve.tensor_tensor(wt[4], ident4, wt[4], ALU.subtract).then_inc(dd.next((j, "XT0")), 1)

                    def X0(j, d, tt):
                        dp, dd, da, dg, wt, bk = ctx_of(d)
                        dve.wait_ge(dp.sem, dp[(j, "L")])
                        lk(ve.tensor_tensor(wt[3], bk[1], cm4(f"lev0{d}"), ALU.mult))
                        ve.tensor_tensor(wt[3], ident4, wt[3], ALU.subtract).then_inc(dd.next((j, "X0")), 1)
                        if need_o(l, tt):
                            dve.wait_ge(dg.sem, dg[(j, "kgl")])
                            dve.wait_ge(dp.sem, dp[(j, "QK")])
                            ve.tensor_tensor(wt[0], bk[2], wt[0], ALU.mult).then_inc(dd.next((j, "AT")), 1)

                    def Yk(k):
                        def f(j, d, tt):
                            dp, dd, da, dg, wt, bk = ctx_of(d)
                            dve.wait_ge(dp.sem, dp[(j, f"Y{k}")])
                            ve.tensor_tensor(wt[5], bk[0], cm4(f"lev{k}{d}"), ALU.mult).then_inc(dd.next((j, f"Y{k}")), 1)
                        return f

                    def Zk(k):
                        def f(j, d, tt):
                            dp, dd, da, dg, wt, bk = ctx_of(d)
                            dve.wait_ge(dp.sem, dp[(j, f"ZT{k}")])
                            if k < LEVELS - 1:
                                ve.tensor_tensor(wt[3], wt[3], bk[1], ALU.subtract).then_inc(dd.next((j, f"X{k}")), 1)
                            ve.tensor_tensor(wt[4], wt[4], bk[2], ALU.subtract).then_inc(dd.next((j, f"XT{k}")), 1)
                        return f

                    def R(j, d, tt):
                        if not j:
                            return
                        dp, dd, da, dg, wt, bk = ctx_of(d)
                        dve.wait_ge(dp.sem, dp[(j, "KS")])
                        ve.tensor_tensor(wt[5], v4(T[:, T_VTOK_DN + tt, :]), bk[1], ALU.subtract).then_inc(dd.next((j, "R")), 1)

                    def vn(j, d, tt):
                        dp, dd, da, dg, wt, bk = ctx_of(d)
                        dve.wait_ge(dp.sem, dp[(j, "VN")])
                        ve.tensor_tensor(wt[3], bk[0], beta[:, tt, 4 * d:4 * d + 4].unsqueeze(2).broadcast_to([P, 4, P]), ALU.mult)\
                            .then_inc(dd.next((j, "vn")), 1)

                    def OS(j, d, tt):
                        dp, dd, da, dg, wt, bk = ctx_of(d)
                        if need_o(l, tt):
                            dve.wait_ge(dp.sem, dp[(j, "O")])
                            o_ = T[:, T_OT:T_OT + 4, P * tt:P * tt + P]
                            if j % 2 == 0:
                                ve.tensor_copy(o_, bk[2]).then_inc(dd.next((j, "O")), 1)
                            else:
                                pj = [g for g in CH if g[1] == 1 - d and g[2] == tt][0][0]
                                dve.wait_ge(e["dd"][1 - d].sem, e["dd"][1 - d][(pj, "O")])
                                ve.tensor_tensor(o_, o_, bk[2], ALU.add).then_inc(dd.next((j, "O")), 1)
                        if j < 3:
                            S = T[:, T_STATE + d, :]
                            dve.wait_ge(dp.sem, dp[(j, "dS")])
                            if j == 0:
                                ve.tensor_copy(v4(S), bk[1]).then_inc(dd.next((j, "S")), 1)
                            else:
                                dve.wait_ge(dg.sem, dg[(j, "gl")])
                                for h in range(4):
                                    last = ve.scalar_tensor_tensor(out=v4(S)[:, h], in0=v4(S)[:, h], scalar=glast[:, d, h:h + 1],
                                                                   in1=bk[1][:, h], op0=ALU.mult, op1=ALU.add)
                                last.then_inc(dd.next((j, "S")), 1)

                    both(M)
                    both(LT)
                    both(X0)
                    for k in range(1, LEVELS):
                        both(Yk(k))
                        both(Zk(k))
                    both(R)
                    both(vn)
                    both(OS)

                def dn_out(i):
                    n_ = 16 + i
                    dve.wait_ge(e["rt"].sem, e["rt"][n_])
                    rt_ = T[:, T_RT + n_ % 2, lat]
                    dve.wait_ge(e["silu"].sem, e["silu"]["z"])
                    lk(ve.scalar_tensor_tensor(out=rt_, in0=T[:, T_OT + i, lat], scalar=col_b[l][:, RB_OUT:RB_OUT + 1], in1=rt_,
                                               op0=ALU.mult, op1=ALU.mult))
                    ve.tensor_tensor(T[:, T_Z + i, lat], rt_, T[:, T_Z + i, lat], ALU.mult).then_inc(e["nrm"].next(n_), 1)

                for k in range(4):
                    part_lo("na", k, T_R[:, T_NQ + k, lat], T[:, T_NQ + k, lat], T_R[:, T_NA_HI[k], lat])
                for v in range(3):
                    piece_lo(v)
                for v in range(SPLIT_MERGE):
                    r_, a = divmod(v, 6)
                    hf, b = divmod(r_, 3)
                    if v == 1:
                        for k in range(KT):
                            part_lo("H", k, H_R[:, k, lat], H[:, k, lat], T_R[:, T_HM_HI + k, lat])
                    if a >= 2:
                        m = a - 2
                        u = U + 8 * r_ + 4 + m
                        dve.wait_ge(s_taken[u % 2], u // 2 + 2)
                        sg_, br_ = T[:, T_SG + m, lat], T[:, T_BR + m, lat]
                        mg_ = T[:, T_MERGED + 4 * hf + m, lat]
                        if b == 0:
                            ve.tensor_tensor(mg_, sg_, br_, ALU.mult).then_inc(e["mgd"].next(4 * r_ + m), 1)
                        else:
                            lk(ve.tensor_tensor(sg_, sg_, br_, ALU.mult))
                            ve.tensor_tensor(mg_, mg_, sg_, ALU.add).then_inc(e["mgd"].next(4 * r_ + m), 1)
                    piece_lo(v + 3)
                    if r_ == 0 and a >= 2:
                        dn_out(a - 2)
                    if v == 5:
                        for k in range(4):
                            part_lo("dn", k, T_R[:, T_Z + k, lat], T[:, T_Z + k, lat], T_R[:, T_DN_HI[k], lat])
                        for k in range(4):
                            part_lo("sc", k, T_R[:, T_U + k, lat], T[:, T_U + k, lat], T_R[:, T_SC_HI[k], lat])
                    if v == 29:
                        for k in range(4):
                            part_lo("mg", k, T_R[:, T_MERGED + k, lat], T[:, T_MERGED + k, lat], T_R[:, T_MG_HI[k], lat])
                for k in range(4, 8):
                    part_lo("mg", k, T_R[:, T_MERGED + k, lat], T[:, T_MERGED + k, lat], T_R[:, T_MG_HI[k], lat])
                U += TILES_MERGE
                for m in range(KT):
                    u = U + m
                    if m + 3 < TILES_OUT:
                        piece_lo(SPLIT_MERGE + m + 3)
                    dve.wait_ge(s_tile[u % 2], u // 2 + 1)
                    for n_, (s0, v) in enumerate(segs):
                        last = ve.scalar_tensor_tensor(out=X[:, m, s0:s0 + 256], in0=bank[u % 2][:, s0:s0 + 256], scalar=mod[:, 16 + m, v:v + 1],
                                                       in1=X[:, m, s0:s0 + 256], op0=ALU.mult, op1=ALU.add)
                        if n_ == len(segs) - 1:
                            last.then_inc(s_taken[u % 2], 1)
                U += TILES_OUT
                K += SPLIT_MERGE + SPLIT_OUT
                q += CHUNKS_MERGE + CHUNKS_OUT
                dve.wait_ge(s_taken[0], U // 2 + 1)
                dve.wait_ge(s_taken[1], U // 2 + 1)
                norm("n2", 32, RA_FFN, lat)

                tr = slice(t0 // P, NTT)
                nt = NTT - t0 // P
                dve.wait_ge(e["rp"].sem, e["rp"]["scores"])
                scores = bank[4][:, 0:64].rearrange("p (t n) -> p t n", t=NTT)[:, tr]
                R_ = lambda i: rs[:, i, tr, :]
                lk(ve.tensor_tensor(R_(1), scores, rbias[:].unsqueeze(1).broadcast_to([P, nt, 16]), ALU.add))
                g4 = lambda i: rs[:, i, tr, :].rearrange("p t (g x) -> p (t g) x", g=4)

                def rank(vals, cmp_):
                    for j in range(4):
                        for lo, hi, op in ((0, j, ALU.is_gt), (j + 1, 4, ALU.is_ge)):
                            if hi > lo:
                                last = ve.tensor_tensor(cmp_[:, :, lo:hi, j], vals[:, :, j:j + 1].broadcast_to([P, cmp_.shape[1], hi - lo]),
                                                        vals[:, :, lo:hi], op)
                        last = ve.memset(cmp_[:, :, j, j], 0.0)
                    return last
                rc = rcmp[:, tr].rearrange("p t g i j -> p (t g) i j")
                lk(rank(g4(1), rc))
                lk(ve.tensor_reduce(g4(2), rc, AX_X, ALU.add))
                lk(ve.tensor_scalar(R_(2), R_(2), 1.5, None, ALU.is_lt))
                lk(ve.tensor_tensor(R_(3), R_(2), R_(1), ALU.mult))
                gs = rs[:, 4, tr, 0:4]
                lk(ve.tensor_reduce(gs.rearrange("p t g -> p t g"), rs[:, 3, tr, :].rearrange("p t (g x) -> p t g x", g=4), AX_X, ALU.add))
                rg = rcmp[:, tr, 0]
                lk(rank(gs, rg))
                lk(ve.tensor_reduce(rs[:, 5, tr, 0:4], rg, AX_X, ALU.add))
                lk(ve.tensor_scalar(rs[:, 5, tr, 0:4], rs[:, 5, tr, 0:4], 0.5, None, ALU.is_lt))
                ve.tensor_tensor(rs[:, 2, tr, :].rearrange("p t (g x) -> p t g x", g=4), rs[:, 2, tr, :].rearrange("p t (g x) -> p t g x", g=4),
                                 rs[:, 5, tr, 0:4].unsqueeze(3).broadcast_to([P, nt, 4, 4]), ALU.mult).then_inc(e["rd"].next("comb"), 1)
                dve.wait_ge(e["rd"].sem, e["rd"]["comb"])
                lk(ve.tensor_tensor(R_(6), R_(2), scores, ALU.mult))
                lk(ve.tensor_reduce(rs[:, 4, tr, 4:5], R_(6), AX_X, ALU.add))
                lk(ve.reciprocal(rs[:, 4, tr, 5:6], rs[:, 4, tr, 4:5]))
                lk(ve.tensor_tensor(R_(7), R_(6), rs[:, 4, tr, 5:6].broadcast_to([P, nt, 16]), ALU.mult))
                for i in (0, 3):
                    ve.tensor_copy(pair[:, tr, :, i], cm("tokid")[:, 0:nt].unsqueeze(2).broadcast_to([P, nt, 16]))
                lk(ve.tensor_copy(pair[:, tr, :, 1], R_(7)))
                ve.tensor_tensor(pair[:, tr, :, 2], R_(7), pair[:, tr, :, 1], ALU.subtract)
                dve.wait_ge(e["rp"].sem, e["rp"]["cnt"])
                cnt = bank[5][:, 0:64].rearrange("p (t n) -> p t n", t=NTT)[:, tr]
                lk(ve.tensor_tensor(R_(3), cnt, R_(2), ALU.mult))
                ve.tensor_scalar(R_(3), R_(3), -1.0, None, ALU.add).then_inc(e["rd"].next("rk"), 1)
                dve.wait_ge(e["rd"].sem, e["rd"]["rk"])
                lk(ve.tensor_scalar(R_(4), R_(3), CAPACITY - 0.5, None, ALU.is_ge))
                ve.tensor_reduce(mx[:, 0, 0:1], rs[:, 4, tr, :].rearrange("p t n -> p (t n)"), AX_X, ALU.add).then_inc(e["rd"].next("ov"), 1)
                for x_ in range(N_EXPERTS):
                    if x_ >= 2:
                        dve.wait_ge(e["ohp"].sem, e["ohp"][x_ - 2])
                    oh_ = onehot[:, x_ % 2, :].rearrange("p (t s) -> p t s", t=NTT)[:, tr]
                    ve.tensor_tensor(oh_, cm("iota").unsqueeze(1).broadcast_to([P, nt, P]), R_(3)[:, :, x_:x_ + 1].broadcast_to([P, nt, P]),
                                     ALU.is_equal).then_inc(e["oh"].next(x_), 1)
                dve.wait_ge(e["rp"].sem, e["rp"]["flag"])
                ve.tensor_scalar(flag[:], bank[5][:, 256:257], 1.0, None, ALU.min).then_inc(e["rd"].next("flag"), 1)
                dve.wait_ge(e["ohp"].sem, N_EXPERTS)
                slots = bank[4][:, 0:64].rearrange("p (n w) -> p n w", w=4)
                ve.tensor_copy(slot_tok[:], slots[:, :, 0])
                lk(ve.tensor_copy(slot_comb[:], slots[:, :, 1]))
                ve.tensor_tensor(slot_comb[:], slots[:, :, 2], slot_comb[:], ALU.add).then_inc(e["rd"].next("slots"), 1)
                lk(ve.tensor_tensor(R_(1), R_(3), cm("ebase").unsqueeze(1).broadcast_to([P, nt, 16]), ALU.add))
                lk(ve.scalar_tensor_tensor(out=R_(1), in0=R_(4), scalar=2.0 * ZERO_ROW, in1=R_(1), op0=ALU.mult, op1=ALU.add))
                lk(ve.scalar_tensor_tensor(out=R_(5), in0=R_(1), scalar=1.0, in1=R_(2), op0=ALU.add, op1=ALU.mult))
                lk(ve.tensor_reduce(mx[:, 0, 0:nt], R_(5), AX_X, ALU.max))
                ve.tensor_scalar(tok_slot[:, 0, tr], mx[:, 0, 0:nt], -1.0, float(ZERO_ROW), ALU.add, ALU.min)
                lk(ve.scalar_tensor_tensor(out=R_(5), in0=R_(2), scalar=-8.0 * ZERO_ROW, in1=R_(1), op0=ALU.mult, op1=ALU.add))
                lk(ve.tensor_reduce(mx[:, 1, 0:nt], R_(5), AX_X, ALU.min))
                ve.tensor_scalar(tok_slot[:, 1, tr], mx[:, 1, 0:nt], 8.0 * ZERO_ROW, float(ZERO_ROW), ALU.add, ALU.min)\
                    .then_inc(e["rd"].next("back"), 1)

                def chunk_lo(p_, c_):
                    dve.wait_ge(s_hi, p_ * 12 + (K + c_ + 1))
                    low(q + c_, T_HI_EXP, N_HI_EXP)

                def rows_lo(i, n_):
                    for hf in range(2):
                        dve.wait_ge(e["xca"], n_ + hf)
                        last = ve.tensor_tensor(T_R[:, T_XT_LO + 2 * i + hf, :], bank[2 + hf][:, :], T_R[:, T_XT + 2 * i + hf, :], ALU.subtract)
                    last.then_inc(e["xcd"], 1)

                for s in range(N_HI_EXP):
                    chunk_lo(0, s)
                rows_lo(0, 1)

                def expert(p_, i, tail):
                    chunk_lo(p_, 6 * i + 4)
                    chunk_lo(p_, 6 * i + 5)
                    dve.wait_ge(s_taken[0], p_ * 4 + (2 * i + U // 2 + 2))
                    dve.wait_ge(s_tile[1], p_ * 4 + (2 * i + U // 2 + 1))
                    comb = slot_comb[:, 2 * p_ + i:2 * p_ + i + 1] if isinstance(p_, int) else slot_comb[:, bass.ds(p_ * 2 + i, 1)]
                    ve.scalar_tensor_tensor(out=T[:, T_HID + i, :], in0=bank[1][:, :], scalar=comb, in1=T[:, T_MSG + i, :],
                                            op0=ALU.mult, op1=ALU.mult).then_inc(s_taken[1], 1)
                    if not tail:
                        rows_lo(1 - i, p_ * 4 + (2 * i + 3))
                    dve.wait_ge(e["hc"], p_ * 2 + (i + 1))
                    ve.tensor_tensor(T_R[:, T_HT_LO + i, :], bank[4 + i][:, :], T_R[:, T_HT + i, :], ALU.subtract).then_inc(e["hcd"], 1)
                    if not tail:
                        chunk_lo(p_, 6 * i + 6)
                        chunk_lo(p_, 6 * i + 7)
                    dve.wait_ge(s_tile[0], p_ * 4 + (2 * i + U // 2 + 2))
                    dve.wait_ge(e["yst"][i], p_ * 16 + 16)
                    ve.tensor_copy(T[:, T_Y + 2 * i, :], bank[0][:, :]).then_inc(s_taken[0], 1)
                    if not tail:
                        chunk_lo(p_, 6 * i + 8)
                        chunk_lo(p_, 6 * i + 9)

                with dve.Fori(0, N_EXPERTS // 2 - 1) as p_:
                    expert(p_, 0, False)
                    expert(p_, 1, False)
                expert(N_EXPERTS // 2 - 1, 0, False)
                expert(N_EXPERTS // 2 - 1, 1, True)
                U += N_EXPERTS * TILES_EXP
                n_tt = NTT - t0 // P

                def both_added(n_):
                    dve.wait_ge(e["bg"][n_ % 2], 32 * (n_ // 2 + 1))
                    for hf in range(2):
                        if n_ >= 2:
                            dve.wait_ge(e["bt"].sem, 2 * (n_ - 2) + hf + 1)
                        t_ = T_GATHER + 4 * (n_ % 2) + hf
                        ve.tensor_tensor(T[:, t_, :], T[:, t_, :], T[:, t_ + 2, :], ALU.add).then_inc(e["bs"].sem, 1)

                both_added(0)
                for n_ in range(n_tt):
                    if n_ + 1 < n_tt:
                        both_added(n_ + 1)
                    tt = t0 // P + n_
                    v = 1 if tt < 2 else 0
                    for hf in range(2):
                        dve.wait_ge(e["bt"].sem, 2 * n_ + hf + 1)
                        for k in range(4):
                            m = 4 * hf + k
                            last = ve.scalar_tensor_tensor(out=X[:, m, P * tt:P * tt + P], in0=bank[6 + hf][:, P * k:P * k + P],
                                                           scalar=mod[:, 40 + m, v:v + 1], in1=X[:, m, P * tt:P * tt + P], op0=ALU.mult, op1=ALU.add)
                        last.then_inc(e["bx"].sem, 1)

                with dve.If(dve.value_load(flag[0:1, 0:1], min_val=0, max_val=1) > 0):
                    dve.wait_ge(e["bx"].sem, 2 * n_tt)
                    for b in range(2):
                        ve.memset(mx[:, b, :], 0.0).then_inc(e["f_taken"][b], 1)
                    for m in range(KT):
                        ve.memset(T[:, F_ACC + m, lat], 0.0)
                    ve.tensor_tensor(R_(6), R_(7), R_(4), ALU.mult).then_inc(e["f_hid"], 4)
                    dve.wait_ge(e["f_comb"], 1)
                    ve.tensor_copy(combT[:, lat], bank[5][0:16, lat]).then_inc(e["f_comb"], 1)
                    with dve.Fori(0, N_EXPERTS // 2) as p_:
                        for i in range(2):
                            dve.wait_ge(e["f_cb"][i], p_ * 16 + 16)
                            for f in range(4):
                                ug, uu = (0, 1, 4, 5)[f], (2, 3, 6, 7)[f]
                                dve.wait_ge(e["f_taken"][ug % 2], p_ * 16 + (8 * i + ug // 2 + 2))
                                dve.wait_ge(e["f_tile"][uu % 2], p_ * 16 + (8 * i + uu // 2 + 1))
                                ve.tensor_tensor(T[:, F_HID + f, lat], T[:, F_MSG + f, lat], bank[uu % 2][:, lat], ALU.mult).then_inc(e["f_taken"][uu % 2], 1)
                                dve.wait_ge(e["f_taken"][uu % 2], p_ * 16 + (8 * i + uu // 2 + 2))
                                ve.tensor_tensor(T[:, F_HID + f, lat], T[:, F_HID + f, lat], T[:, F_CB + i, lat], ALU.mult).then_inc(e["f_hid"], 1)
                            for m in range(KT):
                                ud = 8 + m
                                dve.wait_ge(e["f_tile"][ud % 2], p_ * 16 + (8 * i + ud // 2 + 1))
                                ve.tensor_tensor(T[:, F_ACC + m, lat], T[:, F_ACC + m, lat], bank[ud % 2][:, lat], ALU.add).then_inc(e["f_taken"][ud % 2], 1)
                    for b in range(2):
                        dve.wait_ge(e["f_taken"][b], 8 * N_EXPERTS + 1)
                    for m in range(KT):
                        for s0, v in segs:
                            ve.scalar_tensor_tensor(out=X[:, m, s0:s0 + 256], in0=T[:, F_ACC + m, s0:s0 + 256], scalar=mod[:, 40 + m, v:v + 1],
                                                    in1=X[:, m, s0:s0 + 256], op0=ALU.mult, op1=ALU.add)
                dve.wait_ge(e["bx"].sem, 2 * n_tt)
                ve.memset(mx[:, 0, 0:1], 0.0).then_inc(e["x2"].next("x2"), 1)

            dve.wait_ge(s_turned, 1)
            for i in range(4):
                last = ve.tensor_copy(T[:, i, :], bank[2 + i][:, :])
            last.then_inc(s_store, 1)


_INS = ['x', 'c', 'ctx', 'c_ctx', 'w_ada', 'b_ada', 'norm_mix_g', 'norm_ffn_g', 'w_in', 'na_q_norm_g', 'na_k_norm_g',
        'na_rpb', 'dn_conv_w', 'dn_a_log', 'dn_dt_bias', 'dn_out_norm_g', 'sc_conv_w', 'w_branch_na', 'w_branch_dn',
        'w_branch_sc', 'w_out', 'w_router', 'router_bias', 'moe_w_gate', 'moe_w_up', 'moe_w_down']


def kernel(**inputs):
    import concourse.bacc as _bacc
    from concourse.bass_utils import run_bass_kernel_spmd as _run

    nc = _bacc.Bacc("TRN2", target_bir_lowering=False, num_devices=1)
    arrays, args = {}, {}
    for name in _INS + ["const"]:
        a = constants()[1] if name == "const" else np.ascontiguousarray(inputs[name])
        arrays[f"in_{name}_dram"] = a
        args[name] = nc.dram_tensor(f"in_{name}_dram", a.shape, mybir.dt.from_np(a.dtype), kind="ExternalInput").ap()
    out = nc.dram_tensor("out_0_dram", (1, SEQ, D_MODEL), F32, kind="ExternalOutput").ap()
    build(nc, out=out, **args)
    r = _run(nc, [arrays], core_ids=[0])
    return r.results[0]["out_0_dram"]
```

```python
from contextlib import ExitStack

import numpy as np

import concourse.bass as bass
from concourse import mybir

F32 = mybir.dt.float32
F32R = mybir.dt.float32r
U32 = mybir.dt.uint32
ALU = mybir.AluOpType
ACT = mybir.ActivationFunctionType
AX_X = mybir.AxisListType.X

P = 128
D_MODEL, SEQ, CTX_LEN, DEPTH = 1024, 256, 256, 2
GRID_W = 64
NA_HEADS, NA_D, DN_HEADS, DN_D = 8, 64, 4, 128
WIN_C, WIN_R_MAX = 16, 8
N_EXPERTS, N_GROUPS, D_EXPERT = 16, 4, 512
EPS = 1e-6
NEG_INF = -1e30
TOK = CTX_LEN + SEQ
KT = D_MODEL // P
NTT = TOK // P
RING = 6
CHUNK = 2048
NT = 54
NA_SCALE = NA_D ** -0.5
DN_CHUNK = P
LEVELS = 7
COL_NA, COL_DN, COL_Z, COL_AB, COL_SC, COL_GATE = 0, 1536, 3072, 3584, 3600, 5136
T_NQ, T_NK, T_NV, T_DQ, T_DK, T_DV, T_Z, T_U, T_B, T_C = 0, 4, 8, 12, 16, 20, 24, 28, 32, 36
T_SQ, T_RT = 46, 48
T_BIAS = 40
T_VTOK = 32
T_CONV = 50
T_E = (50, 51, 8, 9)
T_PT = 52
T_KTOK_DN, T_VTOK_DN = 36, 46
T_OT = 32
T_STATE = 44
T_WORK = ((4, 5, 6, 7, 8, 9, 10, 11), (20, 21, 22, 23, 50, 51, 52, 53))
T_MERGED = 12
T_BR, T_SG = 4, 8
T_ROWS = 10
T_RCMP, T_PAIR, T_RS = 20, 21, 23
T_MODROW = 24
T_XROW, T_XT, T_MSG, T_HID, T_HT, T_Y = 0, 4, 8, 10, 12, 14
T_HROW, T_GATHER = 24, 24
T_ONEHOT = 18
T_HI_ADA, N_HI_ADA = 12, 3
T_HI_EXP, N_HI_EXP = 32, 4
T_HI_IN, N_HI_IN = 46, 2
T_H_HI, T_H_LO = 24, 32
T_HI_HALF = (20, 22, 52)
T_HM_HI, T_NA_HI, T_DN_HI, T_SC_HI = 36, (44, 45, 50, 51), (32, 33, 34, 35), (46, 47, 48, 49)
T_MG_HI = T_NA_HI + T_DN_HI
T_XT_LO, T_HT_LO = 48, 52
F_HID, F_MSG, F_ACC, F_CB, F_COMBT = 0, 8, 12, 20, 22
RA_B, RA_MIX, RA_FFN, RA_N = 0, 48, 56, 64
RB_CONV, RB_SC, RB_OUT, RB_QG, RB_KG, RB_N = 0, 60, 72, 73, 74, 75
TILES_ADA, TILES_IN, TILES_MERGE, TILES_OUT, TILES_EXP = 24, 40, 48, 8, 4
CHUNKS_ADA, CHUNKS_IN, CHUNKS_MERGE, CHUNKS_OUT, CHUNKS_EXP = 24, 20, 18, 4, 6
CAPACITY = P
ZERO_ROW = N_EXPERTS * CAPACITY
N_MO = CHUNKS_MERGE + CHUNKS_OUT
ADA_BEHIND = [[0, 1], [2, 3]] + [[i + 2] for i in range(2, N_MO)]
assert sum(ADA_BEHIND, []) == list(range(CHUNKS_ADA)) and DEPTH == 2
Q_LAYER = (0, 2 * CHUNKS_ADA + CHUNKS_IN + N_MO + N_EXPERTS * CHUNKS_EXP)
U_LAYER = (0, TILES_ADA + TILES_IN + TILES_MERGE + TILES_OUT + N_EXPERTS * TILES_EXP)
U_EXPERTS = (U_LAYER[1] - N_EXPERTS * TILES_EXP, U_LAYER[1] + TILES_IN + TILES_MERGE + TILES_OUT)


def merge_pieces(l):
    out, at = [], 0
    for i in range(N_MO):
        ada = [("a", 2 * c_ + h, at + 1 + n) for n, c_ in enumerate(ADA_BEHIND[i] if l == 0 else []) for h in range(2)]
        out += [("m", 2 * i, at)] + ada[:len(ada) // 2] + [("m", 2 * i + 1, at)] + ada[len(ada) // 2:]
        at += 1 + len(ada) // 2
    return out


PIECES = [merge_pieces(l) for l in range(DEPTH)]
MERGE_CHUNKS = [pieces[-1][2] + 1 for pieces in PIECES]
SPLIT_ADA, SPLIT_IN, SPLIT_MERGE, SPLIT_OUT, SPLIT_EXP = 24, 12, 36, 8, 96
K_LAYER = (0, SPLIT_ADA + SPLIT_IN + len(PIECES[0]) + SPLIT_EXP)


def last_uses():
    out = [("t", m) for m in range(TILES_ADA)]
    for l in range(DEPTH):
        t = len(out) if l == 0 else U_LAYER[1]
        out += [("t", t + 2 * m + 1) for m in range(CHUNKS_IN)]
        t += TILES_IN
        for i in range(N_MO):
            out.append(("t", t + (8 * (i // 3) + (3, 5, 7)[i % 3] if i < CHUNKS_MERGE else TILES_MERGE + 2 * (i - CHUNKS_MERGE) + 1)))
            out += [("a", c_) for c_ in ADA_BEHIND[i]] if l == 0 else []
        t += TILES_MERGE + TILES_OUT
        out += [("t", t + 4 * (m // 6) + (0, 0, 1, 1, 2, 3)[m % 6]) for m in range(N_EXPERTS * CHUNKS_EXP)]
    return out


USES = last_uses()


def last_tile_of_piece(v):
    r, a = divmod(v, 6)
    return (8 * r + (2 * a + 1 if a < 2 else a + 2)) if v < SPLIT_MERGE else TILES_MERGE + v - SPLIT_MERGE


def constants():
    a = np.arange(P)
    r, c = a[:, None], a[None, :]
    parts = {
        "ident": (r == c), "ones": np.ones((P, P)), "ones64": (r // 64 == c // 64),
        "tri0": (r <= c), "tri1": (r >= c),
        "neg0": np.where(r <= c, 0.0, NEG_INF), "neg1": np.where(r >= c, 0.0, NEG_INF),
    }
    for k in range(LEVELS):
        s = 1 << k
        m = (r // (2 * s) == c // (2 * s)) & (r // s % 2 == 1) & (c // s % 2 == 0)
        parts[f"lev{k}0"] = m
        parts[f"lev{k}1"] = m.T
    rot = np.zeros((P, P))
    for d in range(P):
        if d % 64 < 32:
            rot[d + 32, d] = -1.0
        else:
            rot[d - 32, d] = 1.0
    parts["rot"] = rot
    parts["flip"] = (r // 64 == c // 64) & (r % 64 == 63 - c % 64)
    n_freq = DN_D // 4
    inv = np.float32(10000.0) ** (-np.arange(n_freq, dtype=np.float32) / np.float32(n_freq))
    t = np.arange(SEQ)
    pos = np.stack([t // GRID_W, t % GRID_W], 0).astype(np.float32)
    ang = pos[a // 64][:, :] * inv[a % 32][:, None]
    parts["cos"], parts["sin"] = np.cos(ang), np.sin(ang)
    qc = a % 64
    c0 = np.clip(qc - WIN_C // 2, 0, GRID_W - WIN_C)[:, None]
    kc = np.arange(GRID_W)[None, :]
    parts["win"] = np.where((kc >= c0) & (kc < c0 + WIN_C), 0.0, NEG_INF / NA_SCALE)
    parts["iota"] = np.broadcast_to(c, (P, P))
    parts["ebase"] = np.broadcast_to(CAPACITY * np.arange(N_EXPERTS)[None, :], (P, N_EXPERTS))
    parts["tokid"] = r + P * np.arange(NTT)[None, :]
    parts["eps"] = np.full((P, 1), EPS)
    at, n = {}, 0
    for name, m in parts.items():
        at[name] = slice(n, n + m.shape[1])
        n += m.shape[1]
    return at, np.ascontiguousarray(np.concatenate([np.asarray(m, np.float32) for m in parts.values()], 1))


class Line:

    def __init__(self, sem, names, before=0):
        self.sem, self.names, self.seen = sem, names, 0
        self.value = {n: before + i + 1 for i, n in enumerate(names)}
        assert len(self.value) == len(names)

    def __getitem__(self, name):
        return self.value[name]

    def next(self, name):
        assert self.names[self.seen] == name, (self.names[self.seen], name)
        self.seen += 1
        return self.sem


def build(nc, x, c, ctx, c_ctx, w_ada, b_ada, norm_mix_g, norm_ffn_g, w_in, na_q_norm_g, na_k_norm_g, na_rpb,
          dn_conv_w, dn_a_log, dn_dt_bias, dn_out_norm_g, sc_conv_w, w_branch_na, w_branch_dn, w_branch_sc, w_out,
          w_router, router_bias, moe_w_gate, moe_w_up, moe_w_down, const, out):
    CA, _ = constants()
    NCONST = const.shape[1]
    rpb_pad = nc.dram_tensor("rpb_pad", [DEPTH, NA_HEADS * 15, P], F32).ap()
    h_rows = [nc.dram_tensor(f"h_rows{l}", [TOK if l < DEPTH - 1 else SEQ, D_MODEL], F32).ap() for l in range(DEPTH)]
    y_rows = [nc.dram_tensor(f"y_rows{l}", [ZERO_ROW + 1, D_MODEL], F32).ap() for l in range(DEPTH)]
    comb_rows = nc.dram_tensor("comb_rows", [DEPTH, N_EXPERTS, TOK], F32).ap()
    with ExitStack() as stack:
        def sb(name, shape, dt=F32):
            return stack.enter_context(nc.sbuf_tensor(name, shape, dt))

        def sem(name):
            return stack.enter_context(nc.semaphore(name))

        X = sb("X", [P, KT, TOK])
        h_at = nc.sbuf_base
        H = sb("H", [P, KT, TOK])
        H_R = nc.alloc_sbuf_tensor_at("H_R", [P, KT, TOK], F32R, offset=h_at)
        w_at = nc.sbuf_base
        W = sb("W", [P, RING, CHUNK])
        W_R = nc.alloc_sbuf_tensor_at("W_R", [P, RING, CHUNK], F32R, offset=w_at)
        t_at = nc.sbuf_base
        T = sb("T", [P, NT, TOK])
        T_R = nc.alloc_sbuf_tensor_at("T_R", [P, NT, TOK], F32R, offset=t_at)
        onehot = nc.alloc_sbuf_tensor_at("onehot", [P, 2, TOK], F32R, offset=t_at + 4 * TOK * T_ONEHOT)
        C = sb("C", [P, NCONST])
        rows_a = [T[0:RA_N, T_ROWS, P * l:P * l + P] for l in range(DEPTH)]
        rows_b = [T[0:RB_N, T_ROWS, P * (2 + l):P * (3 + l)] for l in range(DEPTH)]
        col_a = [sb(f"col_a{l}", [P, RA_N]) for l in range(DEPTH)]
        col_b = [sb(f"col_b{l}", [P, RB_N]) for l in range(DEPTH)]
        wab = [sb(f"wab{l}", [P, KT, 16]) for l in range(DEPTH)]
        alog = [sb(f"alog{l}", [P, 8]) for l in range(DEPTH)]
        dtb = [sb(f"dtb{l}", [P, 8]) for l in range(DEPTH)]
        rows_c = T[0:2 * KT, T_ROWS + 1, 256:384]
        rpb = T[0:NA_HEADS * 15, T_ROWS + 1, 0:P * DEPTH].rearrange("r (l c) -> r l c", l=DEPTH)
        wrt = sb("wrt", [P, KT, N_EXPERTS])
        rbias = sb("rbias", [P, N_EXPERTS])
        silu_c = sb("silu_c", [P, KT, 2])
        silu_r = sb("silu_r", [P, KT, 4], F32R)
        mods = [sb(f"mod{l}", [P, 48, 2]) for l in range(DEPTH)]
        gain = sb("gain", [P, KT, 2])
        ab = sb("ab", [P, NTT, 2, 8])
        gdec = sb("gdec", [P, 2, NTT, 4])
        tmp_g = sb("tmp_g", [P, 3, NTT, 8])
        beta = sb("beta", [P, NTT, 8])
        negG = sb("negG", [P, 2, NTT, 4])
        ea = sb("ea", [P, 8])
        zero_row = sb("zero_row", [1, P // 2])
        glast = sb("glast", [P, 2, 4])
        mx = sb("mx", [P, 4, 4])
        rs = T[:, T_RS, :].rearrange("p (i t n) -> p i t n", i=8, t=NTT)
        rcmp = T[:, T_RCMP, 0:256].rearrange("p (t g i j) -> p t g i j", t=NTT, g=N_GROUPS, i=4)
        combT = T[0:N_EXPERTS, F_COMBT, :]
        pair = T_R[:, T_PAIR, 0:256].rearrange("p (t n w) -> p t n w", t=NTT, n=N_EXPERTS)
        slot_comb = sb("slot_comb", [P, N_EXPERTS])
        slot_tok = sb("slot_tok", [P, N_EXPERTS], U32)
        tok_slot = sb("tok_slot", [P, 2, NTT], U32)
        flag = sb("flag", [P, 1], U32)

        bank = [stack.enter_context(nc.psum_tensor(f"bank{i}", [P, 512], F32)) for i in range(8)]

        def cm(name):
            return C[:, CA[name]]

        def cm4(name):
            return C[:, CA[name]].unsqueeze(1).broadcast_to([P, 4, P])

        def v4(ap):
            return ap.rearrange("p (h c) -> p h c", h=4)

        s_chunk = [sem(f"s_chunk{i}") for i in range(RING)]
        s_tile = [sem(f"s_tile{b}") for b in range(2)]
        s_taken = [sem(f"s_taken{b}") for b in range(2)]
        s_const, s_first, s_xin, s_rows, s_small, s_rpb, s_rpb_out, s_out = (sem(n) for n in (
            "s_const", "s_first", "s_xin", "s_rows", "s_small", "s_rpb", "s_rpb_out", "s_out"))
        s_turned, s_store = sem("s_turned"), sem("s_store")
        s_hi, s_lo = sem("s_hi"), sem("s_lo")
        s_ada_pe, s_ada_dve, s_masks, s_mod1 = (sem(n) for n in ("s_ada_pe", "s_ada_dve", "s_masks", "s_mod1"))
        chain = {n: sem(f"s_{n}_chain") for n in ("dve", "act", "pool")}
        links = {n: 0 for n in chain}

        def link(eng, name, ins):
            links[name] += 1
            ins.then_inc(chain[name], 1)
            eng.wait_ge(chain[name], links[name])

        def line(name, names):
            return Line(sem(name), names)

        shared = {}

        def on(name, names):
            s_, before = shared[name] if name in shared else (sem(name), 0)
            shared[name] = s_, before + len(names)
            return Line(s_, names, before)

        setup_pe = line("setup_pe", ["c"] + [f"x{i}" for i in range(8)] + [f"rows{i}" for i in range(2 * DEPTH)])
        setup_dve = line("setup_dve", ["rpbzero", "silu_r", "rpb"] + [f"x{i}" for i in range(8)] + [f"rows{i}" for i in range(2 * DEPTH)])
        setup_act = line("setup_act", ["silu_c", "silu_hi"])

        def names_na(l):
            return [(qt, h) for qt in range(2 if l == DEPTH - 1 else 0, NTT) for h in range(NA_HEADS)]

        def need_o(l, tt):
            return tt >= 2 or l < DEPTH - 1

        CH = [[(j, d, (j if d == 0 else (1, 0, 3, 2)[j])) for j in range(4) for d in range(2)] for _ in range(1)][0]

        def dn_pe_names(l):
            return {d: [n for j, dd, tt in CH if dd == d for n in (
                [(j, "gB"), (j, "KK")] + ([(j, "QK")] if need_o(l, tt) else []) + [(j, "L")]
                + [(j, f"{w}{k}") for k in range(1, LEVELS) for w in (("Y", "Z", "ZT") if k < LEVELS - 1 else ("Y", "ZT"))]
                + ([(j, "KS")] if j else []) + [(j, "VN")] + ([(j, "O")] if need_o(l, tt) else [])
                + ([(j, "dS")] if j < 3 else []))] for d in range(2)}

        def dn_dve_names(l):
            return {d: [n for j, dd, tt in CH if dd == d for n in (
                [(j, "M"), (j, "LT"), (j, "XT0"), (j, "X0")] + ([(j, "AT")] if need_o(l, tt) else [])
                + [(j, f"{w}{k}") for k in range(1, LEVELS) for w in (("Y", "X", "XT") if k < LEVELS - 1 else ("Y", "XT"))]
                + ([(j, "R")] if j else []) + [(j, "vn")] + ([(j, "O")] if need_o(l, tt) else [])
                + ([(j, "S")] if j < 3 else []))] for d in range(2)}

        def by_pool(w, k):
            return w == "H" or w == "h" and k % 3 != 2

        ev = []
        for l in range(DEPTH):
            e = {}
            n = f"L{l}"
            t0 = 256 if l == DEPTH - 1 else 0
            e["t0"] = t0
            e["modr"] = on("modrow_pe", ["mod"])
            for w in ("n1", "n2"):
                e[w + "sq"] = on("norm_sq_act", list(range(KT)))
                e[w + "ms"] = on("norm_ms_pe", ["ms"])
                e[w + "rt"] = on("norm_rt_act", ["rt"])
                e[w + "x"] = on("norm_x_dve", list(range(KT)))
                e[w + "h"] = on("norm_h_act", list(range(KT)))
            parts = [(w, k) for w, n_ in (("h", 8), ("na", 4), ("H", 8), ("dn", 4), ("sc", 4), ("mg", 8)) for k in range(n_)]
            e["hi"], e["hip"] = (on(n_, [p_ for p_ in parts if by_pool(*p_) == w]) for n_, w in (("hi_act", False), ("hi_pool", True)))
            e["lo"] = on("lo_dve", parts)
            e["ab"] = on("ab_pe", ["ab", "G"])
            e["abd"] = on("ab_dve", ["ab", "x", "beta_g", "negG"])
            e["aba"] = on("ab_act", ["ea", "e", "ln", "sig"])
            e["sq"] = on("sq_act", list(range(20)))
            e["st"] = on("st_pe", list(range(20)))
            e["rt"] = on("rt_act", list(range(20)))
            e["nrm"] = on("nrm_dve", list(range(20)))
            e["conv"] = on("conv_dve", list(range(8)))
            e["convp"] = on("conv_pool", list(range(8, 12)))
            e["silu"] = on("silu_act", list(range(12)) + ["z"])
            e["rot"] = on("rot_pe", list(range(8)))
            e["sc"] = on("sc_dve", ["sc"])
            e["tp"] = on("tp_pe", list(range(12)))
            e["tpc"] = on("tp_act", list(range(12)))
            e["bias_ld"] = sem(n + "bias_ld")
            e["biasf"] = on("bias_pe", list(range(6)))
            e["biasm"] = line(n + "bias_dve", list(range(6)))
            nn = len(names_na(l))
            e["aS"] = on("aS_pe", list(range(nn)))
            e["aM"] = on("aM_dve", list(range(nn)))
            e["aE"] = on("aE_act", list(range(nn)))
            e["aP"] = on("aP_dve", list(range(nn)))
            e["aT"] = on("aT_pe", list(range(nn)))
            e["aC"] = on("aC_act", list(range(nn)))
            e["aO"] = line(n + "aO_pe", list(range(nn)))
            e["aD"] = line(n + "aD_dve", list(range(nn // 2)))
            pn, dn = dn_pe_names(l), dn_dve_names(l)
            e["dp"] = [line(n + f"dn_pe{d}", pn[d]) for d in range(2)]
            e["dd"] = [line(n + f"dn_dve{d}", dn[d]) for d in range(2)]
            e["da"] = [on(f"dn_act{d}", [(j, w) for j in range(4) for w in ("eg", "DT")]) for d in range(2)]
            e["dg"] = [on(f"dn_pool{d}", [(j, w) for j, dd, tt in CH if dd == d for w in ("kgl", "qg", "gl", "kg") if w != "qg" or need_o(l, tt)])
                       for d in range(2)]
            e["mgd"] = on("merge_dve", list(range(TILES_MERGE // 2)))
            e["rp"] = on("router_pe", ["logits", "scores", "cnt", "flag"])
            e["hr"] = line(n + "hrow_pe", list(range(2 * NTT)))
            e["hrc"] = line(n + "hrow_act", list(range(2 * NTT)))
            e["hrd"] = sem(n + "hrow_dma")
            e["ra"] = on("router_act", ["sig"])
            e["rd"] = on("router_dve", ["comb", "rk", "ov", "flag", "slots", "back"])
            e["oh"] = on("onehot_dve", list(range(N_EXPERTS)))
            e["ohp"] = line(n + "onehot_pe", list(range(N_EXPERTS)))
            e["xg"] = [sem(n + f"xg{i}") for i in range(2)]
            e["xt"] = sem(n + "xt_pe")
            e["xca"], e["xcd"] = sem(n + "xc_act"), sem(n + "xc_dve")
            e["ht"], e["hc"], e["hcd"] = sem(n + "ht_pe"), sem(n + "hc_act"), sem(n + "hc_dve")
            e["yst"] = [sem(n + f"yst{i}") for i in range(2)]
            e["bg"] = [sem(f"back{i}") for i in range(NTT)] if l == 0 else ev[0]["bg"]
            e["bs"] = line(n + "back_dve", list(range(2 * NTT)))
            e["bt"] = line(n + "back_pe", list(range(2 * NTT)))
            e["bx"] = line(n + "back_x_dve", list(range(2 * NTT)))
            e["f_chunk"] = [sem(n + f"f_chunk{i}") for i in range(RING)]
            for w in ("f_tile", "f_taken", "f_cb"):
                e[w] = [sem(n + w + str(i)) for i in range(2)]
            e["f_hid"], e["f_comb"], e["f_store"] = sem(n + "f_hid"), sem(n + "f_comb"), sem(n + "f_store")
            e["x2"] = line(n + "x2_dve", ["x2"])
            ev.append(e)

        block = stack.enter_context(nc.Block())

        def chunk_wait(eng, C0, i, per, s):
            assert per % RING == 0 or isinstance(i, int)
            if isinstance(i, int):
                q = C0 + per * i + s
                eng.wait_ge(s_chunk[q % RING], 16 * (q // RING + 1))
            else:
                q = C0 + s
                eng.wait_ge(s_chunk[q % RING], i * (16 * per // RING) + 16 * (q // RING + 1))

        def hi_view(C_, k, t_hi, n_hi):
            b_ = t_hi + 4 * (C_ % n_hi)
            return T_R[:, b_:b_ + 4, :].rearrange("p a b -> p (a b)").rearrange("p (k n) -> p k n", k=k)

        def lo_view(C_, k):
            return W_R[:, C_ % RING, :].rearrange("p (k n) -> p k n", k=k)

        def flat(ap):
            return ap.rearrange("p a b -> p (a b)")

        def piece(Q, l, w):
            kind, v, at = PIECES[l][w]
            half = v % 2
            if kind == "m":
                k = 4 if v < SPLIT_MERGE and v % 6 < 2 else KT
                part = (slice(0, P), slice(0, k), slice(CHUNK // k // 2 * half, CHUNK // k // 2 * (half + 1)))
                rows_ = k
            else:
                k, rows_ = KT, KT // 2
                part = (slice(0, P), slice(rows_ * half, rows_ * (half + 1)), slice(0, CHUNK // KT))
            hi = flat(T_R[:, T_HI_HALF[w % 3]:T_HI_HALF[w % 3] + 2, :]).rearrange("p (k n) -> p k n", k=rows_)
            return w_view(Q + at, k)[part], hi, lo_view(Q + at, k)[part]

        def ada_row(c_):
            at = CA["lev00"].start + 256 * (c_ // 4)
            return C[32 * (c_ % 4):32 * (c_ % 4) + 4, at:at + 256]

        def three(hi, lo, x_hi, x_lo, n):
            return [p_ for k in range(n) for p_ in ((hi(k), x_hi(k)), (lo(k), x_hi(k)), (hi(k), x_lo(k)))]

        def w_view(C_, k):
            return W[:, C_ % RING, :].rearrange("p (k n) -> p k n", k=k)

        @block.sync
        def _(sp):
            def load(C_, src, k):
                sp.dma_start(w_view(C_, k), src).then_inc(s_chunk[C_ % RING], 16)

            def room(C_):
                if C_ >= RING:
                    kind, u = USES[C_ - RING]
                    if kind == "t":
                        sp.wait_ge(s_tile[u % 2], u // 2 + 1)
                    else:
                        sp.wait_ge(s_ada_pe, 2 * u + 2)

            for l in range(DEPTH):
                base = Q_LAYER[l]
                if l == 0:
                    wa = w_ada[0].rearrange("(k p) n -> p k n", p=P)
                    for s in range(RING):
                        room(base + s)
                        load(base + s, wa[:, :, 256 * s:256 * (s + 1)], KT)
                    with sp.Fori(1, CHUNKS_ADA // RING) as i:
                        for s in range(RING):
                            u = s
                            sp.wait_ge(s_tile[u % 2], i * (RING // 2) + (u // 2 + 1 - RING // 2))
                            load(base + s, wa[:, :, bass.ds(i * (256 * RING) + 256 * s, 256)], KT)
                q = base + (CHUNKS_ADA if l == 0 else 0)
                wi = w_in[l].rearrange("(k p) n -> p k n", p=P)
                cols = ([COL_NA + 256 * i for i in range(6)] + [COL_DN + 256 * i for i in range(6)]
                        + [COL_SC + 256 * i for i in range(6)] + [COL_Z + 256 * i for i in range(2)])
                for c0 in cols:
                    room(q)
                    load(q, wi[:, :, c0:c0 + 256], KT)
                    q += 1
                for i in range(N_MO):
                    r_, s_ = divmod(i, 3)
                    hf, b = divmod(r_, 3)
                    room(q)
                    if i >= CHUNKS_MERGE:
                        i_ = i - CHUNKS_MERGE
                        load(q, w_out[l].rearrange("(k p) n -> p k n", p=P)[:, :, 256 * i_:256 * (i_ + 1)], KT)
                    elif s_ == 0:
                        wb = (w_branch_na, w_branch_dn, w_branch_sc)[b]
                        load(q, wb[l].rearrange("(k p) n -> p k n", p=P)[:, :, 512 * hf:512 * (hf + 1)], 4)
                    else:
                        c0 = COL_GATE + D_MODEL * b + 512 * hf + 256 * (s_ - 1)
                        load(q, wi[:, :, c0:c0 + 256], KT)
                    q += 1
                    for c_ in ADA_BEHIND[i] if l == 0 else []:
                        room(q)
                        load(q, w_ada[1].rearrange("(k p) n -> p k n", p=P)[:, :, 256 * c_:256 * (c_ + 1)], KT)
                        q += 1

                def expert(e, s, q):
                    wg, wu, wd = (m[l, bass.ds(e, 1)] if not isinstance(e, int) else m[l, e:e + 1]
                                  for m in (moe_w_gate, moe_w_up, moe_w_down))
                    if s < 4:
                        src = (wg, wu)[s // 2].rearrange("e (k p) n -> p (e k) n", p=P)[:, 4 * (s % 2):4 * (s % 2) + 4, :]
                    else:
                        src = wd.rearrange("e (k p) n -> p (e k) n", p=P)[:, :, 512 * (s - 4):512 * (s - 3)]
                    load(q, src, 4)

                for s in range(6):
                    room(q + s)
                    expert(0, s, q + s)
                with sp.Fori(1, N_EXPERTS) as e:
                    for s in range(6):
                        u = USES[q + s][1]
                        sp.wait_ge(s_tile[u % 2], e * 2 + (u // 2 - 1))
                        expert(e, s, q + s)

                E = ev[l]
                sp.wait_ge(E["rd"].sem, E["rd"]["flag"])
                with sp.If(sp.value_load(flag[0:1, 0:1], min_val=0, max_val=1) > 0):
                    for s in range(6):
                        u = USES[q + 6 * (N_EXPERTS - 1) + s][1]
                        sp.wait_ge(s_tile[u % 2], u // 2 + 1)

                    def f_load(x_, s):
                        wg, wu, wd = (m[l, bass.ds(x_, 1)] if not isinstance(x_, int) else m[l, x_:x_ + 1]
                                      for m in (moe_w_gate, moe_w_up, moe_w_down))
                        if s < 4:
                            src = (wg, wu)[s % 2].rearrange("e (k p) n -> p (e k) n", p=P)[:, :, 256 * (s // 2):256 * (s // 2 + 1)]
                        else:
                            src = wd.rearrange("e (k p) n -> p (e k) n", p=P)[:, :, 512 * (s - 4):512 * (s - 3)]
                        sp.dma_start(w_view(s, KT if s < 4 else 4), src).then_inc(E["f_chunk"][s], 16)
                    for s in range(6):
                        f_load(0, s)
                    with sp.Fori(1, N_EXPERTS) as x_:
                        for s in range(6):
                            sp.wait_ge(E["f_tile"][1], x_ * 8 + ((2, 4, 6, 8, 12, 16)[s] // 2 - 8))
                            f_load(x_, s)
                    sp.wait_ge(E["f_tile"][1], 8 * N_EXPERTS)

        @block.gpsimd
        def _(pool):
            gp = nc.gpsimd
            pool.wait_ge(setup_dve.sem, setup_dve["rpbzero"])
            for l in range(DEPTH):
                pool.dma_start(rpb[:, l, 48:79], na_rpb[l].rearrange("h r c -> (h r) c")).then_inc(s_rpb, 16)
            pool.dma_start(C[:, P:], const[:, P:]).then_inc(s_const, 16)
            for l in range(DEPTH):
                for r0, n, src in ((RA_B, 48, b_ada[l]), (RA_MIX, 8, norm_mix_g[l]), (RA_FFN, 8, norm_ffn_g[l])):
                    pool.dma_start(rows_a[l][r0:r0 + n, :], src.rearrange("(n p) -> n p", p=P)).then_inc(s_rows, 16)
                pool.dma_start(rows_b[l][RB_CONV:RB_SC, :], dn_conv_w[l].rearrange("t (n p) -> (t n) p", p=P)).then_inc(s_rows, 16)
                pool.dma_start(rows_b[l][RB_SC:RB_OUT, :], sc_conv_w[l].rearrange("t (n p) -> (t n) p", p=P)).then_inc(s_rows, 16)
                pool.dma_start(rows_b[l][RB_OUT:RB_QG, :], dn_out_norm_g[l].rearrange("(n p) -> n p", p=P)).then_inc(s_rows, 16)
                for r, g in ((RB_QG, na_q_norm_g), (RB_KG, na_k_norm_g)):
                    for i in range(2):
                        pool.dma_start(rows_b[l][r:r + 1, 64 * i:64 * i + 64], g[l:l + 1]).then_inc(s_rows, 16)
                pool.dma_start(wab[l][:], w_in[l].rearrange("(k p) n -> p k n", p=P)[:, :, COL_AB:COL_AB + 16]).then_inc(s_small, 16)
                pool.dma_start(alog[l][:], dn_a_log[l].rearrange("(a d) h -> a (d h)", a=1).broadcast_to([P, 8])).then_inc(s_small, 16)
                pool.dma_start(dtb[l][:], dn_dt_bias[l].rearrange("(a d) h -> a (d h)", a=1).broadcast_to([P, 8])).then_inc(s_small, 16)
            pool.dma_start(wrt[:], w_router.rearrange("(k p) n -> p k n", p=P)).then_inc(s_small, 16)
            pool.dma_start(rbias[:], router_bias.rearrange("(a n) -> a n", a=1).broadcast_to([P, N_EXPERTS])).then_inc(s_small, 16)
            pool.wait_ge(setup_dve.sem, setup_dve["rpb"])
            for l in range(DEPTH):
                pool.dma_start(rpb_pad[l], rpb[:, l, :]).then_inc(s_rpb_out, 16)
            pool.wait_ge(s_rpb_out, 16 * DEPTH)
            for l in range(DEPTH):
                e = ev[l]
                for k in [k for k in range(KT) if by_pool("h", k)]:
                    pool.wait_ge(e["n1h"].sem, e["n1h"][k])
                    gp.tensor_copy(T_R[:, T_H_HI + k, :], H[:, k, :]).then_inc(e["hip"].next(("h", k)), 1)
                if l:
                    pool.wait_ge(ev[l - 1]["x2"].sem, 1)
                    pool.wait_ge(e["modr"].sem, e["modr"]["mod"])
                    m_ = slice(CA["lev00"].start, CA["lev61"].stop)
                    pool.dma_start(C[:, m_], const[:, m_]).then_inc(s_masks, 16)
                bview = T[:, T_BIAS:T_BIAS + 6, :].rearrange("p a b -> p (a b)").rearrange("p (h j c) -> p h j c", h=8, j=6)
                for qr in range(2):
                    for h in range(NA_HEADS):
                        src = bass.AP(rpb_pad.tensor, l * 120 * P + (h * 15 + 5 - qr) * P, [[1, 64], [P, 6], [1, 64]])
                        pool.dma_start(bview[64 * qr:64 * qr + 64, h], src).then_inc(e["bias_ld"], 16)
                u = U_LAYER[l] + (TILES_ADA if l == 0 else 0) + 24
                for b in range(2):
                    pool.wait_ge(s_taken[b], u // 2 + 1)
                for i in range(8, 12):
                    src, acc, tmp = T[:, T_DQ + i, :], T[:, T_CONV + 1, :], T[:, T_CONV + 2, :]
                    tap = lambda t_, ap: col_b[l][:, RB_CONV + 12 * t_ + i:RB_CONV + 12 * t_ + i + 1].broadcast_to([P, ap.shape[1]])
                    link(pool, "pool", gp.tensor_tensor(acc, src, tap(2, src), ALU.mult))
                    for t_ in (0, 1, 3, 4):
                        link(pool, "pool", gp.tensor_tensor(tmp, src, tap(t_, src), ALU.mult))
                        s_ = t_ - 2
                        o_ = acc.rearrange("p (s n) -> p s n", s=2)[:, :, max(0, -s_):256 - max(0, s_)]
                        i_ = tmp.rearrange("p (s n) -> p s n", s=2)[:, :, max(0, s_):256 - max(0, -s_)]
                        link(pool, "pool", gp.tensor_tensor(o_, o_, i_, ALU.add))
                    gp.tensor_copy(src, acc).then_inc(e["convp"].next(i), 1)
                    pool.wait_ge(e["convp"].sem, e["convp"][i])
                for j, d, tt in CH:
                    dd, da, dp, dg = e["dd"][d], e["da"][d], e["dp"][d], e["dg"][d]
                    wt = [T[:, T_WORK[d][i], :] for i in range(8)]
                    DT, EG, QG, KGL = wt[0], wt[1], wt[6], wt[7]
                    last = 127 if d == 0 else 0
                    ts_ = slice(P * tt, P * tt + P)
                    if j:
                        pool.wait_ge(dp.sem, dp[(j - 1, "dS")])
                    if j == 0:
                        pool.wait_ge(e["tpc"].sem, e["tpc"][11])
                        pool.wait_ge(e["nrm"].sem, e["nrm"][15])
                        pool.wait_ge(e["aD"].sem, len(names_na(l)) // 2)
                    pool.wait_ge(da.sem, da[(j, "DT")])
                    kt = T[:, T_KTOK_DN + tt, :]
                    gp.tensor_tensor(v4(KGL), v4(kt), v4(DT)[:, :, last:last + 1].broadcast_to([P, 4, P]),
                                     ALU.mult).then_inc(dg.next((j, "kgl")), 1)
                    if need_o(l, tt):
                        gp.tensor_tensor(v4(QG), T[:, T_DQ:T_DQ + 4, ts_], v4(EG), ALU.mult).then_inc(dg.next((j, "qg")), 1)
                    if j:
                        pool.wait_ge(dd.sem, dd[(j - 1, "S")])
                    gp.tensor_copy(glast[:, d, :], v4(EG)[:, :, last]).then_inc(dg.next((j, "gl")), 1)
                    pool.wait_ge(dg.sem, dg[(j, "gl")])
                    gp.tensor_tensor(v4(EG), T[:, T_DK:T_DK + 4, ts_], v4(EG), ALU.mult).then_inc(dg.next((j, "kg")), 1)
                for d in range(2):
                    pool.wait_ge(e["dd"][d].sem, len(e["dd"][d].names))
                for k in range(KT):
                    gp.tensor_copy(T_R[:, T_HM_HI + k, e["t0"]:], H[:, k, e["t0"]:]).then_inc(e["hip"].next(("H", k)), 1)
                for tt in range(e["t0"] // P, NTT):
                    pool.wait_ge(e["hrc"].sem, 2 * tt + 2 - e["t0"] // 64)
                    pool.dma_start(h_rows[l][P * tt - e["t0"]:P * tt - e["t0"] + P, :], T[:, T_HROW + 2 * tt:T_HROW + 2 * tt + 2, :].rearrange("p a b -> p (a b)"))\
                        .then_inc(e["hrd"], 16)
                for i in range(2):
                    pool.dma_start(y_rows[l][ZERO_ROW:ZERO_ROW + 1, 512 * i:512 * i + 512].rearrange("a (r n) -> a r n", n=P // 2),
                                   zero_row[:].unsqueeze(1).broadcast_to([1, 8, P // 2])).then_inc(e["yst"][i], 16)
                pool.wait_ge(e["hrd"], 16 * (NTT - e["t0"] // P))
                pool.wait_ge(e["rd"].sem, e["rd"]["slots"])
                UE = U_EXPERTS[l]

                def gather_x(x_):
                    pool.indirect_dma_start(T[:, T_XROW + 2 * (x_ % 2):T_XROW + 2 * (x_ % 2) + 2, :].rearrange("p a b -> p (a b)"), None,
                                            h_rows[l], bass.IndirectOffsetOnAxis(ap=slot_tok[:, x_:x_ + 1], axis=0)).then_inc(e["xg"][x_ % 2], 16)
                gather_x(0)
                gather_x(1)
                for x_ in range(N_EXPERTS):
                    if x_ + 2 < N_EXPERTS:
                        pool.wait_ge(e["xt"], 2 * (x_ + 1))
                        gather_x(x_ + 2)
                    u = UE + TILES_EXP * x_ + 2
                    pool.wait_ge(s_taken[0], u // 2 + 2)
                    pool.wait_ge(s_taken[1], u // 2 + 2)
                    pool.dma_start(y_rows[l][CAPACITY * x_:CAPACITY * (x_ + 1), :],
                                   T[:, T_Y + 2 * (x_ % 2):T_Y + 2 * (x_ % 2) + 2, :].rearrange("p a b -> p (a b)")).then_inc(e["yst"][x_ % 2], 16)
                for i in range(2):
                    pool.wait_ge(e["yst"][i], 16 * (N_EXPERTS // 2 + 1))
                for n_, tt in enumerate(range(e["t0"] // P, NTT)):
                    for i in range(2):
                        t_ = T_GATHER + 4 * n_ + 2 * i
                        pool.indirect_dma_start(T[:, t_:t_ + 2, :].rearrange("p a b -> p (a b)"), None, y_rows[l],
                                                bass.IndirectOffsetOnAxis(ap=tok_slot[:, i, tt:tt + 1], axis=0)).then_inc(e["bg"][n_], 16)

                pool.wait_ge(e["rd"].sem, e["rd"]["flag"])
                with pool.If(pool.value_load(flag[0:1, 0:1], min_val=0, max_val=1) > 0):
                    pool.wait_ge(e["f_comb"], 2)
                    pool.dma_start(comb_rows[l, :, e["t0"]:], combT[:, e["t0"]:]).then_inc(e["f_store"], 16)
                    pool.wait_ge(e["f_store"], 16)

                    def spread(x_, i):
                        src = comb_rows[l, bass.ds(x_, 1)] if not isinstance(x_, int) else comb_rows[l, x_:x_ + 1]
                        pool.dma_start(T[:, F_CB + i, e["t0"]:], src[:, e["t0"]:].broadcast_to([P, TOK - e["t0"]])).then_inc(e["f_cb"][i], 16)
                    for i in range(2):
                        spread(i, i)
                    with pool.Fori(1, N_EXPERTS // 2) as p_:
                        for i in range(2):
                            pool.wait_ge(e["f_hid"], p_ * 8 + 4 * i)
                            spread(p_ * 2 + i, i)

        @block.tensor
        def _(pe):
            mm = nc.tensor.matmul

            def tp(out_, in_):
                k = in_.shape[0]
                return nc.tensor.transpose(out_, in_, C[0:k, CA["ident"]][:, 0:k])

            def tile(U0, per, i, j, pairs, before=None):
                u = U0 + j
                b = u % 2
                if isinstance(i, int):
                    pe.wait_ge(s_taken[b], (u + per * i) // 2 + 1)
                else:
                    pe.wait_ge(s_taken[b], i * (per // 2) + (u // 2 + 1))
                n = len(pairs)
                for k, (a_, r_) in enumerate(pairs):
                    if before and k % 3 == 0:
                        before(k // 3)
                    w_ = r_.shape[1]
                    last = mm(bank[b][:, TOK - w_:TOK], a_, r_, start=(k == 0), stop=(k == n - 1))
                last.then_inc(s_tile[b], 1)

            pe.wait_ge(s_first, 16 * 3)
            tp(bank[0][:, 0:2 * KT], rows_c).then_inc(setup_pe.next("c"), 1)
            pe.wait_ge(s_xin, 16 * NTT)
            for k in range(KT):
                if k >= 6:
                    pe.wait_ge(setup_dve.sem, setup_dve[f"x{k - 6}"])
                for i in range(NTT):
                    m_ = tp(bank[2 + k % 6][:, P * i:P * i + P], T[:, 2 * i + k // 4, P * (k % 4):P * (k % 4) + P])
                m_.then_inc(setup_pe.next(f"x{k}"), 1)
            pe.wait_ge(setup_dve.sem, setup_dve["silu_r"])

            for l in range(DEPTH):
                e = ev[l]
                t0 = e["t0"]
                q = Q_LAYER[l]
                U = U_LAYER[l]
                lat, full = slice(t0, TOK), slice(0, TOK)
                mod = mods[l]

                if l:
                    pe.wait_ge(ev[l - 1]["x2"].sem, 1)
                K = K_LAYER[l]
                if l == 0:
                    with pe.Fori(0, CHUNKS_ADA // RING) as i:
                        for s in range(RING):
                            pe.wait_ge(s_lo, i * RING + (K + s + 1))
                            b = (U + s) % 2
                            pe.wait_ge(s_taken[b], i * (RING // 2) + ((U + s) // 2 + 1))
                            for k in range(KT):
                                mm(bank[b][0:4, 0:256], silu_r[:, k, :], hi_view(q + s, KT, T_HI_ADA, N_HI_ADA)[:, k, :], start=(k == 0), stop=False)
                                last = mm(bank[b][0:4, 0:256], silu_r[:, k, :], lo_view(q + s, KT)[:, k, :], start=False, stop=(k == KT - 1))
                            last.then_inc(s_tile[b], 1)
                    K += SPLIT_ADA
                    q += CHUNKS_ADA
                    U += TILES_ADA
                if l == 0:
                    pe.wait_ge(s_rows, 16 * 10 * DEPTH)
                    pe.wait_ge(setup_dve.sem, setup_dve["x7"])
                    for i in range(2 * DEPTH):
                        rows_, n = ((rows_a, RA_N), (rows_b, RB_N))[i % 2]
                        tp(bank[4 + i][:, 0:n], rows_[i // 2]).then_inc(setup_pe.next(f"rows{i}"), 1)
                    pe.wait_ge(s_const, 16)
                    for b in range(2):
                        pe.wait_ge(s_taken[b], U // 2 + 1)
                    for i in range(48):
                        last = tp(bank[2][:, 4 * i:4 * i + 4], T[0:4, T_MODROW + i // 4, P * (i % 4):P * (i % 4) + P])
                    last.then_inc(e["modr"].next("mod"), 1)

                def mean_square(w, bk, cols):
                    for k in range(KT):
                        pe.wait_ge(e[w + "sq"].sem, e[w + "sq"][k])
                        last = mm(bk[:, cols], cm("ones"), T[:, k, cols], start=(k == 0), stop=(k == KT - 1))
                    last.then_inc(e[w + "ms"].next("ms"), 1)

                mean_square("n1", bank[3], full)
                with pe.Fori(0, 2) as i:
                    for s in range(6):
                        pe.wait_ge(s_lo, i * 6 + (K + s + 1))
                        cols = lat if s < 2 else full
                        hi_, lo_ = hi_view(q + s, KT, T_HI_IN, N_HI_IN), lo_view(q + s, KT)
                        for m in range(2):
                            tile(U, 12, i, 2 * s + m, three(lambda k: hi_[:, k, P * m:P * m + P], lambda k: lo_[:, k, P * m:P * m + P],
                                                            lambda k: T_R[:, T_H_HI + k, cols], lambda k: T_R[:, T_H_LO + k, cols], KT),
                                 lambda k: pe.wait_ge(e["lo"].sem, e["lo"][("h", k)]) if s + m == 0 else None)
                q += 12
                K += SPLIT_IN
                U += 24
                pe.wait_ge(e["bias_ld"], 16 * 16)
                for i in range(6):
                    mm(bank[(4, 5, 6, 7, 2, 3)[i]][:, :], cm("flip"), T[:, T_BIAS + i, :], start=True, stop=True).then_inc(e["biasf"].next(i), 1)
                pe.wait_ge(s_small, 16 * (3 * DEPTH + 2))
                pe.wait_ge(e["biasm"].sem, e["biasm"][5])
                for tt in range(NTT):
                    for k in range(KT):
                        last = mm(bank[3][:, 16 * tt:16 * tt + 16], H[:, k, P * tt:P * tt + P], wab[l][:, k, :],
                                  start=(k == 0), stop=(k == KT - 1))
                last.then_inc(e["ab"].next("ab"), 1)

                def stat(n_, w_, cols):
                    pe.wait_ge(e["sq"].sem, e["sq"][n_])
                    if n_ >= 2:
                        pe.wait_ge(e["rt"].sem, e["rt"][n_ - 2])
                    mm(bank[4 + n_ % 2][:, cols], cm(w_), T[:, T_SQ + n_ % 2, cols], start=True, stop=True)\
                        .then_inc(e["st"].next(n_), 1)

                for s in range(8):
                    chunk_wait(pe, q, 0, 0, s)
                    for m in range(2):
                        j = 2 * s + m
                        tile(U, 0, 0, j, [(w_view(q + s, KT)[:, k, P * m:P * m + P], H[:, k, lat]) for k in range(KT)])
                        isq = j % 8 < 4
                        if j == 2:
                            pe.wait_ge(e["abd"].sem, e["abd"]["beta_g"])
                            for d in range(2):
                                g_ = mm(bank[3][:, 64 + 16 * d:80 + 16 * d], cm(f"tri{d}"), gdec[:, d].rearrange("p t h -> p (t h)"),
                                        start=True, stop=True)
                            g_.then_inc(e["ab"].next("G"), 1)
                        if j == 0:
                            pe.wait_ge(e["biasm"].sem, 6)
                        stat(j, "ones64" if j < 8 else "ones", lat if isq else full)
                        if j >= 8:
                            r_ = j - 8
                            if r_ >= 2:
                                pe.wait_ge(e["nrm"].sem, e["nrm"][j - 2])
                            mm(bank[6 + r_ % 2][:, 0:256], cm("rot"), T[:, T_DQ + r_, 256:512], start=True, stop=True)\
                                .then_inc(e["rot"].next(r_), 1)
                q += 8
                U += 16

                for n_ in range(12):
                    what, tt = divmod(n_, 4)
                    src = (T_NV, T_DK, T_DV)[what]
                    if n_ == 0:
                        pe.wait_ge(e["silu"].sem, e["silu"]["z"])
                        pe.wait_ge(e["nrm"].sem, e["nrm"][15])
                        pe.wait_ge(e["silu"].sem, e["silu"][11])
                    if n_ >= 2:
                        pe.wait_ge(e["tpc"].sem, e["tpc"][n_ - 2])
                    for i in range(4):
                        last = tp(bank[6 + n_ % 2][:, P * i:P * i + P], T[:, src + i, P * tt:P * tt + P])
                    last.then_inc(e["tp"].next(n_), 1)

                items = names_na(l)
                N = len(items)
                pe.wait_ge(e["tpc"].sem, e["tpc"][11])
                pe.wait_ge(e["abd"].sem, e["abd"]["negG"])
                for b in range(2):
                    pe.wait_ge(s_taken[b], U // 2 + 1)
                for n_ in range(N + 3):
                    if n_ < N:
                        qt, h = items[n_]
                        keys = CTX_LEN if qt < 2 else TOK
                        hp = slice(64 * (h % 2), 64 * (h % 2) + 64)
                        if n_ >= 4:
                            pe.wait_ge(e["aE"].sem, e["aE"][n_ - 4])
                        mm(bank[n_ % 4][:, 0:keys], T[hp, T_NQ + h // 2, P * qt:P * qt + P], T[hp, T_NK + h // 2, 0:keys],
                           start=True, stop=True).then_inc(e["aS"].next(n_), 1)
                    if 2 <= n_ <= N + 1:
                        m_ = n_ - 2
                        qt, h = items[m_]
                        nk = 2 if qt < 2 else 4
                        pe.wait_ge(e["aP"].sem, e["aP"][m_])
                        if m_ >= 2:
                            pe.wait_ge(e["aC"].sem, e["aC"][m_ - 2])
                        for i in range(nk):
                            last = tp(bank[4 + m_ % 2][:, P * i:P * i + P], T[:, T_E[m_ % 4], P * i:P * i + P])
                        last.then_inc(e["aT"].next(m_), 1)
                    if n_ >= 3:
                        m_ = n_ - 3
                        qt, h = items[m_]
                        nk = 2 if qt < 2 else 4
                        pe.wait_ge(e["aC"].sem, e["aC"][m_])
                        if m_ >= 4 and m_ % 2 == 0:
                            pe.wait_ge(e["aD"].sem, e["aD"][m_ // 2 - 2])
                        hp = slice(64 * (h % 2), 64 * (h % 2) + 64)
                        for i in range(nk):
                            last = mm(bank[6 + m_ // 2 % 2][hp, 0:P], T[:, T_VTOK + i, 64 * h:64 * h + 64],
                                      T[:, T_PT + m_ % 2, P * i:P * i + P], start=(i == 0), stop=(i == nk - 1))
                        last.then_inc(e["aO"].next(m_), 1)

                pe.wait_ge(e["aD"].sem, N // 2)
                pe.wait_ge(e["abd"].sem, e["abd"]["negG"])
                for j in range(4):
                    grp = [g for g in CH if g[0] == j]

                    def both(f):
                        for g in grp:
                            f(*g)

                    def ctx_of(d):
                        wt = [v4(T[:, T_WORK[d][i], :]) for i in range(8)]
                        return e["dp"][d], e["dd"][d], e["da"][d], e["dg"][d], wt, [v4(bank[2 + 3 * d + i][:, :]) for i in range(3)]

                    def gB(j, d, tt):
                        dp, dd, da, dg, wt, bk = ctx_of(d)
                        ts_ = slice(P * tt, P * tt + P)
                        if j:
                            pe.wait_ge(dd.sem, dd[(j - 1, "S")])
                        for h in range(4):
                            last = mm(bk[0][:, h], gdec[:, d, tt, h:h + 1].broadcast_to([P, P]), cm(f"tri{d}"), start=True, stop=True)
                        last.then_inc(dp.next((j, "gB")), 1)
                        for h in range(4):
                            last = mm(bk[1][:, h], T[:, T_DK + h, ts_], T[:, T_DK + h, ts_], start=True, stop=True)
                        last.then_inc(dp.next((j, "KK")), 1)
                        if need_o(l, tt):
                            for h in range(4):
                                last = mm(bk[2][:, h], T[:, T_DK + h, ts_], T[:, T_DQ + h, ts_], start=True, stop=True)
                            last.then_inc(dp.next((j, "QK")), 1)

                    def L(j, d, tt):
                        dp, dd, da, dg, wt, bk = ctx_of(d)
                        pe.wait_ge(dd.sem, dd[(j, "LT")])
                        for h in range(4):
                            last = tp(bk[1][:, h], wt[2][:, h])
                        last.then_inc(dp.next((j, "L")), 1)

                    def Y(k):
                        def f(j, d, tt):
                            dp, dd, da, dg, wt, bk = ctx_of(d)
                            pe.wait_ge(dd.sem, dd[(j, "X0" if k == 1 else f"X{k - 1}")])
                            pe.wait_ge(da.sem, da[(j, "eg")])
                            for h in range(4):
                                last = mm(bk[0][:, h], wt[2][:, h], wt[3][:, h], start=True, stop=True)
                            last.then_inc(dp.next((j, f"Y{k}")), 1)
                        return f

                    def Z(k):
                        def f(j, d, tt):
                            dp, dd, da, dg, wt, bk = ctx_of(d)
                            pe.wait_ge(dd.sem, dd[(j, f"Y{k}")])
                            if k < LEVELS - 1:
                                for h in range(4):
                                    last = mm(bk[1][:, h], wt[4][:, h], wt[5][:, h], start=True, stop=True)
                                last.then_inc(dp.next((j, f"Z{k}")), 1)
                            for h in range(4):
                                last = mm(bk[2][:, h], wt[5][:, h], wt[4][:, h], start=True, stop=True)
                            last.then_inc(dp.next((j, f"ZT{k}")), 1)
                        return f

                    def KS(j, d, tt):
                        if not j:
                            return
                        dp, dd, da, dg, wt, bk = ctx_of(d)
                        S = v4(T[:, T_STATE + d, :])
                        pe.wait_ge(dg.sem, dg[(j, "kg")])
                        for h in range(4):
                            last = mm(bk[1][:, h], wt[1][:, h], S[:, h], start=True, stop=True)
                        last.then_inc(dp.next((j, "KS")), 1)

                    def VN(j, d, tt):
                        dp, dd, da, dg, wt, bk = ctx_of(d)
                        pe.wait_ge(dd.sem, dd[(j, f"XT{LEVELS - 1}")])
                        R = v4(T[:, T_VTOK_DN + tt, :])
                        if j:
                            pe.wait_ge(dd.sem, dd[(j, "R")])
                            R = wt[5]
                        for h in range(4):
                            last = mm(bk[0][:, h], wt[4][:, h], R[:, h], start=True, stop=True)
                        last.then_inc(dp.next((j, "VN")), 1)

                    def O(j, d, tt):
                        dp, dd, da, dg, wt, bk = ctx_of(d)
                        S = v4(T[:, T_STATE + d, :])
                        pe.wait_ge(dd.sem, dd[(j, "vn")])
                        pe.wait_ge(dg.sem, dg[(j, "kg")])
                        if need_o(l, tt):
                            for h in range(4):
                                if j:
                                    mm(bk[2][:, h], S[:, h], wt[6][:, h], start=True, stop=False)
                                last = mm(bk[2][:, h], wt[3][:, h], wt[0][:, h], start=(j == 0), stop=True)
                            last.then_inc(dp.next((j, "O")), 1)
                        if j < 3:
                            for h in range(4):
                                last = mm(bk[1][:, h], wt[7][:, h], wt[3][:, h], start=True, stop=True)
                            last.then_inc(dp.next((j, "dS")), 1)

                    both(gB)
                    both(L)
                    for k in range(1, LEVELS):
                        both(Y(k))
                        both(Z(k))
                    both(KS)
                    both(VN)
                    both(O)

                pe.wait_ge(e["dd"][0].sem, len(e["dd"][0].names))
                pe.wait_ge(e["dd"][1].sem, len(e["dd"][1].names))
                for i in range(4):
                    pe.wait_ge(e["sq"].sem, e["sq"][16 + i])
                    mm(bank[4 + i][:, lat], cm("ones"), T[:, T_SQ + i, lat], start=True, stop=True).then_inc(e["st"].next(16 + i), 1)
                for w, (kind, v, at) in enumerate(PIECES[l]):
                    if kind == "m" and v == SPLIT_MERGE:
                        pe.wait_ge(e["lo"].sem, e["lo"][("mg", KT - 1)])
                    pe.wait_ge(s_lo, K + w + 1)
                    _, hi_, lo_ = piece(q, l, w)
                    if kind == "a":
                        c_, half = divmod(v, 2)
                        if c_ >= 2 and half == 0:
                            pe.wait_ge(s_ada_dve, c_ - 1)
                        for k in range(KT // 2):
                            mm(bank[2 + c_ % 2][0:4, 0:256], silu_r[:, 4 * half + k, :], hi_[:, k, :], start=(half + k == 0), stop=False)
                            last = mm(bank[2 + c_ % 2][0:4, 0:256], silu_r[:, 4 * half + k, :], lo_[:, k, :], start=False, stop=(half + k == 4))
                        last.then_inc(s_ada_pe, 1)
                        continue
                    if v >= SPLIT_MERGE:
                        tile(U, 0, 0, last_tile_of_piece(v), three(lambda k: hi_[:, k, :], lambda k: lo_[:, k, :],
                                                                   lambda k: T_R[:, T_MG_HI[k], lat], lambda k: T_R[:, T_MERGED + k, lat], KT))
                        continue
                    r_, a = divmod(v, 6)
                    b = r_ % 3
                    if a < 2:
                        pe.wait_ge(e["lo"].sem, e["lo"][(("na", "dn", "sc")[b], 3)])
                        s_hi_, s_lo_ = (T_NA_HI, T_DN_HI, T_SC_HI)[b], (T_NQ, T_Z, T_U)[b]
                        for m in range(2):
                            tile(U, 0, 0, 8 * r_ + 2 * a + m, three(lambda k: hi_[:, k, P * m:P * m + P], lambda k: lo_[:, k, P * m:P * m + P],
                                                                    lambda k: T_R[:, s_hi_[k], lat], lambda k: T_R[:, s_lo_ + k, lat], 4))
                    else:
                        tile(U, 0, 0, 8 * r_ + 2 + a, three(lambda k: hi_[:, k, :], lambda k: lo_[:, k, :],
                                                            lambda k: T_R[:, T_HM_HI + k, lat], lambda k: H_R[:, k, lat], KT),
                             lambda k: pe.wait_ge(e["lo"].sem, e["lo"][("H", k)]) if v == 2 else None)
                K += len(PIECES[l])
                q += MERGE_CHUNKS[l]
                U += TILES_MERGE + TILES_OUT
                if l == 0:
                    pe.wait_ge(s_ada_dve, CHUNKS_ADA)
                mean_square("n2", bank[3], lat)
                for k in range(KT):
                    pe.wait_ge(e["n2h"].sem, e["n2h"][k])
                    last = mm(bank[4][0:16, lat], wrt[:, k, :], H[:, k, lat], start=(k == 0), stop=(k == KT - 1))
                last.then_inc(e["rp"].next("logits"), 1)
                pe.wait_ge(e["ra"].sem, e["ra"]["sig"])
                for tt in range(t0 // P, NTT):
                    last = tp(bank[4][:, 16 * tt:16 * tt + 16], T[0:16, T_ONEHOT, P * tt:P * tt + P])
                last.then_inc(e["rp"].next("scores"), 1)
                for n_ in range(t0 // 64, 2 * NTT):
                    tt, hf = divmod(n_, 2)
                    if n_ >= t0 // 64 + 2:
                        pe.wait_ge(e["hrc"].sem, e["hrc"][n_ - 2] - t0 // 64)
                    for i in range(4):
                        last = tp(bank[6 + n_ % 2][:, P * i:P * i + P], H[:, 4 * hf + i, P * tt:P * tt + P])
                    last.then_inc(e["hr"].sem, 1)
                if l == 0:
                    pe.wait_ge(e["hrc"].sem, 2 * NTT)
                    for i in range(48):
                        g_, at = i // 2 % 4, 8 * (i // 8) + 4 * (i % 2)
                        last = nc.tensor.transpose(bank[(2, 3, 6, 7)[g_]][:, at:at + 4], ada_row(i // 2)[:, P * (i % 2):P * (i % 2) + P],
                                                   C[32 * g_:32 * g_ + 4, CA["ident"].start + 32 * g_:CA["ident"].start + 32 * g_ + 4])
                    last.then_inc(ev[1]["modr"].next("mod"), 1)
                pe.wait_ge(e["rd"].sem, e["rd"]["comb"])
                for tt in range(t0 // P, NTT):
                    for t_ in range(t0 // P, tt + 1):
                        last = mm(bank[5][:, 16 * tt:16 * tt + 16], cm("ones" if t_ < tt else "tri0"), rs[:, 2, t_, :],
                                  start=(t_ == t0 // P), stop=(t_ == tt))
                last.then_inc(e["rp"].next("cnt"), 1)
                for x_ in range(N_EXPERTS):
                    pe.wait_ge(e["oh"].sem, e["oh"][x_])
                    for tt in range(t0 // P, NTT):
                        last = mm(bank[4][:, 4 * x_:4 * x_ + 4], onehot[:, x_ % 2, P * tt:P * tt + P], pair[:, tt, x_, :],
                                  start=(tt == t0 // P), stop=(tt == NTT - 1))
                    last.then_inc(e["ohp"].next(x_), 1)
                pe.wait_ge(e["rd"].sem, e["rd"]["ov"])
                mm(bank[5][:, 256:257], cm("ones"), mx[:, 0, 0:1], start=True, stop=True).then_inc(e["rp"].next("flag"), 1)

                if l == 0:
                    pe.wait_ge(s_mod1, 1)
                def rows_turned(i, x_, first):
                    if first:
                        pe.wait_ge(e["xg"][i], 16)
                        pe.wait_ge(e["hrc"].sem, 2 * NTT - t0 // 64)
                    else:
                        pe.wait_ge(e["xg"][i], (x_ - i) * 8 + 16)
                        pe.wait_ge(e["xcd"], x_)
                    for hf in range(2):
                        for k in range(4):
                            last = tp(bank[2 + hf][:, P * k:P * k + P], T[:, T_XROW + 2 * i + hf, P * k:P * k + P])
                        last.then_inc(e["xt"], 1)

                def expert(p_, i, tail):
                    xt, xt_lo = (T_R[:, t_ + 2 * i:t_ + 2 * i + 2, :].rearrange("p a (k s) -> p (a k) s", k=4) for t_ in (T_XT, T_XT_LO))
                    pe.wait_ge(e["xcd"], p_ * 2 + (i + 1))
                    for t_ in range(2):
                        pe.wait_ge(s_taken[t_], p_ * 4 + (2 * i + (U + t_) // 2 + 1))
                        for c_ in range(2):
                            C_ = q + 6 * i + 2 * t_ + c_
                            pe.wait_ge(s_lo, p_ * 12 + (K + 6 * i + 2 * t_ + c_ + 1))
                            w_hi, w_lo = hi_view(C_, 4, T_HI_EXP, N_HI_EXP), lo_view(C_, 4)
                            for k in range(4):
                                mm(bank[t_][:, :], xt[:, 4 * c_ + k, :], w_hi[:, k, :], start=(c_ + k == 0), stop=False)
                                mm(bank[t_][:, :], xt[:, 4 * c_ + k, :], w_lo[:, k, :], start=False, stop=False)
                                last = mm(bank[t_][:, :], xt_lo[:, 4 * c_ + k, :], w_hi[:, k, :], start=False, stop=(c_ + k == 4))
                        last.then_inc(s_tile[t_], 1)
                    if not tail:
                        rows_turned(1 - i, p_ * 2 + (i + 1), False)
                    pe.wait_ge(s_taken[1], p_ * 4 + (2 * i + U // 2 + 2))
                    for k in range(4):
                        last = tp(bank[4 + i][:, P * k:P * k + P], T[:, T_HID + i, P * k:P * k + P])
                    last.then_inc(e["ht"], 1)
                    pe.wait_ge(e["hcd"], p_ * 2 + (i + 1))
                    for t_ in range(2):
                        C_ = q + 6 * i + 4 + t_
                        pe.wait_ge(s_taken[t_], p_ * 4 + (2 * i + (U + 2 + t_) // 2 + 1))
                        pe.wait_ge(s_lo, p_ * 12 + (K + 6 * i + 4 + t_ + 1))
                        w_hi, w_lo = hi_view(C_, 4, T_HI_EXP, N_HI_EXP), lo_view(C_, 4)
                        for k in range(4):
                            h_hi, h_lo = T_R[:, T_HT + i, P * k:P * k + P], T_R[:, T_HT_LO + i, P * k:P * k + P]
                            mm(bank[t_][:, :], h_hi, w_hi[:, k, :], start=(k == 0), stop=False)
                            mm(bank[t_][:, :], h_hi, w_lo[:, k, :], start=False, stop=False)
                            last = mm(bank[t_][:, :], h_lo, w_hi[:, k, :], start=False, stop=(k == 3))
                        last.then_inc(s_tile[t_], 1)

                rows_turned(0, 0, True)
                pe.wait_ge(e["rd"].sem, e["rd"]["flag"])
                with pe.Fori(0, N_EXPERTS // 2 - 1) as p_:
                    expert(p_, 0, False)
                    expert(p_, 1, False)
                expert(N_EXPERTS // 2 - 1, 0, False)
                expert(N_EXPERTS // 2 - 1, 1, True)
                q += 6 * N_EXPERTS
                U += N_EXPERTS * TILES_EXP
                for n_ in range(2 * (NTT - t0 // P)):
                    pe.wait_ge(e["bs"].sem, n_ + 1)
                    if n_ >= 2:
                        pe.wait_ge(e["bx"].sem, n_ - 1)
                    for k in range(4):
                        last = tp(bank[6 + n_ % 2][:, P * k:P * k + P], T[:, T_GATHER + 4 * (n_ // 2) + n_ % 2, P * k:P * k + P])
                    last.then_inc(e["bt"].sem, 1)

                with pe.If(pe.value_load(flag[0:1, 0:1], min_val=0, max_val=1) > 0):
                    pe.wait_ge(e["f_hid"], 1)
                    for tt in range(t0 // P, NTT):
                        last = tp(bank[5][0:16, P * tt:P * tt + P], rs[:, 6, tt, :])
                    last.then_inc(e["f_comb"], 1)
                    with pe.Fori(0, N_EXPERTS) as x_:
                        for s in range(6):
                            pe.wait_ge(e["f_chunk"][s], x_ * 16 + 16)
                            if s == 4:
                                pe.wait_ge(e["f_hid"], x_ * 4 + 8)
                            for m in range(2 if s < 4 else 4):
                                j = 2 * s + m if s < 4 else 4 * s - 8 + m
                                pe.wait_ge(e["f_taken"][j % 2], x_ * 8 + (j // 2 + 1))
                                n = KT if s < 4 else 4
                                for k in range(n):
                                    last = mm(bank[j % 2][:, lat], w_view(s, n)[:, k, P * m:P * m + P], H[:, k, lat] if s < 4 else T[:, F_HID + k, lat],
                                              start=(k == 0), stop=(k == n - 1))
                                last.then_inc(e["f_tile"][j % 2], 1)

            pe.wait_ge(ev[-1]["x2"].sem, 1)
            for tt in range(2):
                for hf in range(2):
                    for i in range(4):
                        last = tp(bank[2 + 2 * tt + hf][:, P * i:P * i + P], X[:, 4 * hf + i, CTX_LEN + P * tt:CTX_LEN + P * tt + P])
            last.then_inc(s_turned, 1)

        @block.scalar
        def _(act):
            sc = nc.scalar
            eps = C[:, CA["eps"]]
            act.dma_start(C[:, 0:P], const[:, 0:P]).then_inc(s_first, 16)
            for v, src in enumerate((c[0], c_ctx)):
                act.dma_start(rows_c[8 * v:8 * v + 8, :], src.rearrange("(n p) -> n p", p=P)).then_inc(s_first, 16)
            for i in range(NTT):
                src = (ctx if i < 2 else x)[0].rearrange("(t p) d -> t p d", p=P)[i % 2]
                act.dma_start(flat(T[:, 2 * i:2 * i + 2, :]), src).then_inc(s_xin, 16)
            act.wait_ge(setup_pe.sem, setup_pe["c"])
            for v in range(2):
                last = sc.activation(silu_c[:, :, v], bank[0][:, 8 * v:8 * v + 8], ACT.Silu)
            last.then_inc(setup_act.next("silu_c"), 1)
            act.wait_ge(setup_act.sem, setup_act["silu_c"])
            sc.activation(silu_r[:, :, 0:2], silu_c[:], ACT.Copy).then_inc(setup_act.next("silu_hi"), 1)

            for l in range(DEPTH):
                e = ev[l]
                t0 = e["t0"]
                U = U_LAYER[l]
                lat, full = slice(t0, TOK), slice(0, TOK)
                mod = mods[l]

                def taken(u, ins):
                    ins.then_inc(s_taken[u % 2], 1)

                def squares(w, cols, u0):
                    for k in range(KT):
                        if u0:
                            act.wait_ge(s_taken[(u0 + k) % 2], (u0 + k) // 2 + 2)
                        sc.activation(T[:, k, cols], X[:, k, cols], ACT.Square).then_inc(e[w + "sq"].next(k), 1)
                    act.wait_ge(e[w + "ms"].sem, e[w + "ms"]["ms"])
                    link(act, "act", sc.activation(T[:, 8, cols], bank[3][:, cols], ACT.Ln, bias=eps, scale=1.0 / D_MODEL))
                    sc.activation(T[:, 8, cols], T[:, 8, cols], ACT.Exp, scale=-0.5).then_inc(e[w + "rt"].next("rt"), 1)

                def modulate(w, k, sh_at, segs_):
                    act.wait_ge(e[w + "x"].sem, e[w + "x"][k])
                    for s0, v in segs_:
                        last = sc.activation(H[:, k, s0:s0 + 256], H[:, k, s0:s0 + 256], ACT.Identity, scale=gain[:, k, v:v + 1],
                                             bias=mod[:, sh_at + k, v:v + 1])
                    last.then_inc(e[w + "h"].next(k), 1)

                if l == 0:
                    act.wait_ge(setup_dve.sem, setup_dve["x7"])
                else:
                    act.wait_ge(ev[l - 1]["x2"].sem, 1)
                q = Q_LAYER[l]

                def high(C_, t_hi, n_hi):
                    sc.activation(flat(hi_view(C_, 4, t_hi, n_hi)), flat(w_view(C_, 4)), ACT.Copy).then_inc(s_hi, 1)

                if l == 0:
                    for s in range(RING):
                        chunk_wait(act, q, 0, 0, s)
                        if s >= N_HI_ADA:
                            act.wait_ge(s_tile[(U + s - N_HI_ADA) % 2], (U + s - N_HI_ADA) // 2 + 1)
                        high(q + s, T_HI_ADA, N_HI_ADA)
                    with act.Fori(1, CHUNKS_ADA // RING) as i:
                        for s in range(RING):
                            chunk_wait(act, q, i, RING, s)
                            u = U + s - N_HI_ADA + RING
                            act.wait_ge(s_tile[u % 2], i * (RING // 2) + (u // 2 + 1 - RING // 2))
                            high(q + s, T_HI_ADA, N_HI_ADA)
                    U += TILES_ADA
                    q += CHUNKS_ADA

                def part_hi(w, k, dst, src):
                    sc.activation(dst, src, ACT.Copy).then_inc(e["hi"].next((w, k)), 1)

                for s in range(N_HI_IN):
                    chunk_wait(act, q, 0, 0, s)
                    high(q + s, T_HI_IN, N_HI_IN)
                squares("n1", full, 0)
                for k in range(KT):
                    modulate("n1", k, 0, ((0, 1), (CTX_LEN, 0)))
                    if not by_pool("h", k):
                        act.wait_ge(e["n1h"].sem, e["n1h"][k])
                        part_hi("h", k, T_R[:, T_H_HI + k, :], H[:, k, :])
                act.wait_ge(s_rpb_out, 16 * DEPTH)
                for j in range(24):
                    cols = lat if j % 12 < 4 else full
                    act.wait_ge(s_tile[j % 2], (U + j) // 2 + 1)
                    taken(j, sc.activation(T[:, j, cols], bank[j % 2][:, cols], ACT.Copy))
                    if j % 2 == 1 and j // 2 + N_HI_IN < SPLIT_IN:
                        chunk_wait(act, q, 0, 0, j // 2 + N_HI_IN)
                        high(q + j // 2 + N_HI_IN, T_HI_IN, N_HI_IN)
                U += 24
                q += CHUNKS_IN
                act.wait_ge(s_small, 16 * (3 * DEPTH + 2))
                sc.activation(ea[:], alog[l][:], ACT.Exp).then_inc(e["aba"].next("ea"), 1)
                act.wait_ge(e["abd"].sem, e["abd"]["x"])
                sc.activation(tmp_g[:, 1], tmp_g[:, 1], ACT.Exp).then_inc(e["aba"].next("e"), 1)
                act.wait_ge(e["aba"].sem, e["aba"]["e"])
                sc.activation(tmp_g[:, 1], tmp_g[:, 1], ACT.Ln, bias=1.0).then_inc(e["aba"].next("ln"), 1)
                sc.activation(beta[:], ab[:, :, 1, :], ACT.Sigmoid).then_inc(e["aba"].next("sig"), 1)

                def square(n_, src, cols):
                    if n_ >= 2:
                        act.wait_ge(e["st"].sem, e["st"][n_ - 2])
                    sc.activation(T[:, T_SQ + n_ % 2, cols], src, ACT.Square).then_inc(e["sq"].next(n_), 1)

                def roots(j, cols, n):
                    for n_ in (j, j + 1):
                        act.wait_ge(e["st"].sem, e["st"][n_])
                        if n_ >= 2:
                            act.wait_ge(e["nrm"].sem, e["nrm"][n_ - 2])
                        last = sc.activation(T[:, T_RT + n_ % 2, cols], bank[4 + n_ % 2][:, cols], ACT.Ln, bias=eps, scale=1.0 / n)
                    link(act, "act", last)
                    for n_ in (j, j + 1):
                        rt_ = T[:, T_RT + n_ % 2, cols]
                        sc.activation(rt_, rt_, ACT.Exp, scale=-0.5).then_inc(e["rt"].next(n_), 1)

                for j in range(0, 16, 2):
                    if j == 8:
                        for i in range(12):
                            cols = lat if i < 4 else full
                            c_line = e["conv" if i < 8 else "convp"]
                            act.wait_ge(c_line.sem, c_line[i])
                            sc.activation(T[:, T_DQ + i, cols], T[:, T_DQ + i, cols], ACT.Silu).then_inc(e["silu"].next(i), 1)
                        act.wait_ge(e["silu"].sem, e["silu"][11])
                    cols = lat if j % 8 < 4 else full
                    for n_ in (j, j + 1):
                        square(n_, T[:, (T_NQ + n_) if j < 8 else (T_DQ + n_ - 8), cols], cols)
                    for n_ in (j, j + 1):
                        u = U + n_
                        dst = T_U + n_ if n_ < 12 else T_Z + n_ - 12
                        act.wait_ge(s_tile[u % 2], u // 2 + 1)
                        sc.activation(T[:, dst, lat], bank[u % 2][:, lat], ACT.Copy).then_inc(s_taken[u % 2], 1)
                    roots(j, cols, NA_D if j < 8 else 1)
                U += 16
                act.wait_ge(s_taken[1], U // 2 + 1)
                act.wait_ge(s_taken[0], U // 2 + 1)
                for i in range(4):
                    last = sc.activation(T[:, T_Z + i, lat], T[:, T_Z + i, lat], ACT.Silu)
                last.then_inc(e["silu"].next("z"), 1)
                for n_ in range(12):
                    what, tt = divmod(n_, 4)
                    if n_ == 0:
                        act.wait_ge(e["sc"].sem, e["sc"]["sc"])
                        act.wait_ge(e["biasm"].sem, 6)
                    act.wait_ge(e["tp"].sem, e["tp"][n_])
                    dst = (T_VTOK, T_KTOK_DN, T_VTOK_DN)[what] + tt
                    sc.activation(T[:, dst, :], bank[6 + n_ % 2][:, :], ACT.Copy).then_inc(e["tpc"].next(n_), 1)

                items = names_na(l)
                N = len(items)
                for n_ in range(N + 2):
                    if n_ < N:
                        qt, h = items[n_]
                        keys = CTX_LEN if qt < 2 else TOK
                        act.wait_ge(e["aM"].sem, e["aM"][n_])
                        if n_ >= 4:
                            act.wait_ge(e["aT"].sem, e["aT"][n_ - 4])
                        sc.activation(T[:, T_E[n_ % 4], 0:keys], bank[n_ % 4][:, 0:keys], ACT.Exp, bias=mx[:, n_ % 4, 1:2],
                                      scale=NA_SCALE, accum_out=mx[:, n_ % 4, 2:3]).then_inc(e["aE"].next(n_), 1)
                    if n_ >= 2:
                        m_ = n_ - 2
                        qt, h = items[m_]
                        keys = CTX_LEN if qt < 2 else TOK
                        act.wait_ge(e["aT"].sem, e["aT"][m_])
                        if m_ >= 2:
                            act.wait_ge(e["aO"].sem, e["aO"][m_ - 2])
                        sc.activation(T[:, T_PT + m_ % 2, 0:keys], bank[4 + m_ % 2][:, 0:keys], ACT.Copy).then_inc(e["aC"].next(m_), 1)

                for j, d, tt in CH:
                    dd, da, dp, dg = e["dd"][d], e["da"][d], e["dp"][d], e["dg"][d]
                    wt = [T[:, T_WORK[d][i], :] for i in range(8)]
                    act.wait_ge(dd.sem, dd[(j, "M")])
                    if j:
                        act.wait_ge(dp.sem, dp[(j - 1, "dS")])
                    sc.activation(wt[1], bank[2 + 3 * d][:, :], ACT.Exp).then_inc(da.next((j, "eg")), 1)
                    sc.activation(wt[0], wt[0], ACT.Exp).then_inc(da.next((j, "DT")), 1)
                act.wait_ge(e["dd"][0].sem, len(e["dd"][0].names))
                act.wait_ge(e["dd"][1].sem, len(e["dd"][1].names))
                def piece_hi(w):
                    if w < len(PIECES[l]):
                        chunk_wait(act, q, 0, 0, PIECES[l][w][2])
                        w_, hi_, _ = piece(q, l, w)
                        sc.activation(hi_, w_, ACT.Copy).then_inc(s_hi, 1)

                for i in range(4):
                    sc.activation(T[:, T_SQ + i, lat], T[:, T_OT + i, lat], ACT.Square).then_inc(e["sq"].next(16 + i), 1)
                for k in range(4):
                    part_hi("na", k, T_R[:, T_NA_HI[k], lat], T[:, T_NQ + k, lat])
                for w in range(3):
                    piece_hi(w)
                for i in range(4):
                    act.wait_ge(e["st"].sem, e["st"][16 + i])
                    last = sc.activation(T[:, T_SQ + i, lat], bank[4 + i][:, lat], ACT.Ln, bias=eps, scale=1.0 / DN_D)
                link(act, "act", last)
                for i in range(4):
                    sc.activation(T[:, T_SQ + i, lat], T[:, T_SQ + i, lat], ACT.Exp, scale=-0.5).then_inc(e["rt"].next(16 + i), 1)
                for w, (kind, v, at) in enumerate(PIECES[l]):
                    if kind == "a":
                        act.wait_ge(s_ada_pe, v + 1)
                        piece_hi(w + 3)
                        continue
                    if v >= SPLIT_MERGE:
                        u = U + last_tile_of_piece(v)
                        act.wait_ge(s_tile[u % 2], u // 2 + 1)
                        piece_hi(w + 3)
                        continue
                    r_, a = divmod(v, 6)
                    for n_ in ((8 * r_ + 2 * a, 8 * r_ + 2 * a + 1) if a < 2 else (8 * r_ + a + 2,)):
                        u, m_ = U + n_, n_ % 8
                        act.wait_ge(s_tile[u % 2], u // 2 + 1)
                        if r_:
                            act.wait_ge(e["mgd"].sem, e["mgd"][4 * (r_ - 1) + m_ % 4])
                        if m_ < 4:
                            sc.activation(T[:, T_BR + m_, lat], bank[u % 2][:, lat], ACT.Copy).then_inc(s_taken[u % 2], 1)
                        else:
                            sc.activation(T[:, T_SG + m_ - 4, lat], bank[u % 2][:, lat], ACT.Sigmoid).then_inc(s_taken[u % 2], 1)
                    piece_hi(w + 3)
                    if v == 5:
                        for k in range(4):
                            act.wait_ge(e["nrm"].sem, e["nrm"][19])
                            part_hi("dn", k, T_R[:, T_DN_HI[k], lat], T[:, T_Z + k, lat])
                        for k in range(4):
                            part_hi("sc", k, T_R[:, T_SC_HI[k], lat], T[:, T_U + k, lat])
                    if v == 29:
                        for k in range(4):
                            part_hi("mg", k, T_R[:, T_MG_HI[k], lat], T[:, T_MERGED + k, lat])
                    if v == SPLIT_MERGE - 1:
                        for k in range(4, 8):
                            act.wait_ge(e["mgd"].sem, e["mgd"][16 + k])
                            part_hi("mg", k, T_R[:, T_MG_HI[k], lat], T[:, T_MERGED + k, lat])
                U += TILES_MERGE + TILES_OUT
                q += MERGE_CHUNKS[l]
                squares("n2", lat, U - TILES_OUT)
                for k in range(KT):
                    modulate("n2", k, 24, ((0, 1), (CTX_LEN, 0))[t0 // CTX_LEN:])
                act.wait_ge(e["rp"].sem, e["rp"]["logits"])
                sc.activation(T[0:16, T_ONEHOT, lat], bank[4][0:16, lat], ACT.Sigmoid).then_inc(e["ra"].next("sig"), 1)
                for n_ in range(t0 // 64, 2 * NTT):
                    act.wait_ge(e["hr"].sem, n_ + 1 - t0 // 64)
                    sc.activation(T[:, T_HROW + n_, :], bank[6 + n_ % 2][:, :], ACT.Copy).then_inc(e["hrc"].sem, 1)
                for s in range(N_HI_EXP):
                    act.wait_ge(s_chunk[(q + s) % RING], 16 * ((q + s) // RING + 1))
                    high(q + s, T_HI_EXP, N_HI_EXP)

                def rows_hi(i, n_):
                    for hf in range(2):
                        act.wait_ge(e["xt"], n_ + hf)
                        sc.activation(T_R[:, T_XT + 2 * i + hf, :], bank[2 + hf][:, :], ACT.Copy).then_inc(e["xca"], 1)

                rows_hi(0, 1)

                def chunk_hi(p_, c_):
                    C_ = q + c_
                    act.wait_ge(s_chunk[C_ % RING], p_ * 32 + 16 * (C_ // RING + 1))
                    high(C_, T_HI_EXP, N_HI_EXP)

                def expert(p_, i, tail):
                    act.wait_ge(s_tile[0], p_ * 4 + (2 * i + U // 2 + 1))
                    sc.activation(T[:, T_MSG + i, :], bank[0][:, :], ACT.Silu).then_inc(s_taken[0], 1)
                    chunk_hi(p_, 6 * i + 4)
                    chunk_hi(p_, 6 * i + 5)
                    if not tail:
                        rows_hi(1 - i, p_ * 4 + (2 * i + 3))
                    act.wait_ge(e["ht"], p_ * 2 + (i + 1))
                    sc.activation(T_R[:, T_HT + i, :], bank[4 + i][:, :], ACT.Copy).then_inc(e["hc"], 1)
                    if not tail:
                        chunk_hi(p_, 6 * i + 6)
                        chunk_hi(p_, 6 * i + 7)
                        act.wait_ge(s_tile[0], p_ * 4 + (2 * i + U // 2 + 2))
                        chunk_hi(p_, 6 * i + 8)
                    act.wait_ge(s_tile[1], p_ * 4 + (2 * i + U // 2 + 2))
                    act.wait_ge(e["yst"][i], p_ * 16 + 16)
                    sc.activation(T[:, T_Y + 2 * i + 1, :], bank[1][:, :], ACT.Copy).then_inc(s_taken[1], 1)
                    if not tail:
                        chunk_hi(p_, 6 * i + 9)

                with act.Fori(0, N_EXPERTS // 2 - 1) as p_:
                    expert(p_, 0, False)
                    expert(p_, 1, False)
                expert(N_EXPERTS // 2 - 1, 0, False)
                expert(N_EXPERTS // 2 - 1, 1, True)
                act.wait_ge(e["rd"].sem, e["rd"]["flag"])
                with act.If(act.value_load(flag[0:1, 0:1], min_val=0, max_val=1) > 0):
                    with act.Fori(0, N_EXPERTS) as x_:
                        for f in range(4):
                            j = (0, 1, 4, 5)[f]
                            act.wait_ge(e["f_tile"][j % 2], x_ * 8 + (j // 2 + 1))
                            act.wait_ge(e["f_hid"], x_ * 4 + (f + 1))
                            sc.activation(T[:, F_MSG + f, lat], bank[j % 2][:, lat], ACT.Silu).then_inc(e["f_taken"][j % 2], 1)

            act.wait_ge(s_store, 1)
            act.dma_start(out[0].rearrange("(t p) d -> p t d", p=P), T[:, 0:4, :].rearrange("p (t a) b -> p t (a b)", t=2)).then_inc(s_out, 16)
            act.wait_ge(s_out, 16)

        @block.vector
        def _(dve):
            ve = nc.vector

            def lk(ins):
                link(dve, "dve", ins)

            ve.memset(zero_row[:], 0.0)
            ve.memset(rpb[:], 0.0).then_inc(setup_dve.next("rpbzero"), 1)
            for b in range(2):
                ve.memset(mx[:, b, :], 0.0).then_inc(s_taken[b], 1)
            dve.wait_ge(setup_act.sem, setup_act["silu_hi"])
            ve.tensor_tensor(silu_r[:, :, 2:4], silu_c[:], silu_r[:, :, 0:2], ALU.subtract).then_inc(setup_dve.next("silu_r"), 1)
            dve.wait_ge(s_rpb, 16 * DEPTH)
            ve.tensor_scalar(rpb[:], rpb[:], 1.0 / NA_SCALE, None, ALU.mult).then_inc(setup_dve.next("rpb"), 1)
            for k in range(KT):
                dve.wait_ge(setup_pe.sem, setup_pe[f"x{k}"])
                ve.tensor_copy(X[:, k, :], bank[2 + k % 6][:, :]).then_inc(setup_dve.next(f"x{k}"), 1)

            for l in range(DEPTH):
                e = ev[l]
                t0 = e["t0"]
                U = U_LAYER[l]
                lat, full = slice(t0, TOK), slice(0, TOK)
                mod = mods[l]
                segs = [(s0, v) for s0, v in ((0, 1), (CTX_LEN, 0)) if s0 >= t0]
                q, K = Q_LAYER[l], K_LAYER[l]

                def low(C_, t_hi, n_hi):
                    w_ = flat(w_view(C_, 4))
                    ve.tensor_tensor(flat(lo_view(C_, 4)), w_, flat(hi_view(C_, 4, t_hi, n_hi)), ALU.subtract).then_inc(s_lo, 1)

                def mod_row(i, s):
                    b = (U + s) % 2
                    dve.wait_ge(s_tile[b], i * (RING // 2) + ((U + s) // 2 + 1))
                    tile_ = T[0:4, T_MODROW + i * (RING // 2) + s // 2, :] if isinstance(i, int) else \
                        flat(T[0:4, bass.ds(i * (RING // 2) + (T_MODROW + s // 2), 1), :])
                    ve.tensor_copy(tile_[:, 256 * (s % 2):256 * (s % 2) + 256], bank[b][0:4, 0:256]).then_inc(s_taken[b], 1)

                if l == 0:
                    dve.wait_ge(s_hi, K + 1)
                    low(q, T_HI_ADA, N_HI_ADA)
                    n_ = CHUNKS_ADA // RING - 1
                    with dve.Fori(0, n_) as i:
                        for s in range(RING):
                            dve.wait_ge(s_hi, i * RING + (K + s + 2))
                            low(q + s + 1, T_HI_ADA, N_HI_ADA)
                            mod_row(i, s)
                    for s in range(RING):
                        if s < RING - 1:
                            dve.wait_ge(s_hi, n_ * RING + K + s + 2)
                            low(q + s + 1, T_HI_ADA, N_HI_ADA)
                        mod_row(n_, s)
                    U += TILES_ADA
                    K += SPLIT_ADA
                    q += CHUNKS_ADA

                def part_lo(w, k, dst, src, hi):
                    hi_line = e["hip" if by_pool(w, k) else "hi"]
                    dve.wait_ge(hi_line.sem, hi_line[(w, k)])
                    ve.tensor_tensor(dst, src, hi, ALU.subtract).then_inc(e["lo"].next((w, k)), 1)

                def piece_lo(w):
                    if w < len(PIECES[l]):
                        dve.wait_ge(s_hi, K + w + 1)
                        w_, hi_, lo_ = piece(q, l, w)
                        ve.tensor_tensor(lo_, w_, hi_, ALU.subtract).then_inc(s_lo, 1)

                if l == 0:
                    for i in range(2 * DEPTH):
                        dst = ((col_a, RA_N), (col_b, RB_N))[i % 2]
                        dve.wait_ge(setup_pe.sem, setup_pe[f"rows{i}"])
                        ve.tensor_copy(dst[0][i // 2][:, :], bank[4 + i][:, 0:dst[1]]).then_inc(setup_dve.next(f"rows{i}"), 1)
                    dve.wait_ge(setup_dve.sem, setup_dve[f"rows{2 * DEPTH - 1}"])
                def add_products(l_, rows_, mod_of):
                    dve.wait_ge(ev[l_]["modr"].sem, ev[l_]["modr"]["mod"])
                    lk(ve.tensor_copy(mods[l_][:], col_a[l_][:, RA_B:RA_B + 48].unsqueeze(2).broadcast_to([P, 48, 2])))
                    for part in range(2):
                        for rows4, mod_ in zip(rows_, mod_of):
                            last = ve.tensor_tensor(mod_, rows4[..., 2 * part:2 * part + 2], mod_, ALU.add)
                        lk(last)

                if l == 0:
                    add_products(0, [bank[2][:, 0:192].rearrange("p (n v) -> p n v", v=4)], [mod[:]])

                def norm(w, sc_at, row, cols):
                    lk(ve.scalar_tensor_tensor(out=gain[:], in0=mod[:, sc_at:sc_at + 8, :], scalar=1.0,
                                               in1=col_a[l][:, row:row + 8].unsqueeze(2).broadcast_to([P, 8, 2]), op0=ALU.add, op1=ALU.mult))
                    dve.wait_ge(e[w + "rt"].sem, e[w + "rt"]["rt"])
                    for k in range(KT):
                        ve.tensor_tensor(H[:, k, cols], X[:, k, cols], T[:, 8, cols], ALU.mult).then_inc(e[w + "x"].next(k), 1)

                for s in range(N_HI_IN):
                    dve.wait_ge(s_hi, K + s + 1)
                    low(q + s, T_HI_IN, N_HI_IN)
                norm("n1", 8, RA_MIX, full)
                for k in range(KT):
                    part_lo("h", k, T_R[:, T_H_LO + k, :], H[:, k, :], T_R[:, T_H_HI + k, :])
                for s in range(N_HI_IN, SPLIT_IN):
                    dve.wait_ge(s_hi, K + s + 1)
                    low(q + s, T_HI_IN, N_HI_IN)
                q += CHUNKS_IN
                K += SPLIT_IN
                for i in range(6):
                    dve.wait_ge(e["biasf"].sem, e["biasf"][i])
                    ve.tensor_tensor(T[:, T_BIAS + i, :].rearrange("p (n c) -> p n c", c=64), bank[(4, 5, 6, 7, 2, 3)[i]][:, :].rearrange("p (n c) -> p n c", c=64),
                                     C[:, CA["win"]].unsqueeze(1).broadcast_to([P, 8, 64]), ALU.add).then_inc(e["biasm"].next(i), 1)
                dve.wait_ge(e["ab"].sem, e["ab"]["ab"])
                ve.tensor_copy(ab[:], bank[3][:, 0:64].rearrange("p (t w n) -> p t w n", t=4, w=2)).then_inc(e["abd"].next("ab"), 1)
                dve.wait_ge(e["abd"].sem, e["abd"]["ab"])
                lk(ve.tensor_tensor(tmp_g[:, 0], ab[:, :, 0, :], dtb[l][:].unsqueeze(1).broadcast_to([P, NTT, 8]), ALU.add))
                lk(ve.tensor_scalar(tmp_g[:, 2], tmp_g[:, 0], -1.0, None, ALU.mult))
                ve.tensor_tensor(tmp_g[:, 1], tmp_g[:, 0], tmp_g[:, 2], ALU.min).then_inc(e["abd"].next("x"), 1)
                dve.wait_ge(e["aba"].sem, e["aba"]["sig"])
                lk(ve.scalar_tensor_tensor(out=tmp_g[:, 0], in0=tmp_g[:, 0], scalar=0.0, in1=tmp_g[:, 1], op0=ALU.max, op1=ALU.add))
                for d in range(2):
                    last = ve.scalar_tensor_tensor(out=gdec[:, d], in0=tmp_g[:, 0, :, 4 * d:4 * d + 4], scalar=-1.0,
                                                   in1=ea[:, 4 * d:4 * d + 4].unsqueeze(1).broadcast_to([P, NTT, 4]), op0=ALU.mult, op1=ALU.mult)
                last.then_inc(e["abd"].next("beta_g"), 1)
                dve.wait_ge(e["ab"].sem, e["ab"]["G"])
                ve.tensor_scalar(negG[:], bank[3][:, 64:96].rearrange("p (d t h) -> p d t h", d=2, t=4), -1.0, None, ALU.mult)\
                    .then_inc(e["abd"].next("negG"), 1)

                def conv(dst, src, taps, col, cols):
                    n = (TOK - cols.start) // 256
                    half = taps // 2
                    lk(ve.tensor_scalar(T[:, dst, cols], T[:, src, cols], col(half), None, ALU.mult))
                    for t_ in range(taps):
                        s_ = t_ - half
                        if s_ == 0:
                            continue
                        o_ = T[:, dst, cols].rearrange("p (s n) -> p s n", s=n)[:, :, max(0, -s_):256 - max(0, s_)]
                        i_ = T[:, src, cols].rearrange("p (s n) -> p s n", s=n)[:, :, max(0, s_):256 - max(0, -s_)]
                        last = ve.scalar_tensor_tensor(out=o_, in0=i_, scalar=col(t_), in1=o_, op0=ALU.mult, op1=ALU.add)
                        if t_ < taps - 1:
                            lk(last)
                    return last

                def normed(n_, i_, cols, g, rope):
                    dve.wait_ge(e["rt"].sem, e["rt"][n_])
                    rt_ = T[:, T_RT + n_ % 2, cols]
                    if rope:
                        dve.wait_ge(e["rot"].sem, e["rot"][n_ - 8])
                        dve.wait_ge(e["silu"].sem, e["silu"][11])
                        t_ = T[:, i_, 256:512]
                        rb_ = bank[6 + n_ % 2][:, 0:256]
                        ve.tensor_tensor(rb_, rb_, cm("sin"), ALU.mult)
                        lk(ve.tensor_tensor(t_, t_, cm("cos"), ALU.mult))
                        lk(ve.tensor_tensor(t_, t_, rb_, ALU.add))
                    ve.scalar_tensor_tensor(out=T[:, i_, cols], in0=T[:, i_, cols], scalar=g, in1=rt_, op0=ALU.mult, op1=ALU.mult)\
                        .then_inc(e["nrm"].next(n_), 1)

                def conv_dn(i):
                    cols = lat if i < 4 else full
                    lk(conv(T_CONV, T_DQ + i, 5, lambda t_: col_b[l][:, RB_CONV + 12 * t_ + i:RB_CONV + 12 * t_ + i + 1], cols))
                    ve.tensor_copy(T[:, T_DQ + i, cols], T[:, T_CONV, cols]).then_inc(e["conv"].next(i), 1)
                    dve.wait_ge(e["conv"].sem, e["conv"][i])

                dve.wait_ge(s_taken[1], (U + 24) // 2 + 1)
                dve.wait_ge(s_taken[0], (U + 24) // 2 + 1)
                for j in range(8):
                    conv_dn(j)
                    g_ = col_b[l][:, RB_QG:RB_QG + 1] if j < 4 else col_b[l][:, RB_KG:RB_KG + 1]
                    normed(j, T_NQ + j, lat if j < 4 else full, g_, False)
                for j in range(8, 16):
                    q_ = j < 12
                    if j == 13:
                        for i in range(4):
                            if i == 0:
                                dve.wait_ge(s_taken[1], (U + 36) // 2 + 1)
                                dve.wait_ge(s_taken[0], (U + 36) // 2 + 1)
                            lk(ve.tensor_tensor(T[:, T_C + i, lat], T[:, T_C + i, lat], T[:, T_U + i, lat], ALU.mult))
                            lk(conv(T_U + i, T_C + i, 3, lambda t_: col_b[l][:, RB_SC + 4 * t_ + i:RB_SC + 4 * t_ + i + 1], lat))
                            last = ve.tensor_tensor(T[:, T_U + i, lat], T[:, T_U + i, lat], T[:, T_B + i, lat], ALU.mult)
                        last.then_inc(e["sc"].next("sc"), 1)
                    normed(j, T_DQ + j - 8, lat if q_ else full, DN_D ** -0.5 if q_ else 1.0, True)
                U += TILES_IN

                items = names_na(l)
                N = len(items)
                for n_ in range(N + 3):
                    if n_ < N:
                        qt, h = items[n_]
                        keys = CTX_LEN if qt < 2 else TOK
                        b_ = bank[n_ % 4]
                        if n_ >= 4:
                            dve.wait_ge(e["aE"].sem, e["aE"][n_ - 4])
                        dve.wait_ge(e["aS"].sem, e["aS"][n_])
                        if qt >= 2:
                            t_ = qt - 2
                            bv = T[:, T_BIAS:T_BIAS + 6, :].rearrange("p a b -> p (a b)").rearrange("p (h j) -> p h j", h=8)[
                                :, h, 64 * (2 - 2 * t_):64 * (6 - 2 * t_)]
                            lk(ve.tensor_tensor(b_[:, 256:512], b_[:, 256:512], bv, ALU.add))
                        lk(ve.tensor_reduce(mx[:, n_ % 4, 0:1], b_[:, 0:keys], AX_X, ALU.max))
                        ve.tensor_scalar(mx[:, n_ % 4, 1:2], mx[:, n_ % 4, 0:1], -NA_SCALE, None, ALU.mult).then_inc(e["aM"].next(n_), 1)
                    if 1 <= n_ <= N:
                        m_ = n_ - 1
                        qt, h = items[m_]
                        keys = CTX_LEN if qt < 2 else TOK
                        dve.wait_ge(e["aE"].sem, e["aE"][m_])
                        lk(ve.reciprocal(mx[:, m_ % 4, 3:4], mx[:, m_ % 4, 2:3]))
                        ve.tensor_scalar(T[:, T_E[m_ % 4], 0:keys], T[:, T_E[m_ % 4], 0:keys], mx[:, m_ % 4, 3:4], None, ALU.mult)\
                            .then_inc(e["aP"].next(m_), 1)
                    if n_ >= 4 and n_ % 2 == 0:
                        m_ = n_ - 3
                        qt, h = items[m_]
                        dve.wait_ge(e["aO"].sem, e["aO"][m_])
                        ve.tensor_copy(T[:, T_NQ + h // 2, P * qt:P * qt + P], bank[6 + m_ // 2 % 2][:, 0:P]).then_inc(e["aD"].next(m_ // 2), 1)

                if l:
                    dve.wait_ge(s_masks, 16)
                dve.wait_ge(e["tpc"].sem, e["tpc"][11])
                dve.wait_ge(e["aO"].sem, N)
                ident4 = cm4("ident")
                for j in range(4):
                    grp = [g for g in CH if g[0] == j]

                    def both(f):
                        for g in grp:
                            f(*g)

                    def ctx_of(d):
                        wt = [v4(T[:, T_WORK[d][i], :]) for i in range(8)]
                        return e["dp"][d], e["dd"][d], e["da"][d], e["dg"][d], wt, [v4(bank[2 + 3 * d + i][:, :]) for i in range(3)]

                    def M(j, d, tt):
                        dp, dd, da, dg, wt, bk = ctx_of(d)
                        dve.wait_ge(dp.sem, dp[(j, "gB")])
                        for h in range(4):
                            last = ve.scalar_tensor_tensor(out=wt[0][:, h], in0=bk[0][:, h], scalar=negG[:, d, tt, h:h + 1],
                                                           in1=cm(f"neg{d}"), op0=ALU.add, op1=ALU.add)
                        last.then_inc(dd.next((j, "M")), 1)

                    def LT(j, d, tt):
                        dp, dd, da, dg, wt, bk = ctx_of(d)
                        dve.wait_ge(dp.sem, dp[(j, "KK")])
                        dve.wait_ge(da.sem, da[(j, "DT")])
                        for h in range(4):
                            last = ve.scalar_tensor_tensor(out=wt[2][:, h], in0=bk[1][:, h], scalar=beta[:, tt, 4 * d + h:4 * d + h + 1],
                                                           in1=wt[0][:, h], op0=ALU.mult, op1=ALU.mult)
                        last.then_inc(dd.next((j, "LT")), 1)
                        dve.wait_ge(dd.sem, dd[(j, "LT")])
                        lk(ve.tensor_tensor(wt[4], wt[2], cm4(f"lev0{1 - d}"), ALU.mult))
                        ve.tensor_tensor(wt[4], ident4, wt[4], ALU.subtract).then_inc(dd.next((j, "XT0")), 1)

                    def X0(j, d, tt):
                        dp, dd, da, dg, wt, bk = ctx_of(d)
                        dve.wait_ge(dp.sem, dp[(j, "L")])
                        lk(ve.tensor_tensor(wt[3], bk[1], cm4(f"lev0{d}"), ALU.mult))
                        ve.tensor_tensor(wt[3], ident4, wt[3], ALU.subtract).then_inc(dd.next((j, "X0")), 1)
                        if need_o(l, tt):
                            dve.wait_ge(dg.sem, dg[(j, "kgl")])
                            dve.wait_ge(dp.sem, dp[(j, "QK")])
                            ve.tensor_tensor(wt[0], bk[2], wt[0], ALU.mult).then_inc(dd.next((j, "AT")), 1)

                    def Yk(k):
                        def f(j, d, tt):
                            dp, dd, da, dg, wt, bk = ctx_of(d)
                            dve.wait_ge(dp.sem, dp[(j, f"Y{k}")])
                            ve.tensor_tensor(wt[5], bk[0], cm4(f"lev{k}{d}"), ALU.mult).then_inc(dd.next((j, f"Y{k}")), 1)
                        return f

                    def Zk(k):
                        def f(j, d, tt):
                            dp, dd, da, dg, wt, bk = ctx_of(d)
                            dve.wait_ge(dp.sem, dp[(j, f"ZT{k}")])
                            if k < LEVELS - 1:
                                ve.tensor_tensor(wt[3], wt[3], bk[1], ALU.subtract).then_inc(dd.next((j, f"X{k}")), 1)
                            ve.tensor_tensor(wt[4], wt[4], bk[2], ALU.subtract).then_inc(dd.next((j, f"XT{k}")), 1)
                        return f

                    def R(j, d, tt):
                        if not j:
                            return
                        dp, dd, da, dg, wt, bk = ctx_of(d)
                        dve.wait_ge(dp.sem, dp[(j, "KS")])
                        ve.tensor_tensor(wt[5], v4(T[:, T_VTOK_DN + tt, :]), bk[1], ALU.subtract).then_inc(dd.next((j, "R")), 1)

                    def vn(j, d, tt):
                        dp, dd, da, dg, wt, bk = ctx_of(d)
                        dve.wait_ge(dp.sem, dp[(j, "VN")])
                        ve.tensor_tensor(wt[3], bk[0], beta[:, tt, 4 * d:4 * d + 4].unsqueeze(2).broadcast_to([P, 4, P]), ALU.mult)\
                            .then_inc(dd.next((j, "vn")), 1)

                    def OS(j, d, tt):
                        dp, dd, da, dg, wt, bk = ctx_of(d)
                        if need_o(l, tt):
                            dve.wait_ge(dp.sem, dp[(j, "O")])
                            o_ = T[:, T_OT:T_OT + 4, P * tt:P * tt + P]
                            if j % 2 == 0:
                                ve.tensor_copy(o_, bk[2]).then_inc(dd.next((j, "O")), 1)
                            else:
                                pj = [g for g in CH if g[1] == 1 - d and g[2] == tt][0][0]
                                dve.wait_ge(e["dd"][1 - d].sem, e["dd"][1 - d][(pj, "O")])
                                ve.tensor_tensor(o_, o_, bk[2], ALU.add).then_inc(dd.next((j, "O")), 1)
                        if j < 3:
                            S = T[:, T_STATE + d, :]
                            dve.wait_ge(dp.sem, dp[(j, "dS")])
                            if j == 0:
                                ve.tensor_copy(v4(S), bk[1]).then_inc(dd.next((j, "S")), 1)
                            else:
                                dve.wait_ge(dg.sem, dg[(j, "gl")])
                                for h in range(4):
                                    last = ve.scalar_tensor_tensor(out=v4(S)[:, h], in0=v4(S)[:, h], scalar=glast[:, d, h:h + 1],
                                                                   in1=bk[1][:, h], op0=ALU.mult, op1=ALU.add)
                                last.then_inc(dd.next((j, "S")), 1)

                    both(M)
                    both(LT)
                    both(X0)
                    for k in range(1, LEVELS):
                        both(Yk(k))
                        both(Zk(k))
                    both(R)
                    both(vn)
                    both(OS)

                def dn_out(i):
                    n_ = 16 + i
                    dve.wait_ge(e["rt"].sem, e["rt"][n_])
                    rt_ = T[:, T_SQ + i, lat]
                    dve.wait_ge(e["silu"].sem, e["silu"]["z"])
                    lk(ve.scalar_tensor_tensor(out=rt_, in0=T[:, T_OT + i, lat], scalar=col_b[l][:, RB_OUT:RB_OUT + 1], in1=rt_,
                                               op0=ALU.mult, op1=ALU.mult))
                    ve.tensor_tensor(T[:, T_Z + i, lat], rt_, T[:, T_Z + i, lat], ALU.mult).then_inc(e["nrm"].next(n_), 1)

                for k in range(4):
                    part_lo("na", k, T_R[:, T_NQ + k, lat], T[:, T_NQ + k, lat], T_R[:, T_NA_HI[k], lat])
                for w in range(3):
                    piece_lo(w)
                for w, (kind, v, at) in enumerate(PIECES[l]):
                    if kind == "a":
                        piece_lo(w + 3)
                        if v % 2:
                            dve.wait_ge(s_ada_pe, v + 1)
                            ve.tensor_copy(ada_row(v // 2), bank[2 + v // 2 % 2][0:4, 0:256]).then_inc(s_ada_dve, 1)
                        continue
                    if v >= SPLIT_MERGE:
                        m = v - SPLIT_MERGE
                        u = U + TILES_MERGE + m
                        piece_lo(w + 3)
                        dve.wait_ge(s_tile[u % 2], u // 2 + 1)
                        for n_, (s0, v_) in enumerate(segs):
                            last = ve.scalar_tensor_tensor(out=X[:, m, s0:s0 + 256], in0=bank[u % 2][:, s0:s0 + 256], scalar=mod[:, 16 + m, v_:v_ + 1],
                                                           in1=X[:, m, s0:s0 + 256], op0=ALU.mult, op1=ALU.add)
                        last.then_inc(s_taken[u % 2], 1)
                        continue
                    r_, a = divmod(v, 6)
                    hf, b = divmod(r_, 3)
                    if v == 1:
                        for k in range(KT):
                            part_lo("H", k, H_R[:, k, lat], H[:, k, lat], T_R[:, T_HM_HI + k, lat])
                    if a >= 2:
                        m = a - 2
                        u = U + 8 * r_ + 4 + m
                        dve.wait_ge(s_taken[u % 2], u // 2 + 2)
                        sg_, br_ = T[:, T_SG + m, lat], T[:, T_BR + m, lat]
                        mg_ = T[:, T_MERGED + 4 * hf + m, lat]
                        if b == 0:
                            ve.tensor_tensor(mg_, sg_, br_, ALU.mult).then_inc(e["mgd"].next(4 * r_ + m), 1)
                        else:
                            lk(ve.tensor_tensor(sg_, sg_, br_, ALU.mult))
                            ve.tensor_tensor(mg_, mg_, sg_, ALU.add).then_inc(e["mgd"].next(4 * r_ + m), 1)
                    piece_lo(w + 3)
                    if r_ == 0 and a >= 2:
                        dn_out(a - 2)
                    if v == 5:
                        for k in range(4):
                            part_lo("dn", k, T_R[:, T_Z + k, lat], T[:, T_Z + k, lat], T_R[:, T_DN_HI[k], lat])
                        for k in range(4):
                            part_lo("sc", k, T_R[:, T_U + k, lat], T[:, T_U + k, lat], T_R[:, T_SC_HI[k], lat])
                    if v == 29:
                        for k in range(4):
                            part_lo("mg", k, T_R[:, T_MERGED + k, lat], T[:, T_MERGED + k, lat], T_R[:, T_MG_HI[k], lat])
                    if v == SPLIT_MERGE - 1:
                        for k in range(4, 8):
                            part_lo("mg", k, T_R[:, T_MERGED + k, lat], T[:, T_MERGED + k, lat], T_R[:, T_MG_HI[k], lat])
                U += TILES_MERGE + TILES_OUT
                K += len(PIECES[l])
                q += MERGE_CHUNKS[l]
                dve.wait_ge(s_taken[0], U // 2 + 1)
                dve.wait_ge(s_taken[1], U // 2 + 1)
                norm("n2", 32, RA_FFN, lat)

                tr = slice(t0 // P, NTT)
                nt = NTT - t0 // P
                dve.wait_ge(e["rp"].sem, e["rp"]["scores"])
                scores = bank[4][:, 0:64].rearrange("p (t n) -> p t n", t=NTT)[:, tr]
                R_ = lambda i: rs[:, i, tr, :]
                lk(ve.tensor_tensor(R_(1), scores, rbias[:].unsqueeze(1).broadcast_to([P, nt, 16]), ALU.add))
                g4 = lambda i: rs[:, i, tr, :].rearrange("p t (g x) -> p (t g) x", g=4)

                def rank(vals, cmp_):
                    for j in range(4):
                        for lo, hi, op in ((0, j, ALU.is_gt), (j + 1, 4, ALU.is_ge)):
                            if hi > lo:
                                last = ve.tensor_tensor(cmp_[:, :, lo:hi, j], vals[:, :, j:j + 1].broadcast_to([P, cmp_.shape[1], hi - lo]),
                                                        vals[:, :, lo:hi], op)
                        last = ve.memset(cmp_[:, :, j, j], 0.0)
                    return last
                rc = rcmp[:, tr].rearrange("p t g i j -> p (t g) i j")
                lk(rank(g4(1), rc))
                lk(ve.tensor_reduce(g4(2), rc, AX_X, ALU.add))
                lk(ve.tensor_scalar(R_(2), R_(2), 1.5, None, ALU.is_lt))
                lk(ve.tensor_tensor(R_(3), R_(2), R_(1), ALU.mult))
                gs = rs[:, 4, tr, 0:4]
                lk(ve.tensor_reduce(gs.rearrange("p t g -> p t g"), rs[:, 3, tr, :].rearrange("p t (g x) -> p t g x", g=4), AX_X, ALU.add))
                rg = rcmp[:, tr, 0]
                lk(rank(gs, rg))
                lk(ve.tensor_reduce(rs[:, 5, tr, 0:4], rg, AX_X, ALU.add))
                lk(ve.tensor_scalar(rs[:, 5, tr, 0:4], rs[:, 5, tr, 0:4], 0.5, None, ALU.is_lt))
                ve.tensor_tensor(rs[:, 2, tr, :].rearrange("p t (g x) -> p t g x", g=4), rs[:, 2, tr, :].rearrange("p t (g x) -> p t g x", g=4),
                                 rs[:, 5, tr, 0:4].unsqueeze(3).broadcast_to([P, nt, 4, 4]), ALU.mult).then_inc(e["rd"].next("comb"), 1)
                dve.wait_ge(e["rd"].sem, e["rd"]["comb"])
                lk(ve.tensor_tensor(R_(6), R_(2), scores, ALU.mult))
                lk(ve.tensor_reduce(rs[:, 4, tr, 4:5], R_(6), AX_X, ALU.add))
                lk(ve.reciprocal(rs[:, 4, tr, 5:6], rs[:, 4, tr, 4:5]))
                lk(ve.tensor_tensor(R_(7), R_(6), rs[:, 4, tr, 5:6].broadcast_to([P, nt, 16]), ALU.mult))
                for i in (0, 3):
                    ve.tensor_copy(pair[:, tr, :, i], cm("tokid")[:, 0:nt].unsqueeze(2).broadcast_to([P, nt, 16]))
                lk(ve.tensor_copy(pair[:, tr, :, 1], R_(7)))
                ve.tensor_tensor(pair[:, tr, :, 2], R_(7), pair[:, tr, :, 1], ALU.subtract)
                dve.wait_ge(e["rp"].sem, e["rp"]["cnt"])
                cnt = bank[5][:, 0:64].rearrange("p (t n) -> p t n", t=NTT)[:, tr]
                lk(ve.tensor_tensor(R_(3), cnt, R_(2), ALU.mult))
                ve.tensor_scalar(R_(3), R_(3), -1.0, None, ALU.add).then_inc(e["rd"].next("rk"), 1)
                dve.wait_ge(e["rd"].sem, e["rd"]["rk"])
                lk(ve.tensor_scalar(R_(4), R_(3), CAPACITY - 0.5, None, ALU.is_ge))
                ve.tensor_reduce(mx[:, 0, 0:1], rs[:, 4, tr, :].rearrange("p t n -> p (t n)"), AX_X, ALU.add).then_inc(e["rd"].next("ov"), 1)
                if l == 0:
                    add_products(1, [bank[b][:, 0:48].rearrange("p (a h v) -> p a h v", a=6, h=2) for b in (2, 3, 6, 7)],
                                 [mods[1][:].rearrange("p (a g h) v -> p a g h v", a=6, g=4)[:, :, g_] for g_ in range(4)])
                    ve.memset(mx[:, 2, :], 0.0).then_inc(s_mod1, 1)
                for x_ in range(N_EXPERTS):
                    if x_ >= 2:
                        dve.wait_ge(e["ohp"].sem, e["ohp"][x_ - 2])
                    oh_ = onehot[:, x_ % 2, :].rearrange("p (t s) -> p t s", t=NTT)[:, tr]
                    ve.tensor_tensor(oh_, cm("iota").unsqueeze(1).broadcast_to([P, nt, P]), R_(3)[:, :, x_:x_ + 1].broadcast_to([P, nt, P]),
                                     ALU.is_equal).then_inc(e["oh"].next(x_), 1)
                dve.wait_ge(e["rp"].sem, e["rp"]["flag"])
                ve.tensor_scalar(flag[:], bank[5][:, 256:257], 1.0, None, ALU.min).then_inc(e["rd"].next("flag"), 1)
                dve.wait_ge(e["ohp"].sem, N_EXPERTS)
                slots = bank[4][:, 0:64].rearrange("p (n w) -> p n w", w=4)
                ve.tensor_copy(slot_tok[:], slots[:, :, 0])
                lk(ve.tensor_copy(slot_comb[:], slots[:, :, 1]))
                ve.tensor_tensor(slot_comb[:], slots[:, :, 2], slot_comb[:], ALU.add).then_inc(e["rd"].next("slots"), 1)
                lk(ve.tensor_tensor(R_(1), R_(3), cm("ebase").unsqueeze(1).broadcast_to([P, nt, 16]), ALU.add))
                lk(ve.scalar_tensor_tensor(out=R_(1), in0=R_(4), scalar=2.0 * ZERO_ROW, in1=R_(1), op0=ALU.mult, op1=ALU.add))
                lk(ve.scalar_tensor_tensor(out=R_(5), in0=R_(1), scalar=1.0, in1=R_(2), op0=ALU.add, op1=ALU.mult))
                lk(ve.tensor_reduce(mx[:, 0, 0:nt], R_(5), AX_X, ALU.max))
                ve.tensor_scalar(tok_slot[:, 0, tr], mx[:, 0, 0:nt], -1.0, float(ZERO_ROW), ALU.add, ALU.min)
                lk(ve.scalar_tensor_tensor(out=R_(5), in0=R_(2), scalar=-8.0 * ZERO_ROW, in1=R_(1), op0=ALU.mult, op1=ALU.add))
                lk(ve.tensor_reduce(mx[:, 1, 0:nt], R_(5), AX_X, ALU.min))
                ve.tensor_scalar(tok_slot[:, 1, tr], mx[:, 1, 0:nt], 8.0 * ZERO_ROW, float(ZERO_ROW), ALU.add, ALU.min)\
                    .then_inc(e["rd"].next("back"), 1)

                def chunk_lo(p_, c_):
                    dve.wait_ge(s_hi, p_ * 12 + (K + c_ + 1))
                    low(q + c_, T_HI_EXP, N_HI_EXP)

                def rows_lo(i, n_):
                    for hf in range(2):
                        dve.wait_ge(e["xca"], n_ + hf)
                        last = ve.tensor_tensor(T_R[:, T_XT_LO + 2 * i + hf, :], bank[2 + hf][:, :], T_R[:, T_XT + 2 * i + hf, :], ALU.subtract)
                    last.then_inc(e["xcd"], 1)

                for s in range(N_HI_EXP):
                    chunk_lo(0, s)
                rows_lo(0, 1)

                def expert(p_, i, tail):
                    chunk_lo(p_, 6 * i + 4)
                    chunk_lo(p_, 6 * i + 5)
                    dve.wait_ge(s_taken[0], p_ * 4 + (2 * i + U // 2 + 2))
                    dve.wait_ge(s_tile[1], p_ * 4 + (2 * i + U // 2 + 1))
                    comb = slot_comb[:, 2 * p_ + i:2 * p_ + i + 1] if isinstance(p_, int) else slot_comb[:, bass.ds(p_ * 2 + i, 1)]
                    ve.scalar_tensor_tensor(out=T[:, T_HID + i, :], in0=bank[1][:, :], scalar=comb, in1=T[:, T_MSG + i, :],
                                            op0=ALU.mult, op1=ALU.mult).then_inc(s_taken[1], 1)
                    if not tail:
                        rows_lo(1 - i, p_ * 4 + (2 * i + 3))
                    dve.wait_ge(e["hc"], p_ * 2 + (i + 1))
                    ve.tensor_tensor(T_R[:, T_HT_LO + i, :], bank[4 + i][:, :], T_R[:, T_HT + i, :], ALU.subtract).then_inc(e["hcd"], 1)
                    if not tail:
                        chunk_lo(p_, 6 * i + 6)
                        chunk_lo(p_, 6 * i + 7)
                    dve.wait_ge(s_tile[0], p_ * 4 + (2 * i + U // 2 + 2))
                    dve.wait_ge(e["yst"][i], p_ * 16 + 16)
                    ve.tensor_copy(T[:, T_Y + 2 * i, :], bank[0][:, :]).then_inc(s_taken[0], 1)
                    if not tail:
                        chunk_lo(p_, 6 * i + 8)
                        chunk_lo(p_, 6 * i + 9)

                with dve.Fori(0, N_EXPERTS // 2 - 1) as p_:
                    expert(p_, 0, False)
                    expert(p_, 1, False)
                expert(N_EXPERTS // 2 - 1, 0, False)
                expert(N_EXPERTS // 2 - 1, 1, True)
                U += N_EXPERTS * TILES_EXP
                n_tt = NTT - t0 // P

                def both_added(n_):
                    dve.wait_ge(e["bg"][n_], 32 * (l + 1))
                    for hf in range(2):
                        t_ = T_GATHER + 4 * n_ + hf
                        ve.tensor_tensor(T[:, t_, :], T[:, t_, :], T[:, t_ + 2, :], ALU.add).then_inc(e["bs"].sem, 1)

                both_added(0)
                for n_ in range(n_tt):
                    if n_ + 1 < n_tt:
                        both_added(n_ + 1)
                    tt = t0 // P + n_
                    v = 1 if tt < 2 else 0
                    for hf in range(2):
                        dve.wait_ge(e["bt"].sem, 2 * n_ + hf + 1)
                        for k in range(4):
                            m = 4 * hf + k
                            last = ve.scalar_tensor_tensor(out=X[:, m, P * tt:P * tt + P], in0=bank[6 + hf][:, P * k:P * k + P],
                                                           scalar=mod[:, 40 + m, v:v + 1], in1=X[:, m, P * tt:P * tt + P], op0=ALU.mult, op1=ALU.add)
                        last.then_inc(e["bx"].sem, 1)

                with dve.If(dve.value_load(flag[0:1, 0:1], min_val=0, max_val=1) > 0):
                    dve.wait_ge(e["bx"].sem, 2 * n_tt)
                    for b in range(2):
                        ve.memset(mx[:, b, :], 0.0).then_inc(e["f_taken"][b], 1)
                    for m in range(KT):
                        ve.memset(T[:, F_ACC + m, lat], 0.0)
                    ve.tensor_tensor(R_(6), R_(7), R_(4), ALU.mult).then_inc(e["f_hid"], 4)
                    dve.wait_ge(e["f_comb"], 1)
                    ve.tensor_copy(combT[:, lat], bank[5][0:16, lat]).then_inc(e["f_comb"], 1)
                    with dve.Fori(0, N_EXPERTS // 2) as p_:
                        for i in range(2):
                            dve.wait_ge(e["f_cb"][i], p_ * 16 + 16)
                            for f in range(4):
                                ug, uu = (0, 1, 4, 5)[f], (2, 3, 6, 7)[f]
                                dve.wait_ge(e["f_taken"][ug % 2], p_ * 16 + (8 * i + ug // 2 + 2))
                                dve.wait_ge(e["f_tile"][uu % 2], p_ * 16 + (8 * i + uu // 2 + 1))
                                ve.tensor_tensor(T[:, F_HID + f, lat], T[:, F_MSG + f, lat], bank[uu % 2][:, lat], ALU.mult).then_inc(e["f_taken"][uu % 2], 1)
                                dve.wait_ge(e["f_taken"][uu % 2], p_ * 16 + (8 * i + uu // 2 + 2))
                                ve.tensor_tensor(T[:, F_HID + f, lat], T[:, F_HID + f, lat], T[:, F_CB + i, lat], ALU.mult).then_inc(e["f_hid"], 1)
                            for m in range(KT):
                                ud = 8 + m
                                dve.wait_ge(e["f_tile"][ud % 2], p_ * 16 + (8 * i + ud // 2 + 1))
                                ve.tensor_tensor(T[:, F_ACC + m, lat], T[:, F_ACC + m, lat], bank[ud % 2][:, lat], ALU.add).then_inc(e["f_taken"][ud % 2], 1)
                    for b in range(2):
                        dve.wait_ge(e["f_taken"][b], 8 * N_EXPERTS + 1)
                    for m in range(KT):
                        for s0, v in segs:
                            ve.scalar_tensor_tensor(out=X[:, m, s0:s0 + 256], in0=T[:, F_ACC + m, s0:s0 + 256], scalar=mod[:, 40 + m, v:v + 1],
                                                    in1=X[:, m, s0:s0 + 256], op0=ALU.mult, op1=ALU.add)
                dve.wait_ge(e["bx"].sem, 2 * n_tt)
                ve.memset(mx[:, 0, 0:1], 0.0).then_inc(e["x2"].next("x2"), 1)

            dve.wait_ge(s_turned, 1)
            for i in range(4):
                last = ve.tensor_copy(T[:, i, :], bank[2 + i][:, :])
            last.then_inc(s_store, 1)


_INS = ['x', 'c', 'ctx', 'c_ctx', 'w_ada', 'b_ada', 'norm_mix_g', 'norm_ffn_g', 'w_in', 'na_q_norm_g', 'na_k_norm_g',
        'na_rpb', 'dn_conv_w', 'dn_a_log', 'dn_dt_bias', 'dn_out_norm_g', 'sc_conv_w', 'w_branch_na', 'w_branch_dn',
        'w_branch_sc', 'w_out', 'w_router', 'router_bias', 'moe_w_gate', 'moe_w_up', 'moe_w_down']


def kernel(**inputs):
    import concourse.bacc as _bacc
    from concourse.bass_utils import run_bass_kernel_spmd as _run

    nc = _bacc.Bacc("TRN2", target_bir_lowering=False, num_devices=1)
    arrays, args = {}, {}
    for name in _INS + ["const"]:
        a = constants()[1] if name == "const" else np.ascontiguousarray(inputs[name])
        arrays[f"in_{name}_dram"] = a
        args[name] = nc.dram_tensor(f"in_{name}_dram", a.shape, mybir.dt.from_np(a.dtype), kind="ExternalInput").ap()
    out = nc.dram_tensor("out_0_dram", (1, SEQ, D_MODEL), F32, kind="ExternalOutput").ap()
    build(nc, out=out, **args)
    r = _run(nc, [arrays], core_ids=[0])
    return r.results[0]["out_0_dram"]
```
